# Optimizing a Trainium2 kernel written in Bass

```python
import math
import jax, jax.numpy as jnp
from jax import lax
import numpy as np

D_MODEL = 2048
BATCH = 1
SEQ = 256
DEPTH = 2

C_A = 512
H_B = 16
HEAD_DIM = 64
C_B = H_B * HEAD_DIM
C_C = 512
POOL_WINDOWS = (2, 4, 8, 16)
N_POOL_GROUPS = len(POOL_WINDOWS)
C_G = C_C // N_POOL_GROUPS
MIX_WIDTH = C_A + C_B + C_C
IN_WIDTH = 2 * C_A + 3 * C_B + C_C

CONV_WIDTH = 31
CONV_HALF = CONV_WIDTH // 2

DILATED_PATTERNS = ((128, 1), (512, 4), (2048, 16))
ATTN_BLOCK = 64
ROT_DIM = HEAD_DIM // 4
ROPE_THETA = 500000.0

FFN_HIDDEN = int(math.ceil((8 * D_MODEL / 3) / 256) * 256)
EPS = 1e-6
NEG = -1e30


def rms_normalize(t):
    tf = t.astype(jnp.float32)
    return tf * lax.rsqrt(jnp.mean(tf * tf, axis=-1, keepdims=True) + EPS)

def rmsnorm(t, g):
    return (rms_normalize(t) * g.astype(jnp.float32)).astype(t.dtype)

def rope_tables(S):
    pos = jnp.arange(S, dtype=jnp.float32)
    inv = ROPE_THETA ** (-jnp.arange(0, ROT_DIM, 2, dtype=jnp.float32) / ROT_DIM)
    ang = pos[:, None] * inv[None, :]
    return jnp.cos(ang), jnp.sin(ang)

def apply_partial_rope(t, cos, sin):
    half = ROT_DIM // 2
    t1 = t[..., :half]
    t2 = t[..., half:ROT_DIM]
    c = cos[None, :, None, :]
    s = sin[None, :, None, :]
    return jnp.concatenate([t1 * c - t2 * s, t2 * c + t1 * s, t[..., ROT_DIM:]], axis=-1)

def conformer_conv(u, w, b, ln_g, ln_b):
    a, gate = jnp.split(u, 2, axis=-1)
    h = a * jax.nn.sigmoid(gate)
    h = lax.conv_general_dilated(
        h, w[:, None, :], window_strides=(1,),
        padding=[(CONV_HALF, CONV_HALF)],
        dimension_numbers=('NWC', 'WIO', 'NWC'),
        feature_group_count=C_A) + b
    hf = h.astype(jnp.float32)
    mu = jnp.mean(hf, axis=-1, keepdims=True)
    var = jnp.mean(jnp.square(hf - mu), axis=-1, keepdims=True)
    hf = (hf - mu) * lax.rsqrt(var + EPS) * ln_g.astype(jnp.float32) + ln_b.astype(jnp.float32)
    return jax.nn.silu(hf).astype(u.dtype)

def banded_dilated_stats(q, k, v, dilation, half):
    B, S, H, E = q.shape
    L = S // dilation
    nb = -(-L // ATTN_BLOCK)
    Lp = nb * ATTN_BLOCK
    qd = q.reshape(B, L, dilation, H, E)
    kd = k.reshape(B, L, dilation, H, E)
    vd = v.reshape(B, L, dilation, H, E)
    pad_q = ((0, 0), (0, Lp - L), (0, 0), (0, 0), (0, 0))
    pad_kv = ((0, 0), (ATTN_BLOCK, Lp - L + ATTN_BLOCK), (0, 0), (0, 0), (0, 0))
    qb = jnp.pad(qd, pad_q).reshape(B, nb, ATTN_BLOCK, dilation, H, E)
    kb = jnp.pad(kd, pad_kv).reshape(B, nb + 2, ATTN_BLOCK, dilation, H, E)
    vb = jnp.pad(vd, pad_kv).reshape(B, nb + 2, ATTN_BLOCK, dilation, H, E)
    kwin = jnp.concatenate([kb[:, :-2], kb[:, 1:-1], kb[:, 2:]], axis=2)
    vwin = jnp.concatenate([vb[:, :-2], vb[:, 1:-1], vb[:, 2:]], axis=2)
    blk = jnp.arange(nb)[:, None]
    jq = blk * ATTN_BLOCK + jnp.arange(ATTN_BLOCK)[None, :]
    jk = (blk - 1) * ATTN_BLOCK + jnp.arange(3 * ATTN_BLOCK)[None, :]
    mask = ((jnp.abs(jk[:, None, :] - jq[:, :, None]) <= half)
            & (jk[:, None, :] >= 0) & (jk[:, None, :] < L))
    scores = jnp.einsum('bnqrhe,bnkrhe->bnrhqk', qb, kwin)
    maskb = mask[None, :, None, None, :, :]
    scores = jnp.where(maskb, scores, NEG)
    m = jnp.max(scores, axis=-1)
    p = jnp.where(maskb, jnp.exp(scores - m[..., None]), 0.0)
    s = jnp.sum(p, axis=-1)
    o = jnp.einsum('bnrhqk,bnkrhe->bnqrhe', p, vwin)
    m = jnp.transpose(m, (0, 1, 4, 2, 3)).reshape(B, Lp, dilation, H)[:, :L].reshape(B, S, H)
    s = jnp.transpose(s, (0, 1, 4, 2, 3)).reshape(B, Lp, dilation, H)[:, :L].reshape(B, S, H)
    o = o.reshape(B, Lp, dilation, H, E)[:, :L].reshape(B, S, H, E)
    return m, s, o

def dilated_attention(qkv, cos, sin):
    B, S, _ = qkv.shape
    q, k, v = jnp.split(qkv.astype(jnp.float32), 3, axis=-1)
    q = apply_partial_rope(q.reshape(B, S, H_B, HEAD_DIM), cos, sin) * (HEAD_DIM ** -0.5)
    k = apply_partial_rope(k.reshape(B, S, H_B, HEAD_DIM), cos, sin)
    v = v.reshape(B, S, H_B, HEAD_DIM)
    ms, ss, os_ = [], [], []
    for window, dilation in DILATED_PATTERNS:
        m, s, o = banded_dilated_stats(q, k, v, dilation, window // (2 * dilation))
        ms.append(m); ss.append(s); os_.append(o)
    m_all = jnp.stack(ms)
    s_all = jnp.stack(ss)
    o_all = jnp.stack(os_)
    wgt = jnp.exp(m_all - jnp.max(m_all, axis=0, keepdims=True))
    num = jnp.sum(wgt[..., None] * o_all, axis=0)
    den = jnp.sum(wgt * s_all, axis=0)
    out = num / den[..., None]
    return out.reshape(B, S, C_B).astype(qkv.dtype)

def pool_mixer(u, w, scale):
    B, S, _ = u.shape
    uf = u.astype(jnp.float32)
    cs = jnp.concatenate([jnp.zeros((B, 1, C_C), jnp.float32), jnp.cumsum(uf, axis=1)], axis=1)
    pos = jnp.arange(S)
    outs = []
    for gi, win in enumerate(POOL_WINDOWS):
        seg = cs[..., gi * C_G:(gi + 1) * C_G]
        lo = jnp.clip(pos - win // 2, 0, S)
        hi = jnp.clip(pos + win - win // 2, 0, S)
        mean = (seg[:, hi] - seg[:, lo]) / (hi - lo).astype(jnp.float32)[None, :, None]
        outs.append(mean - uf[..., gi * C_G:(gi + 1) * C_G])
    pooled = jnp.stack(outs, axis=2)
    mixed = jnp.einsum('bsgc,gcd->bsgd', pooled, w.astype(jnp.float32))
    return (mixed.reshape(B, S, C_C) * scale.astype(jnp.float32)).astype(u.dtype)

def first_inputs(seed: int = 0) -> dict:
    key = jax.random.key(seed)
    ks = jax.random.split(key, 20)
    f32 = jnp.float32

    def nrm(k, shape, scale):
        return jax.random.normal(k, shape, f32) * scale

    def gain(k, shape):
        return 1.0 + 0.05 * jax.random.normal(k, shape, f32)

    return {
        "x": jax.random.normal(ks[0], (BATCH, SEQ, D_MODEL), f32),
        "w_in": nrm(ks[1], (DEPTH, D_MODEL, IN_WIDTH), D_MODEL ** -0.5),
        "conv_w": nrm(ks[2], (DEPTH, CONV_WIDTH, C_A), CONV_WIDTH ** -0.5),
        "conv_b": nrm(ks[3], (DEPTH, C_A), 0.02),
        "conv_ln_g": gain(ks[4], (DEPTH, C_A)),
        "conv_ln_b": nrm(ks[5], (DEPTH, C_A), 0.02),
        "pool_w": nrm(ks[6], (DEPTH, N_POOL_GROUPS, C_G, C_G), C_G ** -0.5),
        "pool_scale": gain(ks[7], (DEPTH, C_C)),
        "g_mix": gain(ks[8], (DEPTH, MIX_WIDTH)),
        "w_out": nrm(ks[9], (DEPTH, MIX_WIDTH, D_MODEL), MIX_WIDTH ** -0.5),
        "g_pre_mix": gain(ks[10], (DEPTH, D_MODEL)),
        "g_post_mix": gain(ks[11], (DEPTH, D_MODEL)),
        "g_pre_ffn": gain(ks[12], (DEPTH, D_MODEL)),
        "g_post_ffn": gain(ks[13], (DEPTH, D_MODEL)),
        "w_gate": nrm(ks[14], (DEPTH, D_MODEL, FFN_HIDDEN), D_MODEL ** -0.5),
        "w_up": nrm(ks[15], (DEPTH, D_MODEL, FFN_HIDDEN), D_MODEL ** -0.5),
        "w_down": nrm(ks[16], (DEPTH, FFN_HIDDEN, D_MODEL), FFN_HIDDEN ** -0.5),
    }

def first_block(x, w_in, conv_w, conv_b, conv_ln_g, conv_ln_b, pool_w, pool_scale, g_mix,
              w_out, g_pre_mix, g_post_mix, g_pre_ffn, g_post_ffn, w_gate, w_up, w_down):
    S = x.shape[1]
    cos, sin = rope_tables(S)
    a_end = 2 * C_A
    b_end = a_end + 3 * C_B
    for l in range(DEPTH):
        h = rmsnorm(x, g_pre_mix[l])
        proj = h @ w_in[l]
        y_a = conformer_conv(proj[..., :a_end], conv_w[l], conv_b[l], conv_ln_g[l], conv_ln_b[l])
        y_b = dilated_attention(proj[..., a_end:b_end], cos, sin)
        y_c = pool_mixer(proj[..., b_end:], pool_w[l], pool_scale[l])
        y = jnp.concatenate([rms_normalize(y_a), rms_normalize(y_b), rms_normalize(y_c)], axis=-1)
        y = (y * g_mix[l].astype(jnp.float32)).astype(x.dtype)
        x = x + rmsnorm(y @ w_out[l], g_post_mix[l])
        h = rmsnorm(x, g_pre_ffn[l])
        f = (jax.nn.silu(h @ w_gate[l]) * (h @ w_up[l])) @ w_down[l]
        x = x + rmsnorm(f, g_post_ffn[l])
    return x


DEPTH_2 = 1

D_MIX = D_MODEL
D_A = D_MIX // 4
D_B = D_MIX // 4
D_C = D_MIX // 4
D_D = D_MIX // 4
GDN_HEAD_DIM = 128
GDN_HEADS = D_A // GDN_HEAD_DIM
GDN_CONV = 4
GDN_CHUNK = 64
GDN_CHUNK_LOG2 = 6
LRU_BLOCKS = 8
LRU_BLOCK_DIM = D_B // LRU_BLOCKS
LRU_CONV = 4
LRU_C = 8.0
SGU_GROUPS = 4
SGU_GROUP_DIM = D_C // SGU_GROUPS
SGU_CHUNK = 128
SCONV_WIDTH = 3
D_FF = (D_MODEL * 11) // 4
FFN_CONV = 3
IN_SIZES = (D_A, D_A, D_A, D_A, GDN_HEADS, GDN_HEADS, D_B, D_B, 2 * D_C, D_D, D_D, D_D)
N_IN = 4 * D_A + 2 * GDN_HEADS + 2 * D_B + 2 * D_C + 3 * D_D


def _split(t, sizes):
    idx, acc = [], 0
    for s in sizes[:-1]:
        acc += s
        idx.append(acc)
    return jnp.split(t, idx, axis=-1)

def rms_norm(x, w):
    xf = x.astype(jnp.float32)
    y = xf * lax.rsqrt(jnp.mean(xf * xf, axis=-1, keepdims=True) + EPS)
    return (y * w.astype(jnp.float32)).astype(x.dtype)

def layer_norm(x, w, b):
    xf = x.astype(jnp.float32)
    mu = jnp.mean(xf, axis=-1, keepdims=True)
    xc = xf - mu
    y = xc * lax.rsqrt(jnp.mean(xc * xc, axis=-1, keepdims=True) + EPS)
    return y * w.astype(jnp.float32) + b.astype(jnp.float32)

def causal_dwconv(x, w, b=None):
    K, C = w.shape
    y = lax.conv_general_dilated(x, w[:, None, :].astype(x.dtype), window_strides=(1,),
                                 padding=[(K - 1, 0)], dimension_numbers=('NWC', 'WIO', 'NWC'),
                                 feature_group_count=C)
    if b is not None:
        y = y + b.astype(x.dtype)
    return y

def l2norm(t):
    return t * lax.rsqrt(jnp.sum(t * t, axis=-1, keepdims=True) + EPS)

def chunk_gated_delta_rule(q, k, v, g, beta):
    Bn, S, H, Dk = q.shape
    Dv = v.shape[-1]
    nC = S // GDN_CHUNK
    C = GDN_CHUNK
    q = l2norm(q) * (Dk ** -0.5)
    k = l2norm(k)

    def chunks(t):
        return t.reshape(Bn, nC, C, H, -1).transpose(0, 3, 1, 2, 4)

    qc, kc, vc = chunks(q), chunks(k), chunks(v)
    gc = g.reshape(Bn, nC, C, H).transpose(0, 3, 1, 2)
    bc = beta.reshape(Bn, nC, C, H).transpose(0, 3, 1, 2)
    gcum = jnp.cumsum(gc, axis=-1)
    causal = jnp.tril(jnp.ones((C, C), dtype=bool))
    strict = jnp.tril(jnp.ones((C, C), dtype=bool), -1)
    diff = gcum[..., :, None] - gcum[..., None, :]
    decay = jnp.where(causal, jnp.exp(jnp.where(causal, diff, 0.0)), 0.0)
    kb = kc * bc[..., None]
    M = jnp.where(strict, jnp.einsum('bhncd,bhnsd->bhncs', kb, kc) * decay, 0.0)
    N = -M
    T = jnp.eye(C, dtype=jnp.float32) + N
    P = N
    for _ in range(GDN_CHUNK_LOG2 - 1):
        P = jnp.einsum('bhnij,bhnjk->bhnik', P, P)
        T = T + jnp.einsum('bhnij,bhnjk->bhnik', T, P)
    w = jnp.einsum('bhncs,bhnsd->bhncd', T, kb * jnp.exp(gcum)[..., None])
    u = jnp.einsum('bhncs,bhnsd->bhncd', T, vc * bc[..., None])
    attn = jnp.where(causal, jnp.einsum('bhncd,bhnsd->bhncs', qc, kc) * decay, 0.0)
    q_g = qc * jnp.exp(gcum)[..., None]
    k_g = kc * jnp.exp(gcum[..., -1:] - gcum)[..., None]
    g_last = jnp.exp(gcum[..., -1])

    def step(state, inp):
        q_i, a_i, u_i, w_i, k_i, gl_i = inp
        v_new = u_i - jnp.einsum('bhck,bhkv->bhcv', w_i, state)
        o_i = jnp.einsum('bhck,bhkv->bhcv', q_i, state) + jnp.einsum('bhcs,bhsv->bhcv', a_i, v_new)
        state = state * gl_i[..., None, None] + jnp.einsum('bhck,bhcv->bhkv', k_i, v_new)
        return state, o_i

    xs = tuple(jnp.moveaxis(t, 2, 0) for t in (q_g, attn, u, w, k_g, g_last))
    s0 = jnp.zeros((Bn, H, Dk, Dv), jnp.float32)
    _, o = lax.scan(step, s0, xs)
    return o.transpose(1, 0, 3, 2, 4).reshape(Bn, S, H, Dv)

def gdn_mixer(q, k, v, z, b, a, conv_w, a_log, dt_bias, norm_w):
    Bn, S, _ = q.shape
    qkv = jax.nn.silu(causal_dwconv(jnp.concatenate([q, k, v], axis=-1), conv_w))
    q, k, v = jnp.split(qkv, 3, axis=-1)

    def heads(t):
        return t.reshape(Bn, S, GDN_HEADS, GDN_HEAD_DIM).astype(jnp.float32)

    beta = jax.nn.sigmoid(b.astype(jnp.float32))
    g = -jnp.exp(a_log.astype(jnp.float32)) * jax.nn.softplus(a.astype(jnp.float32) + dt_bias.astype(jnp.float32))
    o = chunk_gated_delta_rule(heads(q), heads(k), heads(v), g, beta)
    o = o * lax.rsqrt(jnp.mean(o * o, axis=-1, keepdims=True) + EPS) * norm_w.astype(jnp.float32) * jax.nn.silu(heads(z))
    return o.reshape(Bn, S, D_A).astype(z.dtype)

def lru_scan(a, b):
    def combine(l, r):
        return (l[0] * r[0], r[0] * l[1] + r[1])
    _, h = lax.associative_scan(combine, (a, b), axis=1)
    return h

def rglru_mixer(xb, gate, conv_w, conv_b, wa, ba, wx, bx, lam):
    Bn, S, _ = xb.shape
    xc = causal_dwconv(xb, conv_w, conv_b).astype(jnp.float32)
    xblk = xc.reshape(Bn, S, LRU_BLOCKS, LRU_BLOCK_DIM)
    r = jax.nn.sigmoid(jnp.einsum('bshi,hij->bshj', xblk, wa.astype(jnp.float32)) + ba.astype(jnp.float32)).reshape(Bn, S, D_B)
    i = jax.nn.sigmoid(jnp.einsum('bshi,hij->bshj', xblk, wx.astype(jnp.float32)) + bx.astype(jnp.float32)).reshape(Bn, S, D_B)
    log_a = -LRU_C * r * jax.nn.softplus(-lam.astype(jnp.float32))
    a = jnp.exp(log_a)
    mult = jnp.sqrt(-jnp.expm1(2.0 * log_a))
    h = lru_scan(a, mult * (i * xc))
    return (h * jax.nn.gelu(gate.astype(jnp.float32))).astype(xb.dtype)

def sgu_mixer(uv, ln_w, ln_b, ws, bs):
    Bn, S, _ = uv.shape
    uvf = jax.nn.gelu(uv.astype(jnp.float32))
    u, v = jnp.split(uvf, 2, axis=-1)
    v = layer_norm(v, ln_w, ln_b)
    v = v.reshape(Bn, S // SGU_CHUNK, SGU_CHUNK, SGU_GROUPS, SGU_GROUP_DIM)
    mask = jnp.tril(jnp.ones((SGU_CHUNK, SGU_CHUNK), dtype=bool))
    wsm = jnp.where(mask, ws.astype(jnp.float32), 0.0)
    v = jnp.einsum('gts,bnsgd->bntgd', wsm, v) + bs.astype(jnp.float32).T[:, :, None]
    return (u * v.reshape(Bn, S, D_C)).astype(uv.dtype)

def short_conv_mixer(bg, cg, hh, conv_w):
    return bg * causal_dwconv(cg * hh, conv_w)

def conv_ffn(h, up, conv_w, conv_b, down):
    hid = causal_dwconv(h @ up.astype(h.dtype), conv_w, conv_b)
    gate, val = jnp.split(hid, 2, axis=-1)
    return (jax.nn.gelu(gate) * val) @ down.astype(h.dtype)

def second_inputs(seed: int = 0) -> dict:
    key = jax.random.key(seed)
    ks = iter(jax.random.split(key, 48))
    L = DEPTH_2
    f32 = jnp.float32

    def nrm(shape, scale):
        return jax.random.normal(next(ks), shape, f32) * scale

    def gain(shape):
        return 1.0 + 0.1 * jax.random.normal(next(ks), shape, f32)

    def unif(shape, lo, hi):
        return jax.random.uniform(next(ks), shape, f32, lo, hi)

    s = unif((L, D_B), 0.9, 0.999) ** (1.0 / LRU_C)
    lru_lambda = jnp.log(s) - jnp.log1p(-s)
    dt = jnp.exp(unif((L, GDN_HEADS), float(np.log(1e-3)), float(np.log(1e-1))))
    gdn_dt_bias = dt + jnp.log(-jnp.expm1(-dt))
    return {
        "x": nrm((BATCH, SEQ, D_MODEL), 1.0),
        "pre_mix_norm": gain((L, D_MODEL)),
        "w_in": nrm((L, D_MODEL, N_IN), D_MODEL ** -0.5),
        "gdn_conv_w": nrm((L, GDN_CONV, 3 * D_A), GDN_CONV ** -0.5),
        "gdn_a_log": jnp.log(unif((L, GDN_HEADS), 1.0, 16.0)),
        "gdn_dt_bias": gdn_dt_bias,
        "gdn_norm_w": gain((L, GDN_HEAD_DIM)),
        "lru_conv_w": nrm((L, LRU_CONV, D_B), LRU_CONV ** -0.5),
        "lru_conv_b": nrm((L, D_B), 0.01),
        "lru_wa": nrm((L, LRU_BLOCKS, LRU_BLOCK_DIM, LRU_BLOCK_DIM), LRU_BLOCK_DIM ** -0.5),
        "lru_ba": nrm((L, LRU_BLOCKS, LRU_BLOCK_DIM), 0.01),
        "lru_wx": nrm((L, LRU_BLOCKS, LRU_BLOCK_DIM, LRU_BLOCK_DIM), LRU_BLOCK_DIM ** -0.5),
        "lru_bx": nrm((L, LRU_BLOCKS, LRU_BLOCK_DIM), 0.01),
        "lru_lambda": lru_lambda,
        "sgu_ln_w": gain((L, D_C)),
        "sgu_ln_b": nrm((L, D_C), 0.01),
        "sgu_ws": nrm((L, SGU_GROUPS, SGU_CHUNK, SGU_CHUNK), SGU_CHUNK ** -0.5),
        "sgu_b": gain((L, SGU_GROUPS, SGU_CHUNK)),
        "sconv_w": nrm((L, SCONV_WIDTH, D_D), SCONV_WIDTH ** -0.5),
        "grp_norm_w": gain((L, 3, D_B)),
        "w_out": nrm((L, D_MIX, D_MODEL), D_MIX ** -0.5),
        "post_mix_norm": gain((L, D_MODEL)),
        "pre_ffn_norm": gain((L, D_MODEL)),
        "ffn_up": nrm((L, D_MODEL, 2 * D_FF), D_MODEL ** -0.5),
        "ffn_conv_w": nrm((L, FFN_CONV, 2 * D_FF), FFN_CONV ** -0.5),
        "ffn_conv_b": nrm((L, 2 * D_FF), 0.01),
        "ffn_down": nrm((L, D_FF, D_MODEL), D_FF ** -0.5),
        "post_ffn_norm": gain((L, D_MODEL)),
    }

def second_block(x, pre_mix_norm, w_in, gdn_conv_w, gdn_a_log, gdn_dt_bias, gdn_norm_w,
              lru_conv_w, lru_conv_b, lru_wa, lru_ba, lru_wx, lru_bx, lru_lambda,
              sgu_ln_w, sgu_ln_b, sgu_ws, sgu_b, sconv_w, grp_norm_w, w_out,
              post_mix_norm, pre_ffn_norm, ffn_up, ffn_conv_w, ffn_conv_b, ffn_down,
              post_ffn_norm):
    for l in range(DEPTH_2):
        h = rms_norm(x, pre_mix_norm[l])
        p = h @ w_in[l].astype(h.dtype)
        (q, k, v, z, b_gdn, a_gdn, lru_x, lru_gate, sgu_uv, sc_b, sc_c, sc_h) = _split(p, IN_SIZES)
        y_a = gdn_mixer(q, k, v, z, b_gdn, a_gdn, gdn_conv_w[l], gdn_a_log[l], gdn_dt_bias[l], gdn_norm_w[l])
        y_b = rms_norm(rglru_mixer(lru_x, lru_gate, lru_conv_w[l], lru_conv_b[l], lru_wa[l], lru_ba[l],
                                   lru_wx[l], lru_bx[l], lru_lambda[l]), grp_norm_w[l, 0])
        y_c = rms_norm(sgu_mixer(sgu_uv, sgu_ln_w[l], sgu_ln_b[l], sgu_ws[l], sgu_b[l]), grp_norm_w[l, 1])
        y_d = rms_norm(short_conv_mixer(sc_b, sc_c, sc_h, sconv_w[l]), grp_norm_w[l, 2])
        y = jnp.concatenate([y_a, y_b, y_c, y_d], axis=-1) @ w_out[l].astype(h.dtype)
        x = x + rms_norm(y, post_mix_norm[l])
        h = rms_norm(x, pre_ffn_norm[l])
        y = conv_ffn(h, ffn_up[l], ffn_conv_w[l], ffn_conv_b[l], ffn_down[l])
        x = x + rms_norm(y, post_ffn_norm[l])
    return x


def setup_inputs(seed=0):
    out = dict(first_inputs(seed))
    for name, value in second_inputs(seed + 1).items():
        if name != "x":
            out[name + "_2"] = value
    return out


def reference(
    x, w_in, conv_w, conv_b, conv_ln_g, conv_ln_b, pool_w, pool_scale, g_mix, w_out, g_pre_mix,
    g_post_mix, g_pre_ffn, g_post_ffn, w_gate, w_up, w_down, pre_mix_norm_2, w_in_2,
    gdn_conv_w_2, gdn_a_log_2, gdn_dt_bias_2, gdn_norm_w_2, lru_conv_w_2, lru_conv_b_2,
    lru_wa_2, lru_ba_2, lru_wx_2, lru_bx_2, lru_lambda_2, sgu_ln_w_2, sgu_ln_b_2, sgu_ws_2,
    sgu_b_2, sconv_w_2, grp_norm_w_2, w_out_2, post_mix_norm_2, pre_ffn_norm_2, ffn_up_2,
    ffn_conv_w_2, ffn_conv_b_2, ffn_down_2, post_ffn_norm_2,
):
    x = first_block(
        x, w_in, conv_w, conv_b, conv_ln_g, conv_ln_b, pool_w, pool_scale, g_mix, w_out,
        g_pre_mix, g_post_mix, g_pre_ffn, g_post_ffn, w_gate, w_up, w_down,
    )
    return second_block(
        x, pre_mix_norm_2, w_in_2, gdn_conv_w_2, gdn_a_log_2, gdn_dt_bias_2, gdn_norm_w_2,
        lru_conv_w_2, lru_conv_b_2, lru_wa_2, lru_ba_2, lru_wx_2, lru_bx_2, lru_lambda_2,
        sgu_ln_w_2, sgu_ln_b_2, sgu_ws_2, sgu_b_2, sconv_w_2, grp_norm_w_2, w_out_2,
        post_mix_norm_2, pre_ffn_norm_2, ffn_up_2, ffn_conv_w_2, ffn_conv_b_2, ffn_down_2,
        post_ffn_norm_2,
    )


_drawn_inputs = setup_inputs


def setup_inputs(seed=0):
    import zlib

    import numpy as np

    out = dict(_drawn_inputs(seed))
    spreads = {}
    factors = {'conv_ln_b': 3.332,
     'gdn_norm_w_2': 4.47,
     'lru_conv_b_2': 8.0,
     'lru_ba_2': 200.0,
     'lru_bx_2': 64.0,
     'sgu_ln_w_2': 143.401,
     'sgu_ln_b_2': 200.0,
     'sgu_b_2': 95.551,
     'ffn_conv_b_2': 8.0,
     'lru_wa_2': 3.282}
    for name, (base, spread) in spreads.items():
        noise = np.random.default_rng([zlib.crc32(name.encode()), seed]).standard_normal(out[name].shape)
        drawn = base * np.exp(spread * noise) if base else spread * noise
        out[name] = __import__('jax').numpy.asarray(drawn.astype(out[name].dtype))
    for name, factor in factors.items():
        out[name] = (out[name] * factor).astype(out[name].dtype)
    return out
```

```python
from contextlib import ExitStack

import numpy as np

import concourse.bass as bass
from concourse import mybir

F32 = mybir.dt.float32
F32R = mybir.dt.float32r
ALU = mybir.AluOpType
ACT = mybir.ActivationFunctionType
AX = mybir.AxisListType.X

P = 128
S = 256
NT = S // P
D = 2048
KT = D // P
FF = 5632
FKT = FF // P
DEPTH = 2
EPS = 1e-6
NEG = -1e30
RING = 4
CHUNK = 512
UNIT = 1024

C_ID, C_ONE, C_CAUSAL, C_STRICT, C_CAUSAL_T, C_TRIL = (P * i for i in range(6))
C_ROPE = 6 * P
C_END = C_ROPE + 2 * NT * 8
K_BIAS = 0
K_INV = 2 * S
K_END = K_INV + 4 * S


def shape_constants():
    c = np.zeros((P, C_END), np.float32)
    i = np.arange(P)
    same = (i[:, None] // 64) == (i[None, :] // 64)
    c[:, C_ID:C_ID + P] = np.eye(P)
    c[:, C_ONE:C_ONE + P] = 1.0
    c[:, C_CAUSAL:C_CAUSAL + P] = same & (i[:, None] >= i[None, :])
    c[:, C_STRICT:C_STRICT + P] = same & (i[:, None] > i[None, :])
    c[:, C_CAUSAL_T:C_CAUSAL_T + P] = same & (i[:, None] <= i[None, :])
    c[:, C_TRIL:C_TRIL + P] = i[:, None] >= i[None, :]
    pos = np.arange(S, dtype=np.float32)
    inv = np.float32(500000.0) ** (-np.arange(0, 16, 2, dtype=np.float32) / np.float32(16))
    ang = (pos[:, None] * inv[None, :]).astype(np.float32).reshape(NT, P, 8).transpose(1, 0, 2)
    c[:, C_ROPE:C_ROPE + 16] = np.cos(ang).reshape(P, 16)
    c[:, C_ROPE + 16:C_ROPE + 32] = np.sin(ang).reshape(P, 16)
    k = np.zeros((P, K_END), np.float32)
    q, key = np.arange(S)[:, None], np.arange(S)[None, :]
    count = (abs(q - key) <= 64).astype(int) + ((q - key) % 4 == 0) + ((q - key) % 16 == 0)
    bias = np.where(count > 0, np.log(np.maximum(count, 1)), NEG).astype(np.float32)
    k[:, 0:2 * S] = bias.reshape(NT, P, S).transpose(1, 0, 2).reshape(P, NT * S)
    t = np.arange(S)
    for n, win in enumerate((2, 4, 8, 16)):
        size = np.clip(t + win - win // 2, 0, S) - np.clip(t - win // 2, 0, S)
        k[:, K_INV + n * S:K_INV + (n + 1) * S] = (1.0 / size.astype(np.float32))[None, :]
    return c, k


U_IN1, U_OUT, U_UP, U_DOWN = 9 * 8, 2 * KT, 22 * 8, 2 * FKT
U_LAYER = U_IN1 + U_OUT + U_UP + U_DOWN
U_IN2 = 11 * 8
T_IN1, N_IN1, T_LAYER = 3, 6, 3 + 22
OUT_ORDER = [0, 1, 2, 3, 12, 13, 14, 15, 4, 5, 6, 7, 8, 9, 10, 11]
TAPS = 31
IN2 = dict(q=0, k=512, v=1024, lru_x=2056, lru_gate=2568, sc_b=4104, sc_c=4616, sc_h=5128, z=1536, sgu_u=3080, sgu_v=3592)
T_IN2 = 8
BA = 2048
OUT_ORDER2 = [12, 13, 14, 15, 4, 5, 6, 7, 8, 9, 10, 11, 0, 1, 2, 3]


def build(nc, a, out, stop=None):
    with ExitStack() as ctx:
        def sb(name, shape, dt=F32):
            return ctx.enter_context(nc.sbuf_tensor(name, shape, dt))

        def sem(name):
            return ctx.enter_context(nc.semaphore(name))

        x = sb("x", [P, NT, D])
        XT = sb("XT", [P, KT, 2, S], F32R)
        WS = sb("WS", [P, RING, UNIT])
        WH = sb("WH", [P, RING, UNIT], F32R)
        WL = sb("WL", [P, RING, UNIT], F32R)
        XL = sb("XL", [P, 4, S])
        T1 = sb("T1", [P, 1032])
        T2 = sb("T2", [P, 1024])
        T3 = sb("T3", [P, 1024])
        C = sb("C", [P, C_END])
        PR = sb("PR", [P, 512])
        ROWS = sb("ROWS", [P, 2, P])
        SM = sb("SM", [P, 160])
        w_bah = sb("w_bah", [P, KT, 8], F32R)
        w_bal = sb("w_bal", [P, KT, 8], F32R)
        with nc.sbuf_tensor("HT", [P, FKT, 2, S], F32R) as HT:
            pass
        SCR = sb("SCR", [P, FKT * 2 * S])
        PS = ctx.enter_context(nc.psum_tensor("PS", [P, 8, CHUNK], F32))

        def scr(at, *dims):
            n = int(np.prod(dims))
            v = SCR[:, at:at + n]
            if len(dims) == 2:
                v = v.rearrange("p (a b) -> p a b", a=dims[0])
            if len(dims) == 3:
                v = v.rearrange("p (a b c) -> p a b c", a=dims[0], b=dims[1])
            return v

        ident = C[:, C_ID:C_ID + P]
        ones = C[:, C_ONE:C_ONE + P]

        xs = scr(9528, NT, D)
        junk = scr(4216, NT, D)
        aT, gT = scr(0, 4, S), scr(1024, 4, S)
        HP = S + TAPS - 1
        hpad = scr(2048, 4, HP)
        acc = scr(3192, 4, S)
        UP = S + 16
        upad = scr(4216, 4, UP)
        win_a, win_b = scr(5304, 4, UP), scr(6392, 4, UP)
        pooled = scr(7480, 4, S)
        ycT = scr(8504, 4, S)
        q_nat, k_nat, v_nat = scr(9528, NT, 1024), scr(11576, NT, 1024), scr(13624, NT, 1024)
        qT, kT = scr(15672, 8, S), scr(17720, 8, S)
        KC = scr(19768, K_END)
        rope = scr(21304, 4, 128)
        pw = scr(21816, 4, P)
        neg_s = scr(0, 2, NT * S)
        prob = scr(1024, 2, NT * S)
        probT = scr(2048, 2, NT * S)
        y_b = q_nat
        yb_n = k_nat
        gbc = (T1, T2)
        tmp = scr(0, 2, NT, 1024)
        sq = T3[:, :].rearrange("p (a b) -> p a b", a=4)
        f3 = lambda t: t[:, 0:1024].rearrange("p (a b) -> p a b", a=4)
        flat = lambda v: v.rearrange("p a b -> p (a b)")

        LB = DEPTH
        TB = LB * T_LAYER
        qkv_pad = scr(0, 12, S + 3)
        k_by, v_by, kbg = (scr(1024 * i, 8, P) for i in range(3))
        qkvT = scr(3108, 12, S)
        qh, kh, vh = (qkvT[:, 4 * i:4 * i + 4, :] for i in range(3))
        sc_b, sc_c, sc_pad = scr(6180, 4, S), scr(7204, 4, S), scr(8228, 4, S + 2)
        lru_pad, lru_gate, lru_xc = scr(9260, 4, S + 3), scr(10296, 4, S), scr(11320, 4, S)
        lru_r, lru_i = scr(12344, 4, S), scr(13368, 4, S)
        z, sgu_u, sgu_v = (scr(14392 + 1024 * i, NT, 512) for i in range(3))
        dec, decT, Pm, PmT = (scr(17464 + 1024 * i, 8, P) for i in range(4))
        wa_bd, wx_bd = scr(17464, 4, P), scr(17976, 4, P)
        sgu_lnw, sgu_lnb = scr(18488, 512), scr(19000, 512)
        sgu_ws, sgu_wsT = scr(19512, 4, P), scr(20024, 4, P)
        w_ba = scr(20536, KT, 8)
        state = scr(21560, 4, P)
        wT, u_by, kg = Pm, PmT, dec
        o_by, k_sq = scr(0, 8, P), scr(1024, 8, P)
        egrow = T1[:, 0:1024].rearrange("p (a b) -> p a b", a=8)
        v_beta = T2[:, :].rearrange("p (a b) -> p a b", a=8)
        Tt = T3[:, :].rearrange("p (a b) -> p a b", a=8)
        rows2 = T3[:, 0:5 * P].rearrange("p (a b) -> p a b", a=5)
        ffn_pad = T1[:, :].rearrange("p (a b) -> p a b", a=4)
        conv_j = C[:, C_ROPE:C_ROPE + 32].rearrange("p (k g n) -> p k g n", k=4, g=2)
        mask = lambda at: C[:, at:at + P][:, None, :].to_broadcast((P, 8, P))
        eight = lambda v: v[:, :, None].to_broadcast((P, 8, P))
        pair = lambda b: PS[:, b:b + 2, :].rearrange("p a (m c) -> p (a m) c", c=P)
        quad = lambda b: PS[:, b:b + 2, :].rearrange("p a (m c) -> p (a m) c", c=S)

        ss, rms, rinv = SM[:, 0:2], SM[:, 2:4], SM[:, 4:6]
        ssf, ssf2, rmsf, rinvf = SM[:, 6:10], SM[:, 10:12], SM[:, 12:14], SM[:, 14:16]
        neg_max = SM[:, 16:20]
        den = SM[:, 20:52]
        rden = SM[:, 52:84]
        ssb, rmsb, rinvb = SM[:, 84:86], SM[:, 86:88], SM[:, 88:90]
        epsc, epsc_q, onec = SM[:, 90:91], SM[:, 91:92], SM[:, 92:93]
        gate_in = SM[:, 96:108]
        gate_abs, gate_ln = SM[:, 108:120], SM[:, 120:132]
        a_log, dt_bias = SM[:, 132:136], SM[:, 136:140]
        g_tok, beta, nbeta = SM[:, 16:24], SM[:, 24:32], SM[:, 32:40]
        gcum, gbeta, gtail = SM[:, 40:48], SM[:, 48:56], SM[:, 56:64]
        o_ss, o_rms, o_rinv = SM[:, 64:72], SM[:, 72:80], SM[:, 80:88]
        vm, vv, vs, vr = (SM[:, 140 + 2 * i:142 + 2 * i] for i in range(4))
        cs, cr, ci = (SM[:, 148 + 2 * i:150 + 2 * i] for i in range(3))
        rate = SM[:, 154:158]
        (G2_PRE, G2_FFN, G2_GRP, G2_GDN, L_CB, L_LAM, L_BA, L_BX, L_CW, S_CW, SGU_B) = (
            0, 16, 32, 44, 45, 49, 53, 57, 61, 77, 89)
        GDN_CW, F_CW = 93, 141
        G_PRE, G_FFN, G_MIX, CONV_B, LN_G, LN_B, POOL_SC, CONV_W = 0, 16, 32, 48, 52, 56, 60, 64
        col = lambda i: PR[:, i:i + 1]

        s_stage = [sem(f"s_stage{i}") for i in range(RING)]
        s_hi, s_lo, s_pe = sem("s_hi"), sem("s_lo"), sem("s_pe")
        s_const, s_xload, s_eps = sem("s_const"), sem("s_xload"), sem("s_eps")
        s_rows, s_prt, s_par = sem("s_rows"), sem("s_prt"), sem("s_par")
        s_x = sem("s_x")
        s_ss, s_rms, s_rinv, s_xs, s_tr, s_xh, s_xt = (sem("s_" + n) for n in "ss rms rinv xs tr xh xt".split())
        s_xl, s_freeT, s_freeN = (sem("s_" + n) for n in "xl freeT freeN".split())
        s_sg, s_pad, s_glu, s_cv = (sem("s_" + n) for n in "sg pad glu cv".split())
        s_act, s_h, s_hh, s_ht = (sem("s_" + n) for n in "act h hh ht".split())
        s_gb, s_sf, s_sfs, s_rf, s_rfi, s_pn = (sem("s_" + n) for n in "gb sf sfs rf rfi pn".split())
        s_pool, s_mix, s_yc = (sem("s_" + n) for n in "pool mix yc".split())
        s_rope, s_roped, s_qkt, s_qk = (sem("s_" + n) for n in "rope roped qkt qk".split())
        s_S, s_sb, s_nm, s_p, s_ptr, s_pt, s_o, s_rd, s_yb = (sem("s_" + n) for n in "S sb nm p ptr pt o rd yb".split())
        s_sqr, s_col, s_std, s_rstd, s_ya, s_ycn, s_lna = (sem("s_" + n) for n in "sqr col std rstd ya ycn lna".split())
        s_ssb, s_rb, s_rbi, s_ybn, s_ybt, s_yh, s_yt = (sem("s_" + n) for n in "ssb rb rbi ybn ybt yh yt".split())
        s_out, s_kc = sem("s_out"), sem("s_kc")
        s_rows2, s_prt2, s_par2, s_w2, s_bd = (sem("s2_" + n) for n in "rows prt par small bd".split())
        s_pad2, s_wb, s_wbl, s_ba = (sem("s2_" + n) for n in "pad wb wbl ba".split())
        s_qc, s_qs, s_l2s, s_l2m, s_l2r, s_l2n = (sem("s2_" + n) for n in "qconv qsilu l2sq l2sum l2root l2n".split())
        s_kv, s_kvb = sem("s2_kvT"), sem("s2_kv_by")
        s_dc, s_ac = sem("s2_dve_chain"), sem("s2_act_chain")
        s_gin, s_gln, s_g, s_gcm, s_gcum, s_grow = (sem("s2_" + n) for n in "gin gln g gcm gcum grow".split())
        s_dd, s_de, s_dm, s_kk, s_P, s_Pt, s_att = (sem("s2_" + n) for n in "dd de dm kk P Pt att".split())
        s_sq, s_te, s_tt = (sem("s2_" + n) for n in "sq te tt".split())
        s_fac, s_kbg, s_wu, s_wue = (sem("s2_" + n) for n in "fac kbg wu wue".split())
        s_vn, s_vne, s_os, s_oe, s_st, s_qg = (sem("s2_" + n) for n in "vn vne os oe st qg".split())
        s_on, s_ot = sem("s2_on"), sem("s2_ot")
        s_lm, s_lg, s_la, s_lt, s_lr, s_lsq, s_ly = (sem("s2_" + n) for n in "lm lg la lt lrec lsqrt ly".split())
        s_sy, s_csq, s_csum, s_crt, s_cn = (sem("s2_" + n) for n in "sy csq csum croot cn".split())
        s_gelu, s_gn, s_wsm, s_gm, s_gy, s_gyn, s_gyt = (sem("s2_" + n) for n in "gelu gn wsm gm gy gyn gyt".split())
        s_groot, s_wst, s_eg, s_fac2, s_pte, s_on2, s_tap, s_fc = (sem("s2_" + n) for n in "groot wst eg fac2 pte on2 tap fc".split())
        s_lc, s_scv, s_lix, s_gvn, s_wue2, s_ks, s_oz, s_fc2 = (sem("s2_" + n) for n in "lc scv lix gvn wue2 ks oz fc2".split())
        s_zs, s_y2h, s_y2t, s_cj = (sem("s2_" + n) for n in "zs y2h y2t cj".split())

        block = ctx.enter_context(nc.Block())

        @block.sync
        def _(sp):
            def load(q, i, src, width):
                sp.wait_ge(s_lo, 4 * q + i + 1)
                dst = WS[:, i % RING, :]
                if width:
                    dst = dst.rearrange("p (k n) -> p k n", n=width)
                sp.dma_start(dst, src).then_inc(s_stage[i % RING], 16)

            def chunk512(q, w, c):
                for i in range(8):
                    load(q, i, w[2 * i * P:(2 * i + 2) * P, c].rearrange("(k p) n -> p k n", p=P), CHUNK)

            def out_proj(q, w):
                for c in range(2):
                    for i, kt in enumerate(OUT_ORDER):
                        load(q, 16 * c + i, w[kt * P:(kt + 1) * P, c * 1024:(c + 1) * 1024], 0)

            def down_proj(q, w):
                for c in range(2):
                    with sp.Fori(0, FKT // 4) as r:
                        rows = w.rearrange("(r k p) n -> r k p n", k=4, p=P)
                        for i in range(4):
                            load(q + r + 11 * c, i, rows[r, i, :, c * 1024:(c + 1) * 1024], 0)

            sp.dma_start(C[:, :], a["constants"]).then_inc(s_const, 16)
            for t in range(NT):
                sp.dma_start(x[:, t, :], a["x"][0, t * P:(t + 1) * P, :]).then_inc(s_xload, 16)
            with sp.Fori(0, DEPTH) as l:
                q = l * (U_LAYER // 4)
                sp.wait_ge(s_eps, 1)
                sp.wait_ge(s_prt, 2 * l)
                small = [("g_pre_mix", 16), ("g_pre_ffn", 16), ("g_mix", 16), ("conv_b", 4), ("conv_ln_g", 4),
                         ("conv_ln_b", 4), ("pool_scale", 4)]
                at = 0
                for name, n in small:
                    sp.dma_start(ROWS[at:at + n, 0, :], a[name][l].rearrange("(n p) -> n p", p=P)).then_inc(s_rows, 16)
                    at += n
                sp.dma_start(ROWS[0:4 * TAPS, 1, :], a["conv_w"][l].rearrange("j (n p) -> (j n) p", p=P)).then_inc(s_rows, 16)
                w = a["w_in"][l]
                order = [0, 1, 8, 2, 4, 6, 3, 5, 7]
                for n, c in enumerate(order):
                    chunk512(q + 2 * n, w, slice(c * CHUNK, (c + 1) * CHUNK))
                q1 = q + U_IN1 // 4
                out_proj(q1, a["w_out"][l])
                q2 = q1 + U_OUT // 4
                with sp.Fori(0, 11) as j:
                    chunk512(q2 + 4 * j, a["w_gate"][l], bass.ds(j * CHUNK, CHUNK))
                    chunk512(q2 + 4 * j + 2, a["w_up"][l], bass.ds(j * CHUNK, CHUNK))
                q3 = q2 + U_UP // 4
                down_proj(q3, a["w_down"][l])
            q = DEPTH * (U_LAYER // 4)
            for n, c in enumerate(IN2.values()):
                chunk512(q + 2 * n, a["w_in_2"][0], slice(c, c + CHUNK))
            q += U_IN2 // 4
            for c in range(2):
                for i, kt in enumerate(OUT_ORDER2):
                    load(q, 16 * c + i, a["w_out_2"][0, kt * P:(kt + 1) * P, c * 1024:(c + 1) * 1024], 0)
            q += U_OUT // 4
            with sp.Fori(0, 11) as j:
                chunk512(q + 4 * j, a["ffn_up_2"][0], bass.ds(j * CHUNK, CHUNK))
                chunk512(q + 4 * j + 2, a["ffn_up_2"][0], bass.ds(j * CHUNK + FF, CHUNK))
            q += U_UP // 4
            down_proj(q, a["ffn_down_2"][0])
            sp.wait_ge(s_x, 2 + 2 * 2 * (DEPTH + 1))
            for t in range(NT):
                sp.dma_start(out[0, t * P:(t + 1) * P, :], x[:, t, :]).then_inc(s_out, 16)
            sp.wait_ge(s_out, 32)

        def attention_act(act, l):
            for half in range(2):
                for w, dst in enumerate((qT, kT)):
                    i = 2 * half + w
                    act.wait_ge(s_qkt, 4 * l + i + 1)
                    act.activation(dst[:, 4 * half:4 * half + 4, :].rearrange("p a b -> p (a b)"),
                                   PS[:, 2 * i:2 * i + 2, :].rearrange("p a b -> p (a b)"), ACT.Copy).then_inc(s_qk, 1)
            for i in range(17):
                if i < 16:
                    h = i
                    act.wait_ge(s_nm, 16 * l + h + 1)
                    if h >= 2:
                        act.wait_ge(s_ptr, 16 * l + h - 1)
                    for t in range(NT):
                        ins = act.activation(prob[:, h % 2, t * S:(t + 1) * S], neg_s[:, h % 2, t * S:(t + 1) * S], ACT.Exp,
                                             bias=neg_max[:, 2 * (h % 2) + t:2 * (h % 2) + t + 1], scale=-1.0,
                                             accum_out=den[:, 2 * h + t:2 * h + t + 1])
                    ins.then_inc(s_p, 1)
                if i >= 1:
                    h = i - 1
                    act.wait_ge(s_ptr, 16 * l + h + 1)
                    if h >= 2:
                        act.wait_ge(s_o, 16 * l + h - 1)
                    act.activation(probT[:, h % 2, :], PS[:, 2 + h % 2, :], ACT.Copy).then_inc(s_pt, 1)
            act.wait_ge(s_lna, 3 * l + 1)
            act.activation(sq, acc, ACT.Square).then_inc(s_sqr, 1)
            act.wait_ge(s_col, 4 * l + 2)
            act.activation(aT[:, 0, :], PS[:, 6, 0:S], ACT.Sqrt, scale=1.0 / 512, bias=epsc).then_inc(s_std, 1)
            act.wait_ge(s_lna, 3 * l + 2)
            for n in range(4):
                ins = act.activation(acc[:, n, :], acc[:, n, :], ACT.Silu, scale=col(LN_G + n), bias=col(LN_B + n))
            ins.then_inc(s_lna, 1)
            act.wait_ge(s_lna, 3 * l + 3)
            act.activation(sq, acc, ACT.Square).then_inc(s_sqr, 1)
            act.wait_ge(s_col, 4 * l + 3)
            act.activation(aT[:, 0, :], PS[:, 6, 0:S], ACT.Sqrt, scale=1.0 / 512, bias=epsc).then_inc(s_std, 1)
            act.wait_ge(s_mix, l + 1)
            for n in range(4):
                ins = act.activation(ycT[:, n, :], PS[:, 4 + n // 2, (n % 2) * S:(n % 2 + 1) * S], ACT.Copy,
                                     scale=col(POOL_SC + n))
            ins.then_inc(s_yc, 1)
            act.wait_ge(s_yc, l + 1)
            act.activation(sq, ycT, ACT.Square).then_inc(s_sqr, 1)
            act.wait_ge(s_col, 4 * l + 4)
            act.wait_ge(s_rstd, 3 * l + 2)
            act.activation(aT[:, 0, :], PS[:, 6, 0:S], ACT.Sqrt, scale=1.0 / 512, bias=epsc).then_inc(s_std, 1)

        def ffn_act(act, splits, evac_low, q, l, ti):
            with act.Fori(0, 11) as j:
                qj = q + 4 * j
                splits(qj, 4, 12)
                evac_low(qj, 7, ti + 2 * j, 0)
                act.wait_ge(s_freeT, ti + 2 * j + 1)
                act.activation(f3(T1), f3(T1), ACT.Silu).then_inc(s_act, 1)
                splits(qj, 12, 20)
                evac_low(qj, 15, ti + 2 * j + 1, 4)
                act.wait_ge(s_h, 11 * l + j + 1)
                act.activation(HT[:, bass.ds(4 * j, 4), 0, :], f3(T3), ACT.Copy).then_inc(s_hh, 1)

        def mixers2_act(act):
            chain = [0]

            def link(ins):
                chain[0] += 1
                ins.then_inc(s_ac, 1)
                act.wait_ge(s_ac, chain[0])

            def root_of_sums(k):
                act.wait_ge(s_csum, k)
                act.activation(XL[:, 0, :], PS[:, 6, 0:S], ACT.Sqrt, scale=1.0 / 512, bias=epsc).then_inc(s_crt, 1)

            def high(i0, src, g, signal, value):
                act.wait_ge(signal, value)
                for i in range(4):
                    act.activation(XT[:, OUT_ORDER2[i0 + i], 0, :], src(i), ACT.Copy, scale=col(g + i)).then_inc(s_y2h, 1)

            act.wait_ge(s_gin, 1)
            link(act.activation(gate_abs, gate_in, ACT.Abs))
            link(act.activation(gate_abs, gate_abs, ACT.Exp, scale=-1.0))
            act.activation(gate_ln, gate_abs, ACT.Ln, bias=onec).then_inc(s_gln, 1)
            act.activation(a_log, a_log, ACT.Exp).then_inc(s_gln, 1)
            ba = PS[:, 7, 0:16].rearrange("p (t n) -> p t n", t=NT)
            act.activation(beta.rearrange("p (t h) -> p t h", t=NT), ba[:, :, 0:4], ACT.Sigmoid).then_inc(s_gln, 1)
            act.wait_ge(s_sy, 1)
            act.activation(f3(T1), sc_b, ACT.Square).then_inc(s_csq, 1)
            root_of_sums(1)
            act.wait_ge(s_lm, 1)
            for k, (dst, b) in enumerate(((lru_r, L_BA), (lru_i, L_BX))):
                for n in range(4):
                    ins = act.activation(dst[:, n, :], quad(2 if k == 0 else 4)[:, n, :], ACT.Sigmoid, bias=col(b + n))
                ins.then_inc(s_lg, 1)
            act.wait_ge(s_la, 1)
            act.activation(f3(T1), lru_r, ACT.Tanh).then_inc(s_lt, 1)
            act.activation(f3(T2), lru_r, ACT.Exp).then_inc(s_lt, 1)
            act.wait_ge(s_lr, 1)
            act.activation(f3(T1), f3(T1), ACT.Sqrt).then_inc(s_lsq, 1)
            act.activation(lru_gate, lru_gate, ACT.Gelu_apprx_tanh).then_inc(s_lsq, 1)
            act.wait_ge(s_ly, 1)
            act.activation(f3(T1), lru_xc, ACT.Square).then_inc(s_csq, 1)
            high(0, lambda i: sc_b[:, i, :], G2_GRP + 8, s_cn, 1)
            root_of_sums(2)
            act.activation(sgu_v, sgu_v, ACT.Gelu_apprx_tanh).then_inc(s_gelu, 1)
            act.activation(sgu_u, sgu_u, ACT.Gelu_apprx_tanh).then_inc(s_gelu, 1)
            act.wait_ge(s_gn, 1)
            for t in range(NT):
                link(act.activation(T1[:, 512 * t:512 * t + 512], sgu_v[:, t, :], ACT.Square, accum_out=vv[:, t:t + 1]))
            act.activation(vs, vv, ACT.Sqrt, scale=1.0 / 512, bias=epsc).then_inc(s_groot, 1)
            act.wait_ge(s_wsm, 2)
            act.activation(sgu_wsT.rearrange("p a b -> p (a b)"), PS[:, 2, :], ACT.Copy).then_inc(s_wst, 1)
            high(4, lambda i: lru_xc[:, i, :], G2_GRP, s_cn, 2)
            act.wait_ge(s_gy, 1)
            for t in range(NT):
                link(act.activation(T1[:, 512 * t:512 * t + 512], sgu_v[:, t, :], ACT.Square, accum_out=cs[:, t:t + 1]))
            act.activation(cr, cs, ACT.Sqrt, scale=1.0 / 512, bias=epsc).then_inc(s_groot, 1)
            act.wait_ge(s_gyt, 2)
            high(8, lambda i: quad(6)[:, i, :], G2_GRP + 4, s_gyt, 2)
            act.wait_ge(s_qc, 48)
            act.activation(qkvT.rearrange("p a b -> p (a b)"), qkvT.rearrange("p a b -> p (a b)"), ACT.Silu).then_inc(s_qs, 1)
            act.wait_ge(s_qs, 1)
            for k, src in enumerate((qh, kh)):
                if k:
                    act.wait_ge(s_l2m, 1)
                act.activation(f3(T1), src, ACT.Square).then_inc(s_l2s, 1)
            for k in range(2):
                act.wait_ge(s_l2m, k + 1)
                act.activation(f3(T2) if k == 0 else f3(T3), quad(2 if k == 0 else 4), ACT.Sqrt, scale=128.0 if k == 0 else 1.0,
                               bias=epsc_q if k == 0 else epsc).then_inc(s_l2r, 1)
            act.wait_ge(s_kv, 2)
            act.activation(k_by, pair(2), ACT.Copy).then_inc(s_kvb, 1)
            act.activation(v_by, pair(4), ACT.Copy).then_inc(s_kvb, 1)
            act.wait_ge(s_gcm, 1)
            act.activation(gcum, PS[:, 6, 0:8], ACT.Copy).then_inc(s_gcum, 1)
            act.wait_ge(s_grow, 1)
            act.activation(egrow, pair(2), ACT.Exp).then_inc(s_eg, 1)
            for k, d in enumerate((dec, decT)):
                act.wait_ge(s_dd, k + 1)
                act.activation(d, d, ACT.Exp).then_inc(s_de, 1)
            link(act.activation(gbeta, gcum, ACT.Exp))
            act.wait_ge(s_fac, 1)
            act.activation(gtail, gtail, ACT.Exp).then_inc(s_fac2, 1)
            act.wait_ge(s_Pt, 1)
            act.activation(PmT, pair(4), ACT.Copy).then_inc(s_pte, 1)
            act.wait_ge(s_tt, 1)
            for r in range(4):
                act.wait_ge(s_sq, 2 * r + 2)
                act.activation(PmT, pair(4), ACT.Copy).then_inc(s_pte, 1)
            act.wait_ge(s_fac, 2)
            for m in range(8):
                ins = act.activation(kbg[:, m, :], k_by[:, m, :], ACT.Copy, scale=gbeta[:, m:m + 1])
            ins.then_inc(s_kbg, 1)
            for m in range(8):
                ins = act.activation(v_beta[:, m, :], v_by[:, m, :], ACT.Copy, scale=beta[:, m:m + 1])
            ins.then_inc(s_kbg, 1)
            for m in range(8):
                ins = act.activation(kg[:, m, :], k_by[:, m, :], ACT.Copy, scale=gtail[:, m:m + 1])
            ins.then_inc(s_kbg, 1)
            act.wait_ge(s_wu, 1)
            act.activation(wT, pair(2), ACT.Copy).then_inc(s_wue, 1)
            for n in range(4):
                t, r = n // 2, 64 * (n % 2)
                act.wait_ge(s_os, n + 1)
                act.activation(o_by[r:r + 64, 4 * t:4 * t + 4, :].rearrange("p a b -> p (a b)"), PS[r:r + 64, 3, :],
                               ACT.Copy).then_inc(s_oe, 1)
            act.activation(z, z, ACT.Silu).then_inc(s_zs, 1)
            act.wait_ge(s_on, 1)
            act.activation(o_rms, o_ss, ACT.Sqrt, scale=1.0 / P, bias=epsc).then_inc(s_on2, 1)
            act.wait_ge(s_ot, 1)
            for i in range(4):
                act.activation(XT[:, i, 0, :], quad(6)[:, i, :], ACT.Copy, scale=col(G2_GDN)).then_inc(s_y2h, 1)

        def ffn2_act(act, splits, evac_low, q):
            ti = TB + T_IN2
            with act.Fori(0, 11) as j:
                qj = q + 4 * j
                for g, dst in ((0, T2), (1, T3)):
                    splits(qj, 4 + 8 * g, 12 + 8 * g)
                    evac_low(qj, 7 + 8 * g, ti + 2 * j + g, 4 * g)
                    act.wait_ge(s_freeT, ti + 2 * j + g + 1)
                    act.wait_ge(s_cj, j + 1)
                    for n in range(4):
                        ins = act.activation(f3(dst)[:, n, :], ffn_pad[:, n, 2:2 + S], ACT.Identity, scale=conv_j[:, 2, g, n:n + 1],
                                             bias=conv_j[:, 3, g, n:n + 1])
                    ins.then_inc(s_tap, 1)
                    if g == 0:
                        act.wait_ge(s_fc, 2 * j + 1)
                        act.activation(f3(T2), f3(T2), ACT.Gelu_apprx_tanh).then_inc(s_act, 1)
                act.wait_ge(s_h, 11 * LB + j + 1)
                act.activation(HT[:, bass.ds(4 * j, 4), 0, :], f3(T3), ACT.Copy).then_inc(s_hh, 1)

        @block.scalar
        def _(act):
            def split(q, i):
                act.wait_ge(s_stage[i % RING], 16 * (q + i // RING + 1))
                act.wait_ge(s_pe, 4 * q + i + 1)
                act.activation(WH[:, i % RING, :], WS[:, i % RING, :], ACT.Copy).then_inc(s_hi, 1)

            def splits(q, i0, i1):
                for i in range(i0, i1):
                    split(q, i)

            def product_done(q, i):
                act.wait_ge(s_pe, 4 * q + i + 5)

            def evac_low(q, i, ti, base):
                product_done(q, i)
                act.wait_ge(s_freeT, ti)
                act.activation(XL[:, :, :], PS[:, base:base + 4, S:2 * S], ACT.Copy).then_inc(s_xl, 1)

            def norm_in(n, g):
                for t in range(NT):
                    act.wait_ge(s_x, 2 * n + t + 1)
                    act.activation(junk[:, t, :], x[:, t, :], ACT.Square, accum_out=ss[:, t:t + 1]).then_inc(s_ss, 1)
                for t in range(NT):
                    act.wait_ge(s_ss, 2 * n + t + 1)
                    act.activation(rms[:, t:t + 1], ss[:, t:t + 1], ACT.Sqrt, scale=1.0 / D, bias=epsc).then_inc(s_rms, 1)
                for kt in range(KT):
                    if kt % 2 == 0:
                        act.wait_ge(s_tr, 8 * n + kt // 2 + 1)
                    act.activation(XT[:, kt, 0, :], PS[:, kt // 2, (kt % 2) * S:(kt % 2 + 1) * S], ACT.Copy,
                                   scale=col(g + kt)).then_inc(s_xh, 1)

            def load_post_weight(gname_row):
                for h in range(2):
                    act.dma_start(gbc[h][:, 0:1024], gname_row[:, h * 1024:(h + 1) * 1024].to_broadcast((P, 1024))).then_inc(s_gb, 16)

            def post_squares(m, c):
                for t in range(NT):
                    if t + c:
                        act.wait_ge(s_sf, 4 * m + 2 * c + t)
                    act.activation(XL[:, :, :].rearrange("p a b -> p (a b)"),
                                   PS[:, 4 * c + 2 * t:4 * c + 2 * t + 2, :].rearrange("p a b -> p (a b)"), ACT.Square,
                                   accum_out=ssf[:, 2 * c + t:2 * c + t + 1]).then_inc(s_sf, 1)

            def post_root(m):
                act.wait_ge(s_sfs, m + 1)
                act.activation(rmsf, ssf2, ACT.Sqrt, scale=1.0 / D, bias=epsc).then_inc(s_rf, 1)

            def y_high(kt, src, g):
                act.activation(XT[:, kt, 0, :], src, ACT.Copy, scale=g).then_inc(s_yh, 1)

            def wide_phase(q, m, n_units, first=4, last=False):
                for c in range(2):
                    splits(q, n_units * c + (4 if c else first), n_units * (c + 1) + (0 if c and last else 4))
                    product_done(q, n_units * c + n_units - 1)
                    post_squares(m, c)
                post_root(m)

            act.wait_ge(s_eps, 2)
            act.wait_ge(s_const, 16)
            splits(0, 0, 4)
            with act.Fori(0, DEPTH) as l:
                q = l * (U_LAYER // 4)
                act.wait_ge(s_prt, 2 * l + 2)
                act.activation(PR[:, 0:64], PS[:, 0, 0:64], ACT.Copy).then_inc(s_par, 1)
                act.activation(PR[:, 64:64 + P], PS[:, 0, P:2 * P], ACT.Copy).then_inc(s_par, 1)
                act.wait_ge(s_par, 2 * l + 2)
                norm_in(2 * l, G_PRE)
                act.dma_start(KC, a["key_constants"]).then_inc(s_kc, 16)
                act.dma_start(pw, a["pool_w"][l].rearrange("g c d -> c g d")).then_inc(s_kc, 16)
                ti, ni = l * T_LAYER, l * N_IN1
                for c in range(9):
                    splits(q, 8 * c + 4, 8 * c + 12)
                    if c < 3:
                        evac_low(q, 8 * c + 7, ti + c, 4 * (c % 2))
                        if c == 1:
                            act.wait_ge(s_freeT, ti + 2)
                            act.activation(f3(T1), gT, ACT.Sigmoid).then_inc(s_sg, 1)
                    else:
                        n = c - 3
                        base = 4 * (c % 2)
                        dst = (q_nat, k_nat, v_nat)[n % 3]
                        half = n // 3
                        product_done(q, 8 * c + 7)
                        for t in range(NT):
                            ins = act.activation(dst[:, t, half * 512:(half + 1) * 512], PS[:, base + t, :], ACT.Copy,
                                                 scale=0.125 if n % 3 == 0 else 1.0)
                        ins.then_inc(s_freeN, 1)
                act.wait_ge(s_glu, l + 1)
                load_post_weight(a["g_post_mix"][bass.ds(l, 1)])
                attention_act(act, l)
                for i in range(8):
                    kt = OUT_ORDER[i]
                    src = acc if i < 4 else ycT
                    act.wait_ge(s_ya if i < 4 else s_ycn, l + 1)
                    y_high(kt, src[:, i % 4, :], col(G_MIX + kt))
                for t in range(NT):
                    act.wait_ge(s_yb, 4 * l + 4)
                    act.activation(scr(1024 * t, 1024), y_b[:, t, :], ACT.Square, accum_out=ssb[:, t:t + 1]).then_inc(s_ssb, 1)
                act.wait_ge(s_ssb, 2 * l + 2)
                act.activation(rmsb, ssb, ACT.Sqrt, scale=1.0 / 1024, bias=epsc).then_inc(s_rb, 1)
                splits(q + U_IN1 // 4, 4, 12)
                for i in range(8):
                    if i % 2 == 0:
                        act.wait_ge(s_ybt, 4 * l + i // 2 + 1)
                    y_high(4 + i, PS[:, 4 + i // 2, (i % 2) * S:(i % 2 + 1) * S], col(G_MIX + 4 + i))
                wide_phase(q + U_IN1 // 4, 2 * l, KT, 12)
                norm_in(2 * l + 1, G_FFN)
                ffn_act(act, splits, evac_low, q + (U_IN1 + U_OUT) // 4, l, ti + T_IN1)
                act.wait_ge(s_h, 11 * l + 11)
                load_post_weight(a["g_post_ffn"][bass.ds(l, 1)])
                wide_phase(q + (U_IN1 + U_OUT + U_UP) // 4, 2 * l + 1, FKT)

            a2 = lambda n: a[n + "_2"][0]
            act.wait_ge(s_x, 4 * LB + 2)
            at = 0
            for name, n in (("pre_mix_norm", 16), ("pre_ffn_norm", 16), ("grp_norm_w", 12), ("gdn_norm_w", 1), ("lru_conv_b", 4),
                            ("lru_lambda", 4), ("lru_ba", 4), ("lru_bx", 4), ("lru_conv_w", 16), ("sconv_w", 12), ("sgu_b", 4)):
                v = a2(name)
                if name in ("lru_ba", "lru_bx"):
                    v = v.rearrange("(n h) p -> n (h p)", h=2)
                elif name == "gdn_norm_w":
                    v = v.rearrange("(n p) -> n p", p=P)
                elif len(v.shape) == 1:
                    v = v.rearrange("(n p) -> n p", p=P)
                elif name != "sgu_b":
                    v = v.rearrange("j (n p) -> (j n) p", p=P)
                act.dma_start(rows2[at:at + n, 0, :], v).then_inc(s_rows2, 16)
                at += n
            act.dma_start(rows2[0:48, 1, :], a2("gdn_conv_w").rearrange("j (n p) -> (j n) p", p=P)).then_inc(s_rows2, 16)
            taps = a2("ffn_conv_w").rearrange("j (n p) -> (j n) p", p=P)
            act.dma_start(rows2[:, 2, :], taps[0:128]).then_inc(s_rows2, 16)
            act.dma_start(rows2[:, 3, :], taps[128:256]).then_inc(s_rows2, 16)
            act.dma_start(rows2[0:8, 4, :], taps[256:264]).then_inc(s_rows2, 16)
            act.dma_start(rows2[8:96, 4, :], a2("ffn_conv_b").rearrange("(n p) -> n p", p=P)).then_inc(s_rows2, 16)
            act.dma_start(w_ba, a2("w_in")[:, BA:BA + 8].rearrange("(k p) n -> p k n", p=P)).then_inc(s_w2, 16)
            act.dma_start(a_log, a["gdn_a_log_2"].to_broadcast((P, 4))).then_inc(s_w2, 16)
            act.dma_start(dt_bias, a["gdn_dt_bias_2"].to_broadcast((P, 4))).then_inc(s_w2, 16)
            act.dma_start(sgu_lnw, a["sgu_ln_w_2"].to_broadcast((P, 512))).then_inc(s_w2, 16)
            act.dma_start(sgu_lnb, a["sgu_ln_b_2"].to_broadcast((P, 512))).then_inc(s_w2, 16)
            act.dma_start(sgu_ws, a2("sgu_ws").rearrange("g t s -> t g s")).then_inc(s_w2, 16)
            act.wait_ge(s_bd, 2)
            for w, bd in (("lru_wa", wa_bd), ("lru_wx", wx_bd)):
                m = a2(w).rearrange("(n b) i j -> b i n j", b=2)
                for b in range(2):
                    act.dma_start(bd[64 * b:64 * b + 64, :, 64 * b:64 * b + 64], m[b]).then_inc(s_w2, 16)
            act.wait_ge(s_prt2, 5)
            for r, (at, n) in enumerate(((0, 93), (GDN_CW, 48), (F_CW, 128), (F_CW + 128, 128), (F_CW + 256, 96))):
                act.activation(PR[:, at:at + n], PS[:, r // 4, (r % 4) * P:(r % 4) * P + n], ACT.Copy).then_inc(s_par2, 1)
            act.wait_ge(s_par2, 5)
            norm_in(2 * LB, G2_PRE)
            act.wait_ge(s_w2, 160)
            act.activation(w_bah[:, :, :], w_ba, ACT.Copy).then_inc(s_wb, 1)
            q = DEPTH * (U_LAYER // 4)
            for c in range(11):
                splits(q, 8 * c + 4, 8 * c + 12)
                if c < T_IN2:
                    evac_low(q, 8 * c + 7, TB + c, 4 * (c % 2))
                else:
                    product_done(q, 8 * c + 7)
                    dst = (z, sgu_u, sgu_v)[c - T_IN2]
                    for t in range(NT):
                        ins = act.activation(dst[:, t, :], PS[:, 4 * (c % 2) + t, :], ACT.Copy)
                    ins.then_inc(s_freeN, 1)
            mixers2_act(act)
            q += U_IN2 // 4
            load_post_weight(a["post_mix_norm_2"])
            wide_phase(q, 2 * LB, KT)
            norm_in(2 * LB + 1, G2_FFN)
            q += U_OUT // 4
            ffn2_act(act, splits, evac_low, q)
            act.wait_ge(s_h, 11 * LB + 11)
            load_post_weight(a["post_ffn_norm_2"])
            q += U_UP // 4
            wide_phase(q, 2 * LB + 1, FKT, last=True)

        def divide_heads(dve, l, g):
            dve.wait_ge(s_o, 16 * l + 4 * g + 4)
            dve.reciprocal(rden[:, 8 * g:8 * g + 8], den[:, 8 * g:8 * g + 8]).then_inc(s_rd, 1)
            dve.wait_ge(s_rd, 4 * l + g + 1)
            o = PS[:, 4 + g % 2, :].rearrange("p (h t e) -> p h t e", h=4, t=NT)
            r = rden[:, 8 * g:8 * g + 8].rearrange("p (h t) -> p h t", t=NT)
            dst = y_b[:, :, 256 * g:256 * g + 256].rearrange("p t (h e) -> p h t e", e=64)
            dve.tensor_tensor(dst, o, r[:, :, :, None].to_broadcast((P, 4, NT, 64)), ALU.mult).then_inc(s_yb, 1)

        def attention_dve(dve, l):
            dve.wait_ge(s_kc, 32 * (l + 1))
            for i in range(18):
                if i < 16:
                    h = i
                    dve.wait_ge(s_S, 16 * l + h + 1)
                    if h >= 2:
                        dve.wait_ge(s_p, 16 * l + h - 1)
                    dve.scalar_tensor_tensor(out=neg_s[:, h % 2, :], in0=PS[:, h % 2, :], scalar=-1.0,
                                             in1=KC[:, K_BIAS:K_BIAS + 2 * S], op0=ALU.mult, op1=ALU.subtract).then_inc(s_sb, 1)
                    dve.wait_ge(s_sb, 16 * l + h + 1)
                    dve.tensor_reduce(neg_max[:, 2 * (h % 2):2 * (h % 2) + 2],
                                      neg_s[:, h % 2, :].rearrange("p (t k) -> p t k", t=NT), AX, ALU.min).then_inc(s_nm, 1)
                if i >= 5 and (i - 5) % 4 == 0:
                    g = (i - 5) // 4
                    divide_heads(dve, l, g)
            dve.wait_ge(s_cv, 4 * TAPS * (l + 1))
            dve.wait_ge(s_col, 4 * l + 1)
            mean = PS[:, 6, 0:S]
            for n in range(4):
                ins = dve.scalar_tensor_tensor(out=acc[:, n, :], in0=mean, scalar=-1.0 / 512, in1=acc[:, n, :],
                                               op0=ALU.mult, op1=ALU.add)
            ins.then_inc(s_lna, 1)

            def scale_by_root(k, y, signal):
                dve.wait_ge(s_std, 3 * l + k + 1)
                dve.reciprocal(aT[:, 1, :], aT[:, 0, :]).then_inc(s_rstd, 1)
                dve.wait_ge(s_rstd, 3 * l + k + 1)
                dve.tensor_tensor(y, y, aT[:, 1:2, :].to_broadcast((P, 4, S)), ALU.mult).then_inc(signal, 1)

            dve.wait_ge(s_lna, 3 * l + 1)
            scale_by_root(0, acc, s_lna)
            scale_by_root(1, acc, s_ya)
            dve.wait_ge(s_ya, l + 1)
            scale_by_root(2, ycT, s_ycn)

        def ffn_dve(dve, splits, evac, q, l, ti):
            with dve.Fori(0, 11) as j:
                qj = q + 4 * j
                splits(qj, 4, 12)
                evac(ti + 2 * j, 0, f3(T1))
                splits(qj, 12, 20)
                evac(ti + 2 * j + 1, 4, f3(T2))
                dve.wait_ge(s_act, 11 * l + j + 1)
                dve.wait_ge(s_freeT, ti + 2 * j + 2)
                dve.tensor_tensor(f3(T3), f3(T1), f3(T2), ALU.mult).then_inc(s_h, 1)
                dve.wait_ge(s_hh, 11 * l + j + 1)
                dve.tensor_tensor(HT[:, bass.ds(4 * j, 4), 1, :], f3(T3), HT[:, bass.ds(4 * j, 4), 0, :].bitcast(F32),
                                  ALU.subtract).then_inc(s_ht, 1)

        def conv_ops(dve, dst, pad, tiles, taps, w0, b0, signal):
            ops = []
            count = [0]

            def op(tile, j, before):
                def run():
                    w = col(w0 + tiles * j + tile)
                    if j == 0:
                        if b0 is None:
                            ins = dve.tensor_scalar(dst[:, tile, :], pad[:, tile, 0:S], w, None, ALU.mult)
                        else:
                            ins = dve.tensor_scalar(dst[:, tile, :], pad[:, tile, 0:S], w, col(b0 + tile), ALU.mult, ALU.add)
                    else:
                        dve.wait_ge(signal, before)
                        ins = dve.scalar_tensor_tensor(out=dst[:, tile, :], in0=pad[:, tile, j:j + S], scalar=w,
                                                       in1=dst[:, tile, :], op0=ALU.mult, op1=ALU.add)
                    ins.then_inc(signal, 1)
                return run

            n = 0
            for g in range(tiles // 4):
                for j in range(taps):
                    for k in range(4):
                        ops.append(op(4 * g + k, j, n - 3))
                        n += 1
            return ops

        def mixers2_dve(dve, splits, q_out):
            chain = [0]

            def link(ins):
                chain[0] += 1
                ins.then_inc(s_dc, 1)
                dve.wait_ge(s_dc, chain[0])

            def over_root(k, y, signal, value):
                dve.wait_ge(s_crt, k)
                link(dve.reciprocal(XL[:, 1, :], XL[:, 0, :]))
                dve.tensor_tensor(y, y, XL[:, 1:2, :].to_broadcast((P, 4, S)), ALU.mult).then_inc(signal, 1)

            def low(i0, src, g):
                for i in range(4):
                    kt = OUT_ORDER2[i0 + i]
                    dve.wait_ge(s_y2h, i0 + i + 1 if i0 < 8 else i0 + 4)
                    dve.scalar_tensor_tensor(out=XT[:, kt, 1, :], in0=src(i), scalar=col(g + i) if i0 < 12 else col(g),
                                             in1=XT[:, kt, 0, :].bitcast(F32), op0=ALU.mult, op1=ALU.subtract).then_inc(s_y2t, 1)

            dve.wait_ge(s_ba, 1)
            ba = PS[:, 7, 0:16].rearrange("p (t n) -> p t n", t=NT)
            link(dve.tensor_tensor(gate_in[:, 0:8].rearrange("p (t h) -> p t h", t=NT), ba[:, :, 4:8],
                                   dt_bias[:, None, :].to_broadcast((P, NT, 4)), ALU.add))
            dve.tensor_scalar(gate_in[:, 8:12], PR[:, L_LAM:L_LAM + 4], -1.0, None, ALU.mult).then_inc(s_gin, 1)
            dve.wait_ge(s_freeT, TB + 8)
            link(dve.tensor_tensor(sc_pad[:, :, 2:2 + S], sc_pad[:, :, 2:2 + S], sc_c, ALU.mult))
            for f in conv_ops(dve, sc_c, sc_pad, 4, 3, S_CW, None, s_scv):
                f()
            dve.wait_ge(s_scv, 12)
            dve.tensor_tensor(sc_b, sc_b, sc_c, ALU.mult).then_inc(s_sy, 1)
            dve.wait_ge(s_gin, 1)
            dve.wait_ge(s_gln, 3)
            link(dve.tensor_scalar(gate_in, gate_in, 0.0, None, ALU.max))
            link(dve.tensor_tensor(gate_in, gate_in, gate_ln, ALU.add))
            link(dve.tensor_scalar(rate, gate_in[:, 8:12], -8.0, None, ALU.mult))
            dve.scalar_tensor_tensor(out=g_tok.rearrange("p (t h) -> p t h", t=NT),
                                     in0=gate_in[:, 0:8].rearrange("p (t h) -> p t h", t=NT), scalar=-1.0,
                                     in1=a_log[:, None, :].to_broadcast((P, NT, 4)), op0=ALU.mult, op1=ALU.mult).then_inc(s_g, 1)
            dve.tensor_scalar(nbeta, beta, -1.0, None, ALU.mult).then_inc(s_g, 1)
            over_root(1, sc_b, s_cn, 1)
            dve.wait_ge(s_lg, 2)
            for n in range(4):
                ins = dve.tensor_scalar(lru_r[:, n, :], lru_r[:, n, :], rate[:, n:n + 1], None, ALU.mult)
            ins.then_inc(s_la, 1)
            dve.tensor_tensor(lru_i, lru_i, lru_xc, ALU.mult).then_inc(s_lix, 1)
            dve.wait_ge(s_lt, 2)
            link(dve.tensor_scalar(lru_r, f3(T1), -1.0, 1.0, ALU.mult, ALU.add))
            link(dve.reciprocal(lru_r, lru_r))
            dve.scalar_tensor_tensor(out=f3(T1), in0=f3(T1), scalar=-2.0, in1=lru_r, op0=ALU.mult, op1=ALU.mult).then_inc(s_lr, 1)
            dve.wait_ge(s_lsq, 1)
            dve.wait_ge(s_lix, 1)
            link(dve.tensor_tensor(lru_i, lru_i, f3(T1), ALU.mult))
            for n in range(4):
                ins = dve.tensor_tensor_scan(lru_xc[:, n, :], f3(T2)[:, n, :], lru_i[:, n, :], 0.0, ALU.mult, ALU.add)
            link(ins)
            dve.wait_ge(s_lsq, 2)
            dve.tensor_tensor(lru_xc, lru_xc, lru_gate, ALU.mult).then_inc(s_ly, 1)
            low(0, lambda i: sc_b[:, i, :], G2_GRP + 8)
            over_root(2, lru_xc, s_cn, 2)
            dve.wait_ge(s_gelu, 1)
            link(dve.tensor_reduce(vm, sgu_v, AX, ALU.add))
            link(dve.tensor_scalar(vm, vm, -1.0 / 512, None, ALU.mult))
            for t in range(NT):
                ins = dve.tensor_scalar(sgu_v[:, t, :], sgu_v[:, t, :], vm[:, t:t + 1], None, ALU.add)
            ins.then_inc(s_gn, 1)
            link(dve.tensor_tensor(sgu_ws, sgu_ws, C[:, C_TRIL:C_TRIL + P][:, None, :].to_broadcast((P, 4, P)), ALU.mult))
            dve.sem_inc(s_wsm, 1)
            dve.wait_ge(s_groot, 1)
            link(dve.reciprocal(vr, vs))
            for t in range(NT):
                ins = dve.scalar_tensor_tensor(out=sgu_v[:, t, :], in0=sgu_v[:, t, :], scalar=vr[:, t:t + 1], in1=sgu_lnw,
                                               op0=ALU.mult, op1=ALU.mult)
            link(ins)
            dve.tensor_tensor(sgu_v, sgu_v, sgu_lnb[:, None, :].to_broadcast((P, NT, 512)), ALU.add).then_inc(s_gvn, 1)
            low(4, lambda i: lru_xc[:, i, :], G2_GRP)
            dve.wait_ge(s_gm, 1)
            dve.wait_ge(s_gelu, 2)
            for t in range(NT):
                for g in range(4):
                    ins = dve.scalar_tensor_tensor(out=sgu_v[:, t, g * P:(g + 1) * P], in0=PS[:, 4 + t, g * P:(g + 1) * P],
                                                   scalar=col(SGU_B + g), in1=sgu_u[:, t, g * P:(g + 1) * P],
                                                   op0=ALU.add, op1=ALU.mult)
            ins.then_inc(s_gy, 1)
            dve.wait_ge(s_groot, 2)
            link(dve.reciprocal(ci, cr))
            for t in range(NT):
                dve.tensor_scalar(sgu_v[:, t, :], sgu_v[:, t, :], ci[:, t:t + 1], None, ALU.mult).then_inc(s_gyn, 1)
            low(8, lambda i: quad(6)[:, i, :], G2_GRP + 4)
            for k, (y, r) in enumerate(((qh, T2), (kh, T3))):
                dve.wait_ge(s_l2r, k + 1)
                link(dve.reciprocal(f3(r), f3(r)))
                dve.tensor_tensor(y, y, f3(r), ALU.mult).then_inc(s_l2n, 1)
            dve.wait_ge(s_gcum, 1)
            dve.wait_ge(s_eg, 1)
            for k, (d, at) in enumerate(((dec, C_STRICT), (decT, C_CAUSAL_T))):
                for m in range(8):
                    if k == 0:
                        ins = dve.tensor_scalar(d[:, m, :], pair(2)[:, m, :], -1.0, gcum[:, m:m + 1], ALU.mult, ALU.add)
                    else:
                        ins = dve.tensor_scalar(d[:, m, :], pair(2)[:, m, :], gcum[:, m:m + 1], None, ALU.subtract)
                link(ins)
                dve.tensor_tensor(d, d, mask(at), ALU.mult).then_inc(s_dd, 1)
            for r in (0, 64):
                ins = dve.tensor_tensor(gtail[r:r + 64, :], pair(2)[r:r + 64, :, r + 63], gcum[r:r + 64, :], ALU.subtract)
            ins.then_inc(s_fac, 1)
            for k, (d, at) in enumerate(((dec, C_STRICT), (decT, C_CAUSAL_T))):
                dve.wait_ge(s_de, k + 1)
                dve.tensor_tensor(d, d, mask(at), ALU.mult).then_inc(s_dm, 1)
            dve.wait_ge(s_fac2, 1)
            dve.tensor_tensor(gbeta, gbeta, beta, ALU.mult).then_inc(s_fac, 1)
            dve.wait_ge(s_dm, 1)
            dve.wait_ge(s_kk, 1)
            for m in range(8):
                ins = dve.scalar_tensor_tensor(out=Pm[:, m, :], in0=pair(6)[:, m, :], scalar=nbeta[:, m:m + 1], in1=dec[:, m, :],
                                               op0=ALU.mult, op1=ALU.mult)
            ins.then_inc(s_P, 1)
            dve.wait_ge(s_kk, 2)
            dve.wait_ge(s_dm, 2)
            dve.tensor_tensor(decT, pair(2), decT, ALU.mult).then_inc(s_att, 1)
            dve.wait_ge(s_pte, 1)
            dve.tensor_tensor(Tt, PmT, mask(C_ID), ALU.add).then_inc(s_tt, 1)
            for r in range(5):
                dve.wait_ge(s_sq, min(2 * r + 2, 9))
                dve.tensor_copy(Pm, pair(2)).then_inc(s_P, 1)
                dve.wait_ge(s_te, r + 1)
                dve.tensor_tensor(Tt, Tt, pair(6), ALU.add).then_inc(s_tt, 1)
            dve.wait_ge(s_wu, 2)
            dve.tensor_copy(u_by, pair(4)).then_inc(s_wue2, 1)
            dve.tensor_tensor(qh.rearrange("p h (t c) -> p t h c", t=NT), qh.rearrange("p h (t c) -> p t h c", t=NT),
                              egrow.rearrange("p (t h) c -> p t h c", t=NT), ALU.mult).then_inc(s_qg, 1)
            for n in range(4):
                t, r = n // 2, 64 * (n % 2)
                u = u_by[r:r + 64, 4 * t:4 * t + 4, :].rearrange("p a b -> p (a b)")
                if n:
                    dve.wait_ge(s_vn, n)
                    dve.tensor_tensor(u, u, PS[r:r + 64, 2, :], ALU.subtract).then_inc(s_vne, 1)
                if n < 3:
                    dve.wait_ge(s_ks, n + 1)
                    if n:
                        dve.wait_ge(s_os, n + 1)
                        dve.wait_ge(s_st, n)
                    for h in range(4):
                        if n == 0:
                            ins = dve.tensor_copy(state[:, h, :], PS[:, 6, h * P:(h + 1) * P])
                        else:
                            m = 4 * t + h
                            ins = dve.scalar_tensor_tensor(out=state[:, h, :], in0=state[:, h, :],
                                                           scalar=egrow[:, m, r + 63:r + 64], in1=PS[:, 6, h * P:(h + 1) * P],
                                                           op0=ALU.mult, op1=ALU.add)
                    ins.then_inc(s_st, 1)
            dve.wait_ge(s_oe, 4)
            link(dve.tensor_tensor(k_sq, o_by, o_by, ALU.mult))
            dve.tensor_reduce(o_ss, k_sq, AX, ALU.add).then_inc(s_on, 1)
            dve.wait_ge(s_on2, 1)
            link(dve.reciprocal(o_rinv, o_rms))
            link(dve.tensor_tensor(o_by, o_by, eight(o_rinv), ALU.mult))
            dve.wait_ge(s_zs, 1)
            zz = z.rearrange("p t (h c) -> p (t h) c", c=P)
            dve.tensor_tensor(o_by, o_by, zz, ALU.mult).then_inc(s_oz, 1)
            low(12, lambda i: quad(6)[:, i, :], G2_GDN)

        def ffn2_dve(dve, splits, evac, q):
            ti = TB + T_IN2
            dve.memset(ffn_pad[:, :, 0:2], 0.0).then_inc(s_pad2, 1)
            with dve.Fori(0, 11) as j:
                qj = q + 4 * j
                for k in range(4):
                    for g in range(2):
                        ins = dve.tensor_copy(conv_j[:, k, g, :], PR[:, bass.ds(4 * j + (F_CW + 88 * k + 44 * g), 4)])
                ins.then_inc(s_cj, 1)
                for g, dst in ((0, T2), (1, T3)):
                    splits(qj, 4 + 8 * g, 12 + 8 * g)
                    evac(ti + 2 * j + g, 4 * g, ffn_pad[:, :, 2:2 + S])
                    dve.wait_ge(s_tap, 2 * j + g + 1)
                    for k in range(2):
                        if k:
                            dve.wait_ge(s_fc2, 2 * j + g + 1)
                        for n in range(4):
                            ins = dve.scalar_tensor_tensor(out=f3(dst)[:, n, :], in0=ffn_pad[:, n, k:k + S],
                                                           scalar=conv_j[:, k, g, n:n + 1], in1=f3(dst)[:, n, :],
                                                           op0=ALU.mult, op1=ALU.add)
                        ins.then_inc(s_fc if k else s_fc2, 1)
                dve.wait_ge(s_act, 11 * LB + j + 1)
                dve.wait_ge(s_fc, 2 * j + 2)
                dve.tensor_tensor(f3(T3), f3(T3), f3(T2), ALU.mult).then_inc(s_h, 1)
                dve.wait_ge(s_hh, 11 * LB + j + 1)
                dve.tensor_tensor(HT[:, bass.ds(4 * j, 4), 1, :], f3(T3), HT[:, bass.ds(4 * j, 4), 0, :].bitcast(F32),
                                  ALU.subtract).then_inc(s_ht, 1)

        @block.vector
        def _(dve):
            def split(q, i):
                dve.wait_ge(s_hi, 4 * q + i + 1)
                dve.tensor_tensor(WL[:, i % RING, :], WS[:, i % RING, :], WH[:, i % RING, :].bitcast(F32),
                                  ALU.subtract).then_inc(s_lo, 1)

            def splits(q, i0, i1):
                for i in range(i0, i1):
                    split(q, i)

            def evac(ti, base, dst):
                dve.wait_ge(s_xl, ti + 1)
                dve.tensor_tensor(dst, PS[:, base:base + 4, 0:S], XL[:, :, :], ALU.add).then_inc(s_freeT, 1)

            def norm_in(n, g):
                for t in range(NT):
                    dve.wait_ge(s_rms, 2 * n + t + 1)
                    dve.reciprocal(rinv[:, t:t + 1], rms[:, t:t + 1]).then_inc(s_rinv, 1)
                    dve.wait_ge(s_rinv, 2 * n + t + 1)
                    dve.tensor_scalar(xs[:, t, :], x[:, t, :], rinv[:, t:t + 1], None, ALU.mult).then_inc(s_xs, 1)
                for kt in range(KT):
                    dve.wait_ge(s_xh, 16 * n + 2 * (kt // 2) + 2)
                    dve.scalar_tensor_tensor(out=XT[:, kt, 1, :], in0=PS[:, kt // 2, (kt % 2) * S:(kt % 2 + 1) * S],
                                             scalar=col(g + kt), in1=XT[:, kt, 0, :].bitcast(F32), op0=ALU.mult,
                                             op1=ALU.subtract).then_inc(s_xt, 1)

            def post(m):
                dve.wait_ge(s_sf, 4 * m + 4)
                dve.tensor_tensor(ssf2, ssf[:, 0:2], ssf[:, 2:4], ALU.add).then_inc(s_sfs, 1)
                dve.wait_ge(s_rf, m + 1)
                dve.reciprocal(rinvf, rmsf).then_inc(s_rfi, 1)
                dve.wait_ge(s_rfi, m + 1)
                dve.wait_ge(s_gb, 32 * (m + 1))
                for t in range(NT):
                    for c in range(2):
                        dve.scalar_tensor_tensor(
                            out=tmp[:, c, t, :], in0=PS[:, 4 * c + 2 * t:4 * c + 2 * t + 2, :].rearrange("p a b -> p (a b)"),
                            scalar=rinvf[:, t:t + 1], in1=gbc[c][:, 0:1024], op0=ALU.mult, op1=ALU.mult).then_inc(s_pn, 1)

            def conv(l, i0, i1):
                for i in range(i0, i1):
                    j, n = divmod(i, 4)
                    if i == 0:
                        dve.wait_ge(s_glu, l + 1)
                    if j:
                        dve.wait_ge(s_cv, 4 * TAPS * l + i - 3)
                    w = col(CONV_W + 4 * j + n)
                    if j == 0:
                        dve.tensor_scalar(acc[:, n, :], hpad[:, n, 0:S], w, col(CONV_B + n), ALU.mult, ALU.add).then_inc(s_cv, 1)
                    else:
                        dve.scalar_tensor_tensor(out=acc[:, n, :], in0=hpad[:, n, j:j + S], scalar=w, in1=acc[:, n, :],
                                                 op0=ALU.mult, op1=ALU.add).then_inc(s_cv, 1)

            dve.memset(ROWS[:, :, :], 0.0).then_inc(s_eps, 1)
            dve.memset(epsc, EPS).then_inc(s_eps, 1)
            dve.sem_inc(s_lo, 4)
            dve.wait_ge(s_xload, 32)
            dve.sem_inc(s_x, 2)
            splits(0, 0, 4)
            with dve.Fori(0, DEPTH) as l:
                q = l * (U_LAYER // 4)
                dve.wait_ge(s_par, 2 * l + 2)
                norm_in(2 * l, G_PRE)
                ti = l * T_LAYER
                for v in (hpad[:, :, 0:15], hpad[:, :, 15 + S:HP], upad[:, :, 0:8], upad[:, :, 8 + S:UP]):
                    ins = dve.memset(v, 0.0)
                ins.then_inc(s_pad, 1)
                done = 0
                for c in range(9):
                    for i in range(8 * c + 4, 8 * c + 12):
                        split(q, i)
                        if c >= 2 and done < 4 * TAPS:
                            nxt = min(done + 3, 4 * TAPS)
                            conv(l, done, nxt)
                            done = nxt
                    if c < 3:
                        evac(ti + c, 4 * (c % 2), (aT, gT, upad[:, :, 8:8 + S])[c])
                    if c == 1:
                        dve.wait_ge(s_sg, l + 1)
                        dve.wait_ge(s_freeT, ti + 1)
                        dve.tensor_tensor(hpad[:, :, 15:15 + S], aT, f3(T1), ALU.mult).then_inc(s_glu, 1)
                assert done == 4 * TAPS
                attention_dve(dve, l)
                for i in range(8):
                    kt = OUT_ORDER[i]
                    src = (acc if i < 4 else ycT)[:, i % 4, :]
                    dve.wait_ge(s_yh, 16 * l + i + 1)
                    dve.scalar_tensor_tensor(out=XT[:, kt, 1, :], in0=src, scalar=col(G_MIX + kt),
                                             in1=XT[:, kt, 0, :].bitcast(F32), op0=ALU.mult, op1=ALU.subtract).then_inc(s_yt, 1)
                dve.wait_ge(s_rb, l + 1)
                dve.reciprocal(rinvb, rmsb).then_inc(s_rbi, 1)
                dve.wait_ge(s_rbi, l + 1)
                for t in range(NT):
                    dve.tensor_scalar(yb_n[:, t, :], y_b[:, t, :], rinvb[:, t:t + 1], None, ALU.mult).then_inc(s_ybn, 1)
                splits(q + U_IN1 // 4, 4, 12)
                for i in range(8):
                    kt = 4 + i
                    dve.wait_ge(s_yh, 16 * l + 8 + 2 * (i // 2) + 2)
                    dve.scalar_tensor_tensor(out=XT[:, kt, 1, :], in0=PS[:, 4 + i // 2, (i % 2) * S:(i % 2 + 1) * S],
                                             scalar=col(G_MIX + kt), in1=XT[:, kt, 0, :].bitcast(F32), op0=ALU.mult,
                                             op1=ALU.subtract).then_inc(s_yt, 1)
                splits(q + U_IN1 // 4, 12, U_OUT + 4)
                post(2 * l)
                norm_in(2 * l + 1, G_FFN)
                ffn_dve(dve, splits, evac, q + (U_IN1 + U_OUT) // 4, l, ti + T_IN1)
                splits(q + (U_IN1 + U_OUT + U_UP) // 4, 4, U_DOWN + 4)
                post(2 * l + 1)

            dve.wait_ge(s_x, 4 * LB + 2)
            dve.memset(wa_bd, 0.0).then_inc(s_bd, 1)
            dve.memset(wx_bd, 0.0).then_inc(s_bd, 1)
            dve.memset(epsc_q, 128 * EPS)
            dve.memset(onec, 1.0).then_inc(s_pad2, 1)
            dve.wait_ge(s_par2, 5)
            norm_in(2 * LB, G2_PRE)
            dve.wait_ge(s_wb, 1)
            dve.tensor_tensor(w_bal[:, :, :], w_ba, w_bah[:, :, :].bitcast(F32), ALU.subtract).then_inc(s_wbl, 1)
            for v in (qkv_pad[:, :, 0:3], sc_pad[:, :, 0:2], lru_pad[:, :, 0:3]):
                ins = dve.memset(v, 0.0)
            ins.then_inc(s_pad2, 1)
            q = DEPTH * (U_LAYER // 4)
            lists = {3: conv_ops(dve, qkvT, qkv_pad, 12, 4, GDN_CW, None, s_qc),
                     5: conv_ops(dve, lru_xc, lru_pad, 4, 4, L_CW, L_CB, s_lc)}
            pending = []
            for c in range(11):
                for i in range(8 * c + 4, 8 * c + 12):
                    split(q, i)
                    if c >= 3:
                        for _ in range(2):
                            if pending:
                                pending.pop(0)()
                if c < T_IN2:
                    dst = (qkv_pad[:, 0:4, 3:3 + S], qkv_pad[:, 4:8, 3:3 + S], qkv_pad[:, 8:12, 3:3 + S], lru_pad[:, :, 3:3 + S],
                           lru_gate, sc_b, sc_c, sc_pad[:, :, 2:2 + S])[c]
                    evac(TB + c, 4 * (c % 2), dst)
                if c == 2:
                    pending += lists[3]
                if c == 4:
                    pending += lists[5]
            for f in pending:
                f()
            mixers2_dve(dve, splits, q + U_IN2 // 4)
            q += U_IN2 // 4
            splits(q, 4, U_OUT + 4)
            post(2 * LB)
            norm_in(2 * LB + 1, G2_FFN)
            q += U_OUT // 4
            ffn2_dve(dve, splits, evac, q)
            q += U_UP // 4
            splits(q, 4, U_DOWN)
            post(2 * LB + 1)

        @block.gpsimd
        def _(pool):
            def add_residual(m):
                for t in range(NT):
                    for c in range(2):
                        pool.wait_ge(s_pn, 4 * m + 2 * t + c + 1)
                        ins = pool.tensor_tensor(x[:, t, c * 1024:(c + 1) * 1024], x[:, t, c * 1024:(c + 1) * 1024],
                                                 tmp[:, c, t, :], ALU.add)
                    ins.then_inc(s_x, 1)

            def rope_half(l, w, half, i):
                n = 3 * half + w
                pool.wait_ge(s_freeN, N_IN1 * l + n + 1)
                v = (q_nat, k_nat)[w][:, :, half * 512:(half + 1) * 512].rearrange("p t (h e) -> p t h e", e=64)
                t1, t2 = v[:, :, :, 0:8], v[:, :, :, 8:16]
                cos = C[:, C_ROPE:C_ROPE + 16].rearrange("p (t e) -> p t e", t=NT)[:, :, None, :].to_broadcast((P, NT, 8, 8))
                sin = C[:, C_ROPE + 16:C_ROPE + 32].rearrange("p (t e) -> p t e", t=NT)[:, :, None, :].to_broadcast((P, NT, 8, 8))
                r = [rope[:, k, :].rearrange("p (t h e) -> p t h e", t=NT, h=8) for k in range(4)]
                pool.wait_ge(s_roped, 8 * l + 2 * i)
                for k, (u, f) in enumerate(((t1, cos), (t2, sin), (t2, cos), (t1, sin))):
                    ins = pool.tensor_tensor(r[k], u, f, ALU.mult)
                ins.then_inc(s_rope, 1)
                pool.wait_ge(s_rope, 4 * l + i + 1)
                pool.tensor_tensor(t1, r[0], r[1], ALU.subtract).then_inc(s_roped, 1)
                pool.tensor_tensor(t2, r[2], r[3], ALU.add).then_inc(s_roped, 1)

            pool.wait_ge(s_const, 16)
            with pool.Fori(0, DEPTH) as l:
                pool.wait_ge(s_pad, l + 1)
                pool.wait_ge(s_kc, 32 * (l + 1))
                pool.wait_ge(s_freeT, l * T_LAYER + 3)
                inv = KC[:, K_INV:K_END].rearrange("p (n s) -> p n s", n=4)
                src, width, did = upad, UP, 0
                for k in range(4):
                    d, win = 1 << k, 2 << k
                    width -= d
                    dst = (win_a, win_b)[k % 2]
                    if did:
                        pool.wait_ge(s_pool, 12 * l + did)
                    pool.tensor_tensor(dst[:, k:4, 0:width], src[:, k:4, 0:width], src[:, k:4, d:d + width],
                                       ALU.add).then_inc(s_pool, 1)
                    pool.wait_ge(s_pool, 12 * l + did + 1)
                    at = 8 - win // 2
                    pool.tensor_tensor(pooled[:, k, :], dst[:, k, at:at + S], inv[:, k, :], ALU.mult).then_inc(s_pool, 1)
                    pool.wait_ge(s_pool, 12 * l + did + 2)
                    ins = pool.tensor_tensor(pooled[:, k, :], pooled[:, k, :], upad[:, k, 8:8 + S], ALU.subtract)
                    ins.then_inc(s_pool, 1)
                    did += 3
                    src = dst
                i = 0
                for half in range(2):
                    for w in range(2):
                        rope_half(l, w, half, i)
                        i += 1
                add_residual(2 * l)
                add_residual(2 * l + 1)
            for m in (2 * LB, 2 * LB + 1):
                add_residual(m)

        def attention_pe(pe, mm, l):
            for half in range(2):
                for w, src in enumerate((q_nat, k_nat)):
                    i = 2 * half + w
                    pe.wait_ge(s_roped, 8 * l + 2 * i + 2)
                    pe.wait_ge(s_freeN, N_IN1 * l + 6)
                    for j in range(4):
                        for t in range(NT):
                            last = pe.transpose(PS[:, 2 * i + j // 2, (j % 2) * S + t * P:(j % 2) * S + (t + 1) * P],
                                                src[:, t, (4 * half + j) * P:(4 * half + j + 1) * P], ident)
                    last.then_inc(s_qkt, 1)
            pe.wait_ge(s_qk, 4 * l + 4)
            for i in range(18):
                if i < 16:
                    h = i
                    if h >= 2:
                        pe.wait_ge(s_sb, 16 * l + h - 1)
                    p0 = 64 * (h % 2)
                    for t in range(NT):
                        last = mm(PS[:, h % 2, t * S:(t + 1) * S], qT[p0:p0 + 64, h // 2, t * P:(t + 1) * P],
                                  kT[p0:p0 + 64, h // 2, :], True, True)
                    last.then_inc(s_S, 1)
                if 1 <= i <= 16:
                    h = i - 1
                    pe.wait_ge(s_p, 16 * l + h + 1)
                    if h >= 2:
                        pe.wait_ge(s_pt, 16 * l + h - 1)
                    for t in range(NT):
                        for k in range(2):
                            last = pe.transpose(PS[:, 2 + h % 2, k * S + t * P:k * S + (t + 1) * P],
                                                prob[:, h % 2, t * S + k * P:t * S + (k + 1) * P], ident)
                    last.then_inc(s_ptr, 1)
                if i >= 2:
                    h = i - 2
                    pe.wait_ge(s_pt, 16 * l + h + 1)
                    if h % 4 == 0 and h >= 8:
                        pe.wait_ge(s_yb, 4 * l + h // 4 - 1)
                    for t in range(NT):
                        o = PS[:, 4 + (h // 4) % 2, (h % 4) * 128 + t * 64:(h % 4) * 128 + (t + 1) * 64]
                        for k in range(2):
                            last = mm(o, probT[:, h % 2, k * S + t * P:k * S + (t + 1) * P], v_nat[:, k, h * 64:(h + 1) * 64], k == 0, k == 1)
                    last.then_inc(s_o, 1)
            def column_sums(src, signal):
                for n in range(4):
                    last = mm(PS[:, 6, 0:S], ones, src[:, n, :], n == 0, n == 3)
                last.then_inc(signal, 1)

            pe.wait_ge(s_cv, 4 * TAPS * (l + 1))
            column_sums(acc, s_col)
            pe.wait_ge(s_sqr, 3 * l + 1)
            column_sums(sq, s_col)
            pe.wait_ge(s_pool, 12 * (l + 1))
            pe.wait_ge(s_yb, 4 * l + 4)
            pe.wait_ge(s_kc, 32 * (l + 1))
            for n in range(4):
                last = mm(PS[:, 4 + n // 2, (n % 2) * S:(n % 2 + 1) * S], pw[:, n, :], pooled[:, n, :], True, True)
            last.then_inc(s_mix, 1)
            pe.wait_ge(s_sqr, 3 * l + 2)
            pe.wait_ge(s_std, 3 * l + 1)
            column_sums(sq, s_col)
            pe.wait_ge(s_sqr, 3 * l + 3)
            pe.wait_ge(s_std, 3 * l + 2)
            column_sums(sq, s_col)

        def ffn_pe(pe, chunk_T, q, ti, xt):
            with pe.Fori(0, 11) as j:
                pe.wait_ge(s_xt, xt)
                pe.wait_ge(s_freeT, ti + 2 * j)
                chunk_T(q + 4 * j, 0, 0)
                chunk_T(q + 4 * j + 2, 0, 4)

        def down_pe(pe, wide_units, q, l):
            for c in range(2):
                wide_units(q, FKT * c, HT, list(range(FKT)), c, 0, FKT, lambda i, kt: None if c else pe.wait_ge(s_ht, 11 * l + i // 4 + 1))

        def mixers2_pe(pe, mm):
            def column_sums(src):
                for n in range(4):
                    last = mm(PS[:, 6, 0:S], ones, src[:, n, :], n == 0, n == 3)
                last.then_inc(s_csum, 1)

            def each(bank, lhs, rhs, signal):
                for m in range(8):
                    last = mm(pair(bank)[:, m, :], lhs(m), rhs(m), True, True)
                last.then_inc(signal, 1)

            head = lambda v, m: v[:, m % 4, (m // 4) * P:(m // 4 + 1) * P]
            pe.wait_ge(s_freeN, N_IN1 * LB + 3)
            pe.wait_ge(s_csq, 1)
            column_sums(f3(T1))
            pe.wait_ge(s_lc, 16)
            pe.wait_ge(s_w2, 160)
            for n in range(4):
                mm(quad(2)[:, n, :], wa_bd[:, n, :], lru_xc[:, n, :], True, True)
                last = mm(quad(4)[:, n, :], wx_bd[:, n, :], lru_xc[:, n, :], True, True)
            last.then_inc(s_lm, 1)
            pe.wait_ge(s_csq, 2)
            pe.wait_ge(s_crt, 1)
            column_sums(f3(T1))
            pe.wait_ge(s_wsm, 1)
            pe.wait_ge(s_lg, 2)
            for g in range(4):
                last = pe.transpose(PS[:, 2, g * P:(g + 1) * P], sgu_ws[:, g, :], ident)
            last.then_inc(s_wsm, 1)
            pe.wait_ge(s_gvn, 1)
            pe.wait_ge(s_wst, 1)
            for t in range(NT):
                for g in range(4):
                    last = mm(PS[:, 4 + t, g * P:(g + 1) * P], sgu_wsT[:, g, :], sgu_v[:, t, g * P:(g + 1) * P], True, True)
            last.then_inc(s_gm, 1)
            pe.wait_ge(s_crt, 2)
            for t in range(NT):
                pe.wait_ge(s_gyn, t + 1)
                for g in range(4):
                    last = pe.transpose(quad(6)[:, g, t * P:(t + 1) * P], sgu_v[:, t, g * P:(g + 1) * P], ident)
                last.then_inc(s_gyt, 1)
            for k, b in ((0, 2), (1, 4)):
                pe.wait_ge(s_l2s, k + 1)
                if k:
                    pe.wait_ge(s_gy, 1)
                for h in range(4):
                    last = mm(quad(b)[:, h, :], ones, f3(T1)[:, h, :], True, True)
                last.then_inc(s_l2m, 1)
            pe.wait_ge(s_l2n, 2)
            for k, (b, src) in enumerate(((2, kh), (4, vh))):
                for m in range(8):
                    last = pe.transpose(pair(b)[:, m, :], head(src, m), ident)
                last.then_inc(s_kv, 1)
            pe.wait_ge(s_g, 1)
            pe.wait_ge(s_y2t, 12)
            ct = C[:, C_CAUSAL_T:C_CAUSAL_T + P]
            mm(PS[:, 6, 0:8], ct, g_tok, True, True).then_inc(s_gcm, 1)
            pe.wait_ge(s_kvb, 2)
            each(2, lambda m: g_tok[:, m:m + 1].to_broadcast((P, P)), lambda m: ct, s_grow)
            pe.wait_ge(s_gcum, 1)
            each(6, lambda m: head(kh, m), lambda m: head(kh, m), s_kk)
            pe.wait_ge(s_dd, 2)
            pe.wait_ge(s_fac, 1)
            each(2, lambda m: head(kh, m), lambda m: head(qh, m), s_kk)
            pe.wait_ge(s_P, 1)
            for m in range(8):
                last = pe.transpose(pair(4)[:, m, :], Pm[:, m, :], ident)
            last.then_inc(s_Pt, 1)
            pe.wait_ge(s_att, 1)
            for r in range(5):
                pe.wait_ge(s_pte, r + 1)
                each(2, lambda m: PmT[:, m, :], lambda m: Pm[:, m, :], s_sq)
                if r < 4:
                    each(4, lambda m: Pm[:, m, :], lambda m: PmT[:, m, :], s_sq)
                pe.wait_ge(s_P, r + 2)
                pe.wait_ge(s_tt, r + 1)
                each(6, lambda m: Pm[:, m, :], lambda m: Tt[:, m, :], s_te)
            pe.wait_ge(s_tt, 6)
            pe.wait_ge(s_kbg, 3)
            each(2, lambda m: kbg[:, m, :], lambda m: Tt[:, m, :], s_wu)
            each(4, lambda m: Tt[:, m, :], lambda m: v_beta[:, m, :], s_wu)
            pe.wait_ge(s_wue, 1)
            pe.wait_ge(s_wue2, 1)
            pe.wait_ge(s_qg, 1)
            for n in range(4):
                t, r = n // 2, 64 * (n % 2)
                if n:
                    pe.wait_ge(s_st, n)
                    for h in range(4):
                        last = mm(PS[r:r + 64, 2, h * P:(h + 1) * P], wT[:, 4 * t + h, r:r + 64], state[:, h, :], True, True)
                    last.then_inc(s_vn, 1)
                    pe.wait_ge(s_vne, n)
                    pe.wait_ge(s_oe, n)
                if n < 3:
                    for h in range(4):
                        m = 4 * t + h
                        last = mm(PS[:, 6, h * P:(h + 1) * P], kg[r:r + 64, m, :], u_by[r:r + 64, m, :], True, True)
                    last.then_inc(s_ks, 1)
                for h in range(4):
                    m = 4 * t + h
                    o = PS[r:r + 64, 3, h * P:(h + 1) * P]
                    if n:
                        mm(o, head(qh, m)[:, r:r + 64], state[:, h, :], True, False)
                    last = mm(o, decT[r:r + 64, m, r:r + 64], u_by[r:r + 64, m, :], n == 0, True)
                last.then_inc(s_os, 1)
            pe.wait_ge(s_oz, 1)
            for m in range(8):
                last = pe.transpose(quad(6)[:, m % 4, (m // 4) * P:(m // 4 + 1) * P], o_by[:, m, :], ident)
            last.then_inc(s_ot, 1)

        @block.tensor
        def _(pe):
            def unit_ready(q, i):
                pe.wait_ge(s_lo, 4 * q + i + 5)

            def mm(o, w, r, start, stop):
                return pe.matmul(o, w, r, start=start, stop=stop, skip_group_check=True)

            def chunk_T(q, i0, base, xready=None):
                for i in range(8):
                    unit_ready(q, i0 + i)
                    slot = (i0 + i) % RING
                    for k in range(2):
                        kt = 2 * i + k
                        if xready:
                            xready(kt)
                        for n in range(4):
                            c = k * CHUNK + n * P
                            mm(PS[:, base + n, :], WH[:, slot, c:c + P], XT[:, kt, :, :].rearrange("p a b -> p (a b)"), kt == 0, False)
                            last = mm(PS[:, base + n, 0:S], WL[:, slot, c:c + P], XT[:, kt, 0, :], False, kt == KT - 1)
                    last.then_inc(s_pe, 1)

            def three(out_of, xt, tok, wh, wl, cols, first, final):
                hi, lo = xt[:, 0, tok], xt[:, 1, tok]
                for n in range(cols):
                    mm(out_of(n), hi, wh[:, n * CHUNK:(n + 1) * CHUNK], first, False)
                for n in range(cols):
                    mm(out_of(n), hi, wl[:, n * CHUNK:(n + 1) * CHUNK], False, False)
                for n in range(cols):
                    last = mm(out_of(n), lo, wh[:, n * CHUNK:(n + 1) * CHUNK], False, final)
                return last

            def chunk_N(q, i0, base):
                for i in range(8):
                    unit_ready(q, i0 + i)
                    slot = (i0 + i) % RING
                    for k in range(2):
                        kt = 2 * i + k
                        for t in range(NT):
                            last = three(lambda n: PS[:, base + t, :], XT[:, kt], slice(t * P, (t + 1) * P),
                                         WH[:, slot, k * CHUNK:(k + 1) * CHUNK], WL[:, slot, k * CHUNK:(k + 1) * CHUNK],
                                         1, kt == 0, kt == KT - 1)
                    last.then_inc(s_pe, 1)

            def wide_units(q, i0, src, order, c, lo_, hi_, ready):
                for i in range(lo_, hi_):
                    unit_ready(q, i0 + i)
                    ready(i, order[i])
                    slot = (i0 + i) % RING
                    for t in range(NT):
                        last = three(lambda n: PS[:, 4 * c + 2 * t + n, :], src[:, order[i]], slice(t * P, (t + 1) * P),
                                     WH[:, slot, :], WL[:, slot, :], 2, i == 0, i == len(order) - 1)
                    last.then_inc(s_pe, 1)
                return last

            def norm_in(n):
                for t in range(NT):
                    pe.wait_ge(s_xs, 2 * n + t + 1)
                    for j in range(8):
                        for k in range(2):
                            kt = 2 * j + k
                            last = pe.transpose(PS[:, j, k * S + t * P:k * S + (t + 1) * P], xs[:, t, kt * P:(kt + 1) * P], ident)
                        if t == 1:
                            last.then_inc(s_tr, 1)

            pe.sem_inc(s_pe, 4)
            pe.wait_ge(s_const, 16)
            with pe.Fori(0, DEPTH) as l:
                q = l * (U_LAYER // 4)
                pe.wait_ge(s_rows, 16 * 8 * (l + 1))
                pe.wait_ge(s_x, 4 * l + 2)
                for r in range(2):
                    pe.transpose(PS[:, 0, r * P:(r + 1) * P], ROWS[:, r, :], ident).then_inc(s_prt, 1)
                pe.wait_ge(s_par, 2 * l + 2)
                norm_in(2 * l)
                ti, ni = T_LAYER * l, N_IN1 * l
                for c in range(9):
                    base = 4 * (c % 2)
                    if c == 0:
                        pe.wait_ge(s_xt, 32 * l + 8)
                    elif c == 1:
                        pe.wait_ge(s_xt, 32 * l + 16)
                    elif c < 5:
                        pe.wait_ge(s_freeT, ti + c - 1)
                    else:
                        pe.wait_ge(s_freeN, ni + c - 4)
                    if c < 3:
                        chunk_T(q, 8 * c, base, (lambda kt: pe.wait_ge(s_xt, 32 * l + kt + 1)) if c == 0 else None)
                    else:
                        chunk_N(q, 8 * c, base)
                attention_pe(pe, mm, l)
                q1 = q + U_IN1 // 4
                wide_units(q1, 0, XT, OUT_ORDER, 0, 0, 8, lambda i, kt: pe.wait_ge(s_yt, 16 * l + i + 1))
                for t in range(NT):
                    pe.wait_ge(s_ybn, 2 * l + t + 1)
                    for j in range(4):
                        for k in range(2):
                            kt = 2 * j + k
                            last = pe.transpose(PS[:, 4 + j, k * S + t * P:k * S + (t + 1) * P], yb_n[:, t, kt * P:(kt + 1) * P], ident)
                        if t == 1:
                            last.then_inc(s_ybt, 1)
                wide_units(q1, 0, XT, OUT_ORDER, 0, 8, 16, lambda i, kt: pe.wait_ge(s_yt, 16 * l + i + 1))
                wide_units(q1, 16, XT, OUT_ORDER, 1, 0, 16, lambda i, kt: None)
                pe.wait_ge(s_x, 4 * l + 4)
                norm_in(2 * l + 1)
                ffn_pe(pe, chunk_T, q1 + U_OUT // 4, ti + T_IN1, 32 * l + 32)
                q3 = q1 + (U_OUT + U_UP) // 4
                down_pe(pe, wide_units, q3, l)
            pe.wait_ge(s_rows2, 16 * 16)
            pe.wait_ge(s_x, 4 * LB + 2)
            for r in range(5):
                pe.transpose(PS[:, r // 4, (r % 4) * P:(r % 4 + 1) * P], rows2[:, r, :], ident).then_inc(s_prt2, 1)
            pe.wait_ge(s_par2, 5)
            norm_in(2 * LB)
            q = DEPTH * (U_LAYER // 4)
            for c in range(11):
                base = 4 * (c % 2)
                if c < 2:
                    pe.wait_ge(s_xt, 32 * LB + 8 * c + 8)
                elif c < 9:
                    pe.wait_ge(s_freeT, TB + c - 1)
                elif c == 9:
                    pe.wait_ge(s_freeT, TB + 8)
                    pe.wait_ge(s_wbl, 1)
                    for t in range(NT):
                        for kt in range(KT):
                            hi, lo = XT[:, kt, 0, t * P:(t + 1) * P], XT[:, kt, 1, t * P:(t + 1) * P]
                            o = PS[:, 7, 8 * t:8 * t + 8]
                            mm(o, hi, w_bah[:, kt, :], kt == 0, False)
                            mm(o, hi, w_bal[:, kt, :], False, False)
                            last = mm(o, lo, w_bah[:, kt, :], False, kt == KT - 1)
                    last.then_inc(s_ba, 1)
                else:
                    pe.wait_ge(s_freeN, N_IN1 * LB + 1)
                if c < T_IN2:
                    chunk_T(q, 8 * c, base, (lambda kt: pe.wait_ge(s_xt, 32 * LB + kt + 1)) if c == 0 else None)
                else:
                    chunk_N(q, 8 * c, base)
            mixers2_pe(pe, mm)
            q += U_IN2 // 4
            for c in range(2):
                wide_units(q, 16 * c, XT, OUT_ORDER2, c, 0, KT, (lambda i, kt: None) if c else (lambda i, kt: pe.wait_ge(s_y2t, i + 1)))
            pe.wait_ge(s_x, 4 * LB + 4)
            norm_in(2 * LB + 1)
            q += U_OUT // 4
            with pe.Fori(0, 11) as j:
                pe.wait_ge(s_xt, 32 * LB + 32)
                pe.wait_ge(s_freeT, TB + T_IN2 + 2 * j)
                chunk_T(q + 4 * j, 0, 0)
                chunk_T(q + 4 * j + 2, 0, 4)
            q += U_UP // 4
            down_pe(pe, wide_units, q, LB)


INPUTS = """x w_in conv_w conv_b conv_ln_g conv_ln_b pool_w pool_scale g_mix w_out g_pre_mix g_post_mix g_pre_ffn
g_post_ffn w_gate w_up w_down pre_mix_norm_2 w_in_2 gdn_conv_w_2 gdn_a_log_2 gdn_dt_bias_2 gdn_norm_w_2 lru_conv_w_2
lru_conv_b_2 lru_wa_2 lru_ba_2 lru_wx_2 lru_bx_2 lru_lambda_2 sgu_ln_w_2 sgu_ln_b_2 sgu_ws_2 sgu_b_2 sconv_w_2
grp_norm_w_2 w_out_2 post_mix_norm_2 pre_ffn_norm_2 ffn_up_2 ffn_conv_w_2 ffn_conv_b_2 ffn_down_2
post_ffn_norm_2""".split()


def kernel(**inputs):
    import concourse.bacc as bacc
    from concourse.bass_utils import run_bass_kernel_spmd

    nc = bacc.Bacc("TRN2", target_bir_lowering=False, num_devices=1)
    constants, key_constants = shape_constants()
    arrays = {f"in_{n}_dram": np.ascontiguousarray(inputs[n]) for n in INPUTS}
    arrays["in_constants_dram"] = constants
    arrays["in_key_constants_dram"] = key_constants
    a = {n[3:-5]: nc.dram_tensor(n, v.shape, F32, kind="ExternalInput").ap() for n, v in arrays.items()}
    out = nc.dram_tensor("out_dram", (1, S, D), F32, kind="ExternalOutput").ap()
    build(nc, a, out)
    return run_bass_kernel_spmd(nc, [arrays], core_ids=[0]).results[0]["out_dram"]
```

```python
from contextlib import ExitStack

import numpy as np

import concourse.bass as bass
from concourse import mybir

F32 = mybir.dt.float32
F32R = mybir.dt.float32r
ALU = mybir.AluOpType
ACT = mybir.ActivationFunctionType
AX = mybir.AxisListType.X

P = 128
S = 256
NT = S // P
D = 2048
KT = D // P
FF = 5632
FKT = FF // P
DEPTH = 2
EPS = 1e-6
NEG = -1e30
RING = 4
CHUNK = 512
UNIT = 1024

C_ID, C_ONE, C_CAUSAL, C_STRICT, C_CAUSAL_T, C_TRIL = (P * i for i in range(6))
C_ROPE = 6 * P
C_END = C_ROPE + 2 * NT * 8
K_BIAS = 0
K_INV = 2 * S
K_END = K_INV + 4 * S


def shape_constants():
    c = np.zeros((P, C_END), np.float32)
    i = np.arange(P)
    same = (i[:, None] // 64) == (i[None, :] // 64)
    c[:, C_ID:C_ID + P] = np.eye(P)
    c[:, C_ONE:C_ONE + P] = 1.0
    c[:, C_CAUSAL:C_CAUSAL + P] = same & (i[:, None] >= i[None, :])
    c[:, C_STRICT:C_STRICT + P] = same & (i[:, None] > i[None, :])
    c[:, C_CAUSAL_T:C_CAUSAL_T + P] = same & (i[:, None] <= i[None, :])
    c[:, C_TRIL:C_TRIL + P] = i[:, None] >= i[None, :]
    pos = np.arange(S, dtype=np.float32)
    inv = np.float32(500000.0) ** (-np.arange(0, 16, 2, dtype=np.float32) / np.float32(16))
    ang = (pos[:, None] * inv[None, :]).astype(np.float32).reshape(NT, P, 8).transpose(1, 0, 2)
    c[:, C_ROPE:C_ROPE + 16] = np.cos(ang).reshape(P, 16)
    c[:, C_ROPE + 16:C_ROPE + 32] = np.sin(ang).reshape(P, 16)
    k = np.zeros((P, K_END), np.float32)
    q, key = np.arange(S)[:, None], np.arange(S)[None, :]
    count = (abs(q - key) <= 64).astype(int) + ((q - key) % 4 == 0) + ((q - key) % 16 == 0)
    bias = np.where(count > 0, np.log(np.maximum(count, 1)), NEG).astype(np.float32)
    k[:, 0:2 * S] = bias.reshape(NT, P, S).transpose(1, 0, 2).reshape(P, NT * S)
    t = np.arange(S)
    for n, win in enumerate((2, 4, 8, 16)):
        size = np.clip(t + win - win // 2, 0, S) - np.clip(t - win // 2, 0, S)
        k[:, K_INV + n * S:K_INV + (n + 1) * S] = (1.0 / size.astype(np.float32))[None, :]
    return c, k


U_IN1, U_OUT, U_UP, U_DOWN = 9 * 8, 2 * KT, 22 * 8, 2 * FKT
U_LAYER = U_IN1 + U_OUT + U_UP + U_DOWN
U_IN2 = 11 * 8
T_IN1, N_IN1, T_LAYER = 3, 6, 3 + 22
OUT_ORDER = [0, 1, 2, 3, 12, 13, 14, 15, 4, 5, 6, 7, 8, 9, 10, 11]
TAPS = 31
HEADS = 16
TURN_QK_BANK = [2, 6, 2, 4]
score_bank = lambda h: 2 if h < 8 else 4 + h % 2
SCORES_AT = [47 + 2 * h for h in range(8)] + [69 + h for h in range(8)]
TURN_AT = [s + 1 for s in SCORES_AT]
OUTPUT_AT = [s + 2 for s in SCORES_AT[:8]] + [72, 73, 73] + [74 + h for h in range(5)]
POOL_AT, POOL_RMS_AT = 40, 42
TURN_QK_AT = [44, 46, 64, 67]
CONV_FROM, MEAN_AT, VAR_AT, RMS_AT = 16, 58, 60, 62
SQUARES_AT = [65, 65, 75, 78]
heads_at = lambda table, u: [h for h in range(HEADS) if table[h] == u]
IN2 = dict(q=0, k=512, v=1024, lru_x=2056, lru_gate=2568, sc_b=4104, sc_c=4616, sc_h=5128, z=1536, sgu_u=3080, sgu_v=3592)
T_IN2 = 8
BA = 2048
OUT_ORDER2 = [12, 13, 14, 15, 4, 5, 6, 7, 8, 9, 10, 11, 0, 1, 2, 3]


def build(nc, a, out, stop=None):
    with ExitStack() as ctx:
        def sb(name, shape, dt=F32):
            return ctx.enter_context(nc.sbuf_tensor(name, shape, dt))

        def sem(name):
            return ctx.enter_context(nc.semaphore(name))

        x = sb("x", [P, NT, D])
        with nc.sbuf_tensor("XT", [P, KT, 2, S], F32R) as XT:
            pass
        XS = sb("XS", [P, KT * 2 * S])
        WS = sb("WS", [P, RING, UNIT])
        WH = sb("WH", [P, RING, UNIT], F32R)
        WL = sb("WL", [P, RING, UNIT], F32R)
        XL = sb("XL", [P, 4, S])
        T1 = sb("T1", [P, 1032])
        T2 = sb("T2", [P, 1024])
        T3 = sb("T3", [P, 1024])
        C = sb("C", [P, C_END])
        PR = sb("PR", [P, 512])
        ROWS = sb("ROWS", [P, 2, P])
        SM = sb("SM", [P, 164])
        w_bah = sb("w_bah", [P, KT, 8], F32R)
        w_bal = sb("w_bal", [P, KT, 8], F32R)
        with nc.sbuf_tensor("HT", [P, FKT, 2, S], F32R) as HT:
            pass
        SCR = sb("SCR", [P, FKT * 2 * S])
        PS = ctx.enter_context(nc.psum_tensor("PS", [P, 8, CHUNK], F32))

        def scr(at, *dims):
            n = int(np.prod(dims))
            v = SCR[:, at:at + n]
            if len(dims) == 2:
                v = v.rearrange("p (a b) -> p a b", a=dims[0])
            if len(dims) == 3:
                v = v.rearrange("p (a b c) -> p a b c", a=dims[0], b=dims[1])
            return v

        ident = C[:, C_ID:C_ID + P]
        ones = C[:, C_ONE:C_ONE + P]

        xs = scr(9528, NT, D)
        junk = scr(4216, NT, D)
        aT, gT = scr(0, 4, S), scr(1024, 4, S)
        HP = S + TAPS - 1
        hpad = scr(2048, 4, HP)
        acc = scr(3192, 4, S)
        UP = S + 16
        upad = scr(4216, 4, UP)
        win_a, win_b = scr(5304, 4, UP), scr(6392, 4, UP)
        pooled = scr(7480, 4, S)
        ycT = scr(8504, 4, S)
        q_nat, k_nat, v_nat = scr(9528, NT, 1024), scr(11576, NT, 1024), scr(13624, NT, 1024)
        qT, kT = scr(15672, 8, S), scr(17720, 8, S)
        KC = scr(19768, K_END)
        rope = scr(21304, 4, 128)
        pw = scr(21816, 4, P)
        neg_s = scr(0, 2, NT * S)
        prob = scr(1024, 2, NT * S)
        probT = scr(5304, 2, NT * S)
        y_b = q_nat
        yb_n = k_nat
        gbc = (T1, T2)
        post_tmp = lambda down: scr(0, 2, NT, 1024) if not down else (
            XS[:, 0:4096].rearrange("p (c t n) -> p c t n", c=2, t=NT))
        sq = T3[:, :].rearrange("p (a b) -> p a b", a=4)
        f3 = lambda t: t[:, 0:1024].rearrange("p (a b) -> p a b", a=4)
        flat = lambda v: v.rearrange("p a b -> p (a b)")

        LB = DEPTH
        TB = LB * T_LAYER
        qkv_pad = scr(0, 12, S + 3)
        k_by, v_by, kbg = (scr(1024 * i, 8, P) for i in range(3))
        qkvT = scr(3108, 12, S)
        qh, kh, vh = (qkvT[:, 4 * i:4 * i + 4, :] for i in range(3))
        sc_b, sc_c, sc_pad = scr(6180, 4, S), scr(7204, 4, S), scr(8228, 4, S + 2)
        lru_pad, lru_gate, lru_xc = scr(9260, 4, S + 3), scr(10296, 4, S), scr(11320, 4, S)
        lru_r, lru_i = scr(12344, 4, S), scr(13368, 4, S)
        z, sgu_u, sgu_v = (scr(14392 + 1024 * i, NT, 512) for i in range(3))
        dec, decT, Pm, PmT = (scr(17464 + 1024 * i, 8, P) for i in range(4))
        wa_bd, wx_bd = scr(17464, 4, P), scr(17976, 4, P)
        sgu_lnw, sgu_lnb = scr(18488, 512), scr(19000, 512)
        sgu_ws, sgu_wsT = scr(19512, 4, P), scr(20024, 4, P)
        w_ba = scr(20536, KT, 8)
        state = scr(21560, 4, P)
        wT, u_by, kg = Pm, PmT, dec
        o_by, k_sq = scr(0, 8, P), scr(1024, 8, P)
        egrow = T1[:, 0:1024].rearrange("p (a b) -> p a b", a=8)
        v_beta = T2[:, :].rearrange("p (a b) -> p a b", a=8)
        Tt = T3[:, :].rearrange("p (a b) -> p a b", a=8)
        rows2 = T3[:, 0:5 * P].rearrange("p (a b) -> p a b", a=5)
        ffn_pad = T1[:, :].rearrange("p (a b) -> p a b", a=4)
        conv_j = C[:, C_ROPE:C_ROPE + 32].rearrange("p (k g n) -> p k g n", k=4, g=2)
        mask = lambda at: C[:, at:at + P][:, None, :].to_broadcast((P, 8, P))
        eight = lambda v: v[:, :, None].to_broadcast((P, 8, P))
        pair = lambda b: PS[:, b:b + 2, :].rearrange("p a (m c) -> p (a m) c", c=P)
        quad = lambda b: PS[:, b:b + 2, :].rearrange("p a (m c) -> p (a m) c", c=S)

        ssp = SM[:, 160:164]
        ss, rms, rinv = SM[:, 0:2], SM[:, 2:4], SM[:, 4:6]
        ssf, ssf2, rmsf, rinvf = SM[:, 6:10], SM[:, 10:12], SM[:, 12:14], SM[:, 14:16]
        neg_max = SM[:, 16:20]
        den = SM[:, 20:52]
        rden = SM[:, 52:84]
        ssb, rmsb, rinvb = SM[:, 84:86], SM[:, 86:88], SM[:, 88:90]
        ssb4 = SM[:, 140:148].rearrange("p (t g) -> p t g", t=NT)
        epsc, epsc_q, onec = SM[:, 90:91], SM[:, 91:92], SM[:, 92:93]
        gate_in = SM[:, 96:108]
        gate_abs, gate_ln = SM[:, 108:120], SM[:, 120:132]
        a_log, dt_bias = SM[:, 132:136], SM[:, 136:140]
        g_tok, beta, nbeta = SM[:, 16:24], SM[:, 24:32], SM[:, 32:40]
        gcum, gbeta, gtail = SM[:, 40:48], SM[:, 48:56], SM[:, 56:64]
        o_ss, o_rms, o_rinv = SM[:, 64:72], SM[:, 72:80], SM[:, 80:88]
        vm, vv, vs, vr = (SM[:, 140 + 2 * i:142 + 2 * i] for i in range(4))
        cs, cr, ci = (SM[:, 148 + 2 * i:150 + 2 * i] for i in range(3))
        rate = SM[:, 154:158]
        (G2_PRE, G2_FFN, G2_GRP, G2_GDN, L_CB, L_LAM, L_BA, L_BX, L_CW, S_CW, SGU_B) = (
            0, 16, 32, 44, 45, 49, 53, 57, 61, 77, 89)
        GDN_CW, F_CW = 93, 141
        G_PRE, G_FFN, G_MIX, CONV_B, LN_G, LN_B, POOL_SC, CONV_W = 0, 16, 32, 48, 52, 56, 60, 64
        col = lambda i: PR[:, i:i + 1]

        s_stage = [sem(f"s_stage{i}") for i in range(RING)]
        s_hi, s_lo, s_pe = sem("s_hi"), sem("s_lo"), sem("s_pe")
        s_const, s_xload, s_eps = sem("s_const"), sem("s_xload"), sem("s_eps")
        s_rows, s_prt, s_par = sem("s_rows"), sem("s_prt"), sem("s_par")
        s_x = sem("s_x")
        s_ss, s_sst, s_rms, s_rinv, s_xs, s_xs2, s_tr, s_xh, s_xt = (
            sem("s_" + n) for n in "ss ss_total rms rinv xs xs2 tr xh xt".split())
        s_xl, s_freeT, s_freeN = (sem("s_" + n) for n in "xl freeT freeN".split())
        s_sg, s_pad, s_glu, s_cv = (sem("s_" + n) for n in "sg pad glu cv".split())
        s_act, s_h, s_hh, s_ht = (sem("s_" + n) for n in "act h hh ht".split())
        s_gb, s_sf, s_sfs, s_rf, s_rfi, s_pn = (sem("s_" + n) for n in "gb sf sfs rf rfi pn".split())
        s_pool, s_mix, s_yc = (sem("s_" + n) for n in "pool mix yc".split())
        s_rope, s_roped, s_qkt, s_qk = (sem("s_" + n) for n in "rope roped qkt qk".split())
        s_S, s_sb, s_nm, s_p, s_ptr, s_pt, s_o, s_rd, s_yb = (sem("s_" + n) for n in "S sb nm p ptr pt o rd yb".split())
        s_sqr, s_col, s_std, s_rstd, s_ya, s_ycn, s_lna = (sem("s_" + n) for n in "sqr col std rstd ya ycn lna".split())
        s_ssb, s_sbs, s_rb, s_rbi, s_ybn, s_ybt, s_yh, s_yt = (sem("s_" + n) for n in "ssb sbs rb rbi ybn ybt yh yt".split())
        s_out, s_kc = sem("s_out"), sem("s_kc")
        s_rows2, s_prt2, s_par2, s_w2, s_bd = (sem("s2_" + n) for n in "rows prt par small bd".split())
        s_wb, s_wbl, s_ba = (sem("s2_" + n) for n in "wb wbl ba".split())
        s_qc, s_qs, s_l2s, s_l2m, s_l2r, s_l2n = (sem("s2_" + n) for n in "qconv qsilu l2sq l2sum l2root l2n".split())
        s_kv, s_kvb = sem("s2_kvT"), sem("s2_kv_by")
        s_dc, s_ac = sem("s2_dve_chain"), sem("s2_act_chain")
        s_gin, s_gln, s_g, s_gcm, s_gcum, s_grow = (sem("s2_" + n) for n in "gin gln g gcm gcum grow".split())
        s_dd, s_de, s_dm, s_kk, s_P, s_Pt, s_att = (sem("s2_" + n) for n in "dd de dm kk P Pt att".split())
        s_sq, s_te, s_tt = (sem("s2_" + n) for n in "sq te tt".split())
        s_fac, s_kbg, s_wu, s_wue = (sem("s2_" + n) for n in "fac kbg wu wue".split())
        s_vn, s_vne, s_os, s_oe, s_st, s_qg = (sem("s2_" + n) for n in "vn vne os oe st qg".split())
        s_on, s_ot = sem("s2_on"), sem("s2_ot")
        s_lm, s_lg, s_la, s_lt, s_lr, s_lsq, s_ly = (sem("s2_" + n) for n in "lm lg la lt lrec lsqrt ly".split())
        s_sy, s_csq, s_csum, s_crt, s_cn = (sem("s2_" + n) for n in "sy csq csum croot cn".split())
        s_gelu, s_gn, s_wsm, s_gm, s_gy, s_gyn, s_gyt = (sem("s2_" + n) for n in "gelu gn wsm gm gy gyn gyt".split())
        s_groot, s_wst, s_eg, s_fac2, s_pte, s_on2, s_tap, s_fc = (sem("s2_" + n) for n in "groot wst eg fac2 pte on2 tap fc".split())
        s_lc, s_scv, s_gvn, s_wue2, s_ks, s_oz = (sem("s2_" + n) for n in "lc scv gvn wue2 ks oz".split())
        s_zs, s_y2h, s_y2t, s_cj = (sem("s2_" + n) for n in "zs y2h y2t cj".split())

        block = ctx.enter_context(nc.Block())

        @block.sync
        def _(sp):
            def load(q, i, src, width):
                sp.wait_ge(s_lo, 4 * q + i + 1)
                dst = WS[:, i % RING, :]
                if width:
                    dst = dst.rearrange("p (k n) -> p k n", n=width)
                sp.dma_start(dst, src).then_inc(s_stage[i % RING], 16)

            def chunk512(q, w, c):
                for i in range(8):
                    load(q, i, w[2 * i * P:(2 * i + 2) * P, c].rearrange("(k p) n -> p k n", p=P), CHUNK)

            def out_proj(q, w):
                for c in range(2):
                    for i, kt in enumerate(OUT_ORDER):
                        load(q, 16 * c + i, w[kt * P:(kt + 1) * P, c * 1024:(c + 1) * 1024], 0)

            def down_proj(q, w):
                for c in range(2):
                    with sp.Fori(0, FKT // 4) as r:
                        rows = w.rearrange("(r k p) n -> r k p n", k=4, p=P)
                        for i in range(4):
                            load(q + r + 11 * c, i, rows[r, i, :, c * 1024:(c + 1) * 1024], 0)

            sp.dma_start(C[:, :], a["constants"]).then_inc(s_const, 16)
            for t in range(NT):
                sp.dma_start(x[:, t, :], a["x"][0, t * P:(t + 1) * P, :]).then_inc(s_xload, 16)
            with sp.Fori(0, DEPTH) as l:
                q = l * (U_LAYER // 4)
                sp.wait_ge(s_eps, 1)
                sp.wait_ge(s_prt, 2 * l)
                small = [("g_pre_mix", 16), ("g_pre_ffn", 16), ("g_mix", 16), ("conv_b", 4), ("conv_ln_g", 4),
                         ("conv_ln_b", 4), ("pool_scale", 4)]
                at = 0
                for name, n in small:
                    sp.dma_start(ROWS[at:at + n, 0, :], a[name][l].rearrange("(n p) -> n p", p=P)).then_inc(s_rows, 16)
                    at += n
                sp.dma_start(ROWS[0:4 * TAPS, 1, :], a["conv_w"][l].rearrange("j (n p) -> (j n) p", p=P)).then_inc(s_rows, 16)
                w = a["w_in"][l]
                order = [0, 1, 8, 2, 4, 6, 3, 5, 7]
                for n, c in enumerate(order):
                    chunk512(q + 2 * n, w, slice(c * CHUNK, (c + 1) * CHUNK))
                q1 = q + U_IN1 // 4
                out_proj(q1, a["w_out"][l])
                q2 = q1 + U_OUT // 4
                with sp.Fori(0, 11) as j:
                    chunk512(q2 + 4 * j, a["w_gate"][l], bass.ds(j * CHUNK, CHUNK))
                    chunk512(q2 + 4 * j + 2, a["w_up"][l], bass.ds(j * CHUNK, CHUNK))
                q3 = q2 + U_UP // 4
                down_proj(q3, a["w_down"][l])
            q = DEPTH * (U_LAYER // 4)
            for n, c in enumerate(IN2.values()):
                chunk512(q + 2 * n, a["w_in_2"][0], slice(c, c + CHUNK))
            q += U_IN2 // 4
            for c in range(2):
                for i, kt in enumerate(OUT_ORDER2):
                    load(q, 16 * c + i, a["w_out_2"][0, kt * P:(kt + 1) * P, c * 1024:(c + 1) * 1024], 0)
            q += U_OUT // 4
            with sp.Fori(0, 11) as j:
                chunk512(q + 4 * j, a["ffn_up_2"][0], bass.ds(j * CHUNK, CHUNK))
                chunk512(q + 4 * j + 2, a["ffn_up_2"][0], bass.ds(j * CHUNK + FF, CHUNK))
            q += U_UP // 4
            down_proj(q, a["ffn_down_2"][0])
            sp.wait_ge(s_x, 4 + 8 * (DEPTH + 1))
            for t in range(NT):
                sp.dma_start(out[0, t * P:(t + 1) * P, :], x[:, t, :]).then_inc(s_out, 16)
            sp.wait_ge(s_out, 32)

        def mixers_act(act, l, u):
            def root_of_sums(k):
                act.wait_ge(s_col, 4 * l + k + 1)
                act.activation(XL[:, 0, :], PS[:, 3, 0:S], ACT.Sqrt, scale=1.0 / 512, bias=epsc).then_inc(s_std, 1)

            if u == POOL_AT:
                act.wait_ge(s_mix, l + 1)
                for n in range(4):
                    ins = act.activation(ycT[:, n, :], PS[:, 6 + n // 2, (n % 2) * S:(n % 2 + 1) * S], ACT.Copy,
                                         scale=col(POOL_SC + n))
                ins.then_inc(s_yc, 1)
                act.wait_ge(s_yc, l + 1)
                act.activation(sq, ycT, ACT.Square).then_inc(s_sqr, 1)
            if u == POOL_RMS_AT:
                root_of_sums(0)
            if u == MEAN_AT:
                act.wait_ge(s_lna, 3 * l + 1)
                act.activation(sq, acc, ACT.Square).then_inc(s_sqr, 1)
            if u == VAR_AT:
                act.wait_ge(s_rstd, 3 * l + 1)
                root_of_sums(2)
                act.wait_ge(s_lna, 3 * l + 2)
                for n in range(4):
                    ins = act.activation(acc[:, n, :], acc[:, n, :], ACT.Silu, scale=col(LN_G + n), bias=col(LN_B + n))
                ins.then_inc(s_lna, 1)
                act.wait_ge(s_lna, 3 * l + 3)
                act.activation(sq, acc, ACT.Square).then_inc(s_sqr, 1)
            if u == RMS_AT:
                act.wait_ge(s_rstd, 3 * l + 2)
                root_of_sums(3)
            if u in TURN_QK_AT:
                i = TURN_QK_AT.index(u)
                half, dst = i // 2, (qT, kT)[i % 2]
                act.wait_ge(s_qkt, 4 * l + i + 1)
                act.activation(flat(dst[:, 4 * half:4 * half + 4, :]), flat(PS[:, TURN_QK_BANK[i]:TURN_QK_BANK[i] + 2, :]),
                               ACT.Copy).then_inc(s_qk, 1)
            for h in heads_at(SCORES_AT, u):
                act.wait_ge(s_nm, 16 * l + h + 1)
                if h >= 2:
                    act.wait_ge(s_ptr, 16 * l + h - 1)
                for t in range(NT):
                    ins = act.activation(prob[:, h % 2, t * S:(t + 1) * S], neg_s[:, h % 2, t * S:(t + 1) * S], ACT.Exp,
                                         bias=neg_max[:, 2 * (h % 2) + t:2 * (h % 2) + t + 1], scale=-1.0,
                                         accum_out=den[:, 2 * h + t:2 * h + t + 1])
                ins.then_inc(s_p, 1)
            for h in heads_at(TURN_AT, u):
                act.wait_ge(s_ptr, 16 * l + h + 1)
                if h >= 2:
                    act.wait_ge(s_o, 16 * l + h - 1)
                act.activation(probT[:, h % 2, :], PS[:, 6, :], ACT.Copy).then_inc(s_pt, 1)
            for g in [g for g in range(4) if SQUARES_AT[g] == u]:
                act.wait_ge(s_yb, 4 * l + g + 1)
                if g >= 2:
                    act.wait_ge(s_ssb, 8 * l + 2 * g - 2)
                for t in range(NT):
                    at = (2 * (g % 2) + t) * 256
                    act.activation(T3[:, at:at + 256], y_b[:, t, 256 * g:256 * g + 256], ACT.Square,
                                   accum_out=ssb4[:, t, g:g + 1]).then_inc(s_ssb, 1)
                if g == 3:
                    act.wait_ge(s_sbs, l + 1)
                    act.activation(rmsb, ssb, ACT.Sqrt, scale=1.0 / 1024, bias=epsc).then_inc(s_rb, 1)

        def ffn_act(act, splits, evac_low, q, l, ti):
            with act.Fori(0, 11) as j:
                qj = q + 4 * j
                splits(qj, 4, 12)
                evac_low(qj, 7, ti + 2 * j, 0)
                act.wait_ge(s_freeT, ti + 2 * j + 1)
                act.activation(f3(T1), f3(T1), ACT.Silu).then_inc(s_act, 1)
                splits(qj, 12, 20)
                evac_low(qj, 15, ti + 2 * j + 1, 4)
                act.wait_ge(s_h, 11 * l + j + 1)
                act.activation(HT[:, bass.ds(4 * j, 4), 0, :], f3(T3), ACT.Copy).then_inc(s_hh, 1)

        def mixers2_act(act):
            chain = [0]

            def link(ins):
                chain[0] += 1
                ins.then_inc(s_ac, 1)
                act.wait_ge(s_ac, chain[0])

            def root_of_sums(k):
                act.wait_ge(s_csum, k)
                act.activation(XL[:, 0, :], PS[:, 6, 0:S], ACT.Sqrt, scale=1.0 / 512, bias=epsc).then_inc(s_crt, 1)

            def high(i0, src, g, signal, value):
                act.wait_ge(signal, value)
                for i in range(4):
                    act.activation(XT[:, OUT_ORDER2[i0 + i], 0, :], src(i), ACT.Copy, scale=col(g + i)).then_inc(s_y2h, 1)

            act.wait_ge(s_gin, 1)
            link(act.activation(gate_abs, gate_in, ACT.Abs))
            link(act.activation(gate_abs, gate_abs, ACT.Exp, scale=-1.0))
            act.activation(gate_ln, gate_abs, ACT.Ln, bias=onec).then_inc(s_gln, 1)
            act.activation(a_log, a_log, ACT.Exp).then_inc(s_gln, 1)
            ba = PS[:, 7, 0:16].rearrange("p (t n) -> p t n", t=NT)
            act.activation(beta.rearrange("p (t h) -> p t h", t=NT), ba[:, :, 0:4], ACT.Sigmoid).then_inc(s_gln, 1)
            act.wait_ge(s_sy, 1)
            act.activation(f3(T1), sc_b, ACT.Square).then_inc(s_csq, 1)
            root_of_sums(1)
            act.wait_ge(s_lm, 1)
            for k, (dst, b) in enumerate(((lru_r, L_BA), (lru_i, L_BX))):
                for n in range(4):
                    ins = act.activation(dst[:, n, :], quad(2 if k == 0 else 4)[:, n, :], ACT.Sigmoid, bias=col(b + n))
                ins.then_inc(s_lg, 1)
            act.wait_ge(s_la, 1)
            act.activation(f3(T1), lru_r, ACT.Tanh).then_inc(s_lt, 1)
            act.activation(f3(T2), lru_r, ACT.Exp).then_inc(s_lt, 1)
            act.wait_ge(s_lr, 1)
            act.activation(f3(T1), f3(T1), ACT.Sqrt).then_inc(s_lsq, 1)
            act.activation(lru_gate, lru_gate, ACT.Gelu_apprx_tanh).then_inc(s_lsq, 1)
            act.wait_ge(s_ly, 1)
            act.activation(f3(T1), lru_xc, ACT.Square).then_inc(s_csq, 1)
            high(0, lambda i: sc_b[:, i, :], G2_GRP + 8, s_cn, 1)
            root_of_sums(2)
            act.activation(sgu_v, sgu_v, ACT.Gelu_apprx_tanh).then_inc(s_gelu, 1)
            act.activation(sgu_u, sgu_u, ACT.Gelu_apprx_tanh).then_inc(s_gelu, 1)
            act.wait_ge(s_gn, 1)
            for t in range(NT):
                link(act.activation(T1[:, 512 * t:512 * t + 512], sgu_v[:, t, :], ACT.Square, accum_out=vv[:, t:t + 1]))
            act.activation(vs, vv, ACT.Sqrt, scale=1.0 / 512, bias=epsc).then_inc(s_groot, 1)
            act.wait_ge(s_wsm, 2)
            act.activation(sgu_wsT.rearrange("p a b -> p (a b)"), PS[:, 2, :], ACT.Copy).then_inc(s_wst, 1)
            high(4, lambda i: lru_xc[:, i, :], G2_GRP, s_cn, 2)
            act.wait_ge(s_gy, 1)
            for t in range(NT):
                link(act.activation(T1[:, 512 * t:512 * t + 512], sgu_v[:, t, :], ACT.Square, accum_out=cs[:, t:t + 1]))
            act.activation(cr, cs, ACT.Sqrt, scale=1.0 / 512, bias=epsc).then_inc(s_groot, 1)
            act.wait_ge(s_gyt, 2)
            high(8, lambda i: quad(6)[:, i, :], G2_GRP + 4, s_gyt, 2)
            act.wait_ge(s_qc, 48)
            act.activation(qkvT.rearrange("p a b -> p (a b)"), qkvT.rearrange("p a b -> p (a b)"), ACT.Silu).then_inc(s_qs, 1)
            act.wait_ge(s_qs, 1)
            for k, src in enumerate((qh, kh)):
                if k:
                    act.wait_ge(s_l2m, 1)
                act.activation(f3(T1), src, ACT.Square).then_inc(s_l2s, 1)
            for k in range(2):
                act.wait_ge(s_l2m, k + 1)
                act.activation(f3(T2) if k == 0 else f3(T3), quad(2 if k == 0 else 4), ACT.Sqrt, scale=128.0 if k == 0 else 1.0,
                               bias=epsc_q if k == 0 else epsc).then_inc(s_l2r, 1)
            act.wait_ge(s_kv, 2)
            act.activation(k_by, pair(2), ACT.Copy).then_inc(s_kvb, 1)
            act.activation(v_by, pair(4), ACT.Copy).then_inc(s_kvb, 1)
            act.wait_ge(s_gcm, 1)
            act.activation(gcum, PS[:, 6, 0:8], ACT.Copy).then_inc(s_gcum, 1)
            act.wait_ge(s_grow, 1)
            act.activation(egrow, pair(2), ACT.Exp).then_inc(s_eg, 1)
            for k, d in enumerate((dec, decT)):
                act.wait_ge(s_dd, k + 1)
                act.activation(d, d, ACT.Exp).then_inc(s_de, 1)
            link(act.activation(gbeta, gcum, ACT.Exp))
            act.wait_ge(s_fac, 1)
            act.activation(gtail, gtail, ACT.Exp).then_inc(s_fac2, 1)
            act.wait_ge(s_Pt, 1)
            act.activation(PmT, pair(4), ACT.Copy).then_inc(s_pte, 1)
            act.wait_ge(s_tt, 1)
            for r in range(4):
                act.wait_ge(s_sq, 2 * r + 2)
                act.activation(PmT, pair(4), ACT.Copy).then_inc(s_pte, 1)
            act.wait_ge(s_fac, 2)
            for m in range(8):
                ins = act.activation(kbg[:, m, :], k_by[:, m, :], ACT.Copy, scale=gbeta[:, m:m + 1])
            ins.then_inc(s_kbg, 1)
            for m in range(8):
                ins = act.activation(v_beta[:, m, :], v_by[:, m, :], ACT.Copy, scale=beta[:, m:m + 1])
            ins.then_inc(s_kbg, 1)
            for m in range(8):
                ins = act.activation(kg[:, m, :], k_by[:, m, :], ACT.Copy, scale=gtail[:, m:m + 1])
            ins.then_inc(s_kbg, 1)
            act.wait_ge(s_wu, 1)
            act.activation(wT, pair(2), ACT.Copy).then_inc(s_wue, 1)
            for n in range(4):
                t, r = n // 2, 64 * (n % 2)
                act.wait_ge(s_os, n + 1)
                act.activation(o_by[r:r + 64, 4 * t:4 * t + 4, :].rearrange("p a b -> p (a b)"), PS[r:r + 64, 3, :],
                               ACT.Copy).then_inc(s_oe, 1)
            act.activation(z, z, ACT.Silu).then_inc(s_zs, 1)
            act.wait_ge(s_on, 1)
            act.activation(o_rms, o_ss, ACT.Sqrt, scale=1.0 / P, bias=epsc).then_inc(s_on2, 1)
            act.wait_ge(s_ot, 1)
            for i in range(4):
                act.activation(XT[:, i, 0, :], quad(6)[:, i, :], ACT.Copy, scale=col(G2_GDN)).then_inc(s_y2h, 1)

        def ffn2_act(act, splits, evac_low, q):
            ti = TB + T_IN2
            splits(q, 4, 6)
            with act.Fori(0, 11) as j:
                qj = q + 4 * j
                for g, dst in ((0, T2), (1, T3)):
                    splits(qj, 6 + 8 * g, 12 + 8 * g)
                    evac_low(qj, 7 + 8 * g, ti + 2 * j + g, 4 * g)
                    act.wait_ge(s_freeT, ti + 2 * j + g + 1)
                    act.wait_ge(s_cj, j + 1)
                    for n in range(4):
                        ins = act.activation(f3(dst)[:, n, :], ffn_pad[:, n, 2:2 + S], ACT.Identity, scale=conv_j[:, 2, g, n:n + 1],
                                             bias=conv_j[:, 3, g, n:n + 1])
                    ins.then_inc(s_tap, 1)
                    splits(qj, 12 + 8 * g, 14 + 8 * g)
                    if g == 0:
                        act.wait_ge(s_fc, 2 * j + 1)
                        act.activation(f3(T2), f3(T2), ACT.Gelu_apprx_tanh).then_inc(s_act, 1)
                act.wait_ge(s_h, 11 * LB + j + 1)
                act.activation(HT[:, bass.ds(4 * j, 4), 0, :], f3(T3), ACT.Copy).then_inc(s_hh, 1)

        @block.scalar
        def _(act):
            def split(q, i):
                act.wait_ge(s_stage[i % RING], 16 * (q + i // RING + 1))
                act.wait_ge(s_pe, 4 * q + i + 1)
                act.activation(WH[:, i % RING, :], WS[:, i % RING, :], ACT.Copy).then_inc(s_hi, 1)

            def splits(q, i0, i1):
                for i in range(i0, i1):
                    split(q, i)

            def product_done(q, i):
                act.wait_ge(s_pe, 4 * q + i + 5)

            def evac_low(q, i, ti, base):
                product_done(q, i)
                act.wait_ge(s_freeT, ti)
                act.activation(XL[:, :, :], PS[:, base:base + 4, S:2 * S], ACT.Copy).then_inc(s_xl, 1)

            def norm_in(n, g):
                def root(t):
                    act.wait_ge(s_sst, 2 * n + t + 1)
                    act.activation(rms[:, t:t + 1], ss[:, t:t + 1], ACT.Sqrt, scale=1.0 / D, bias=epsc).then_inc(s_rms, 1)

                def scale_half(t):
                    act.wait_ge(s_rinv, 2 * n + t + 1)
                    act.activation(xs[:, t, 1024:2048], x[:, t, 1024:2048], ACT.Copy, scale=rinv[:, t:t + 1]).then_inc(s_xs2, 1)

                for t in range(NT):
                    for c in range(2):
                        if (t, c) == (1, 1):
                            root(0)
                        act.wait_ge(s_x, 4 * n + 2 * t + c + 1)
                        act.activation(junk[:, t, c * 1024:(c + 1) * 1024], x[:, t, c * 1024:(c + 1) * 1024], ACT.Square,
                                       accum_out=ssp[:, 2 * t + c:2 * t + c + 1]).then_inc(s_ss, 1)
                scale_half(0)
                root(1)
                scale_half(1)
                for kt in range(KT):
                    if kt % 2 == 0:
                        act.wait_ge(s_tr, 8 * n + kt // 2 + 1)
                    act.activation(XT[:, kt, 0, :], PS[:, kt // 2, (kt % 2) * S:(kt % 2 + 1) * S], ACT.Copy,
                                   scale=col(g + kt)).then_inc(s_xh, 1)

            def load_post_weight(gname_row):
                for h in range(2):
                    act.dma_start(gbc[h][:, 0:1024], gname_row[:, h * 1024:(h + 1) * 1024].to_broadcast((P, 1024))).then_inc(s_gb, 16)

            def post_squares(m, c):
                for t in range(NT):
                    if t + c:
                        act.wait_ge(s_sf, 4 * m + 2 * c + t)
                    act.activation(XL[:, :, :].rearrange("p a b -> p (a b)"),
                                   PS[:, 4 * c + 2 * t:4 * c + 2 * t + 2, :].rearrange("p a b -> p (a b)"), ACT.Square,
                                   accum_out=ssf[:, 2 * c + t:2 * c + t + 1]).then_inc(s_sf, 1)

            def post_root(m):
                act.wait_ge(s_sfs, m + 1)
                act.activation(rmsf, ssf2, ACT.Sqrt, scale=1.0 / D, bias=epsc).then_inc(s_rf, 1)

            def y_high(kt, src, g):
                act.activation(XT[:, kt, 0, :], src, ACT.Copy, scale=g).then_inc(s_yh, 1)

            def wide_phase(q, m, n_units, first=4, last=False):
                for c in range(2):
                    splits(q, n_units * c + (4 if c else first), n_units * (c + 1) + (0 if c and last else 4))
                    product_done(q, n_units * c + n_units - 1)
                    post_squares(m, c)
                post_root(m)

            act.wait_ge(s_eps, 2)
            act.wait_ge(s_const, 16)
            splits(0, 0, 4)
            with act.Fori(0, DEPTH) as l:
                q = l * (U_LAYER // 4)
                act.wait_ge(s_prt, 2 * l + 2)
                act.activation(PR[:, 0:64], PS[:, 0, 0:64], ACT.Copy).then_inc(s_par, 1)
                act.activation(PR[:, 64:64 + P], PS[:, 0, P:2 * P], ACT.Copy).then_inc(s_par, 1)
                act.wait_ge(s_par, 2 * l + 2)
                norm_in(2 * l, G_PRE)
                act.dma_start(KC, a["key_constants"]).then_inc(s_kc, 16)
                act.dma_start(pw, a["pool_w"][l].rearrange("g c d -> c g d")).then_inc(s_kc, 16)
                ti, ni = l * T_LAYER, l * N_IN1
                for c in range(9):
                    for i in range(8):
                        split(q, 8 * c + 4 + i)
                        if i < 7:
                            mixers_act(act, l, 8 * c + i)
                    if c < 3:
                        evac_low(q, 8 * c + 7, ti + c, 4 * (c % 2))
                        if c == 1:
                            act.wait_ge(s_freeT, ti + 2)
                            act.activation(f3(T1), gT, ACT.Sigmoid).then_inc(s_sg, 1)
                    else:
                        n = c - 3
                        base = 4 * (c % 2)
                        dst = (q_nat, k_nat, v_nat)[n % 3]
                        half = n // 3
                        product_done(q, 8 * c + 7)
                        for t in range(NT):
                            ins = act.activation(dst[:, t, half * 512:(half + 1) * 512], PS[:, base + t, :], ACT.Copy,
                                                 scale=0.125 if n % 3 == 0 else 1.0)
                        ins.then_inc(s_freeN, 1)
                    if c == 3:
                        act.wait_ge(s_glu, l + 1)
                        load_post_weight(a["g_post_mix"][bass.ds(l, 1)])
                    if c == 8:
                        for i in range(8):
                            kt = OUT_ORDER[i]
                            act.wait_ge(s_ya if i < 4 else s_ycn, l + 1)
                            y_high(kt, (acc if i < 4 else ycT)[:, i % 4, :], col(G_MIX + kt))
                    mixers_act(act, l, 8 * c + 7)
                for u in range(U_IN1, U_IN1 + 8):
                    split(q, u + RING)
                    mixers_act(act, l, u)
                for i in range(8):
                    if i % 2 == 0:
                        act.wait_ge(s_ybt, 4 * l + i // 2 + 1)
                    y_high(4 + i, PS[:, 4 + i // 2, (i % 2) * S:(i % 2 + 1) * S], col(G_MIX + 4 + i))
                wide_phase(q + U_IN1 // 4, 2 * l, KT, 12)
                norm_in(2 * l + 1, G_FFN)
                ffn_act(act, splits, evac_low, q + (U_IN1 + U_OUT) // 4, l, ti + T_IN1)
                act.wait_ge(s_h, 11 * l + 11)
                load_post_weight(a["g_post_ffn"][bass.ds(l, 1)])
                wide_phase(q + (U_IN1 + U_OUT + U_UP) // 4, 2 * l + 1, FKT)

            a2 = lambda n: a[n + "_2"][0]
            act.wait_ge(s_x, 8 * LB + 4)
            at = 0
            for name, n in (("pre_mix_norm", 16), ("pre_ffn_norm", 16), ("grp_norm_w", 12), ("gdn_norm_w", 1), ("lru_conv_b", 4),
                            ("lru_lambda", 4), ("lru_ba", 4), ("lru_bx", 4), ("lru_conv_w", 16), ("sconv_w", 12), ("sgu_b", 4)):
                v = a2(name)
                if name in ("lru_ba", "lru_bx"):
                    v = v.rearrange("(n h) p -> n (h p)", h=2)
                elif name == "gdn_norm_w":
                    v = v.rearrange("(n p) -> n p", p=P)
                elif len(v.shape) == 1:
                    v = v.rearrange("(n p) -> n p", p=P)
                elif name != "sgu_b":
                    v = v.rearrange("j (n p) -> (j n) p", p=P)
                act.dma_start(rows2[at:at + n, 0, :], v).then_inc(s_rows2, 16)
                at += n
            act.dma_start(rows2[0:48, 1, :], a2("gdn_conv_w").rearrange("j (n p) -> (j n) p", p=P)).then_inc(s_rows2, 16)
            taps = a2("ffn_conv_w").rearrange("j (n p) -> (j n) p", p=P)
            act.dma_start(rows2[:, 2, :], taps[0:128]).then_inc(s_rows2, 16)
            act.dma_start(rows2[:, 3, :], taps[128:256]).then_inc(s_rows2, 16)
            act.dma_start(rows2[0:8, 4, :], taps[256:264]).then_inc(s_rows2, 16)
            act.dma_start(rows2[8:96, 4, :], a2("ffn_conv_b").rearrange("(n p) -> n p", p=P)).then_inc(s_rows2, 16)
            act.dma_start(w_ba, a2("w_in")[:, BA:BA + 8].rearrange("(k p) n -> p k n", p=P)).then_inc(s_w2, 16)
            act.dma_start(a_log, a["gdn_a_log_2"].to_broadcast((P, 4))).then_inc(s_w2, 16)
            act.dma_start(dt_bias, a["gdn_dt_bias_2"].to_broadcast((P, 4))).then_inc(s_w2, 16)
            act.dma_start(sgu_lnw, a["sgu_ln_w_2"].to_broadcast((P, 512))).then_inc(s_w2, 16)
            act.dma_start(sgu_lnb, a["sgu_ln_b_2"].to_broadcast((P, 512))).then_inc(s_w2, 16)
            act.dma_start(sgu_ws, a2("sgu_ws").rearrange("g t s -> t g s")).then_inc(s_w2, 16)
            act.wait_ge(s_bd, 2)
            for w, bd in (("lru_wa", wa_bd), ("lru_wx", wx_bd)):
                m = a2(w).rearrange("(n b) i j -> b i n j", b=2)
                for b in range(2):
                    act.dma_start(bd[64 * b:64 * b + 64, :, 64 * b:64 * b + 64], m[b]).then_inc(s_w2, 16)
            act.wait_ge(s_prt2, 5)
            for r, (at, n) in enumerate(((0, 93), (GDN_CW, 48), (F_CW, 128), (F_CW + 128, 128), (F_CW + 256, 96))):
                act.activation(PR[:, at:at + n], PS[:, r // 4, (r % 4) * P:(r % 4) * P + n], ACT.Copy).then_inc(s_par2, 1)
            act.wait_ge(s_par2, 5)
            norm_in(2 * LB, G2_PRE)
            act.wait_ge(s_w2, 160)
            act.activation(w_bah[:, :, :], w_ba, ACT.Copy).then_inc(s_wb, 1)
            q = DEPTH * (U_LAYER // 4)
            for c in range(11):
                splits(q, 8 * c + 4, 8 * c + 12)
                if c < T_IN2:
                    evac_low(q, 8 * c + 7, TB + c, 4 * (c % 2))
                else:
                    product_done(q, 8 * c + 7)
                    dst = (z, sgu_u, sgu_v)[c - T_IN2]
                    for t in range(NT):
                        ins = act.activation(dst[:, t, :], PS[:, 4 * (c % 2) + t, :], ACT.Copy)
                    ins.then_inc(s_freeN, 1)
            mixers2_act(act)
            q += U_IN2 // 4
            load_post_weight(a["post_mix_norm_2"])
            wide_phase(q, 2 * LB, KT)
            norm_in(2 * LB + 1, G2_FFN)
            q += U_OUT // 4
            ffn2_act(act, splits, evac_low, q)
            act.wait_ge(s_h, 11 * LB + 11)
            load_post_weight(a["post_ffn_norm_2"])
            q += U_UP // 4
            wide_phase(q, 2 * LB + 1, FKT, 6, last=True)

        def mixers_dve(dve, l, u):
            def scale_by_root(k, y, signal):
                dve.wait_ge(s_std, 3 * l + k + 1)
                dve.reciprocal(XL[:, 1, :], XL[:, 0, :]).then_inc(s_rstd, 1)
                dve.wait_ge(s_rstd, 3 * l + k + 1)
                dve.tensor_tensor(y, y, XL[:, 1:2, :].to_broadcast((P, 4, S)), ALU.mult).then_inc(signal, 1)

            for h in heads_at(SCORES_AT, u):
                if h == 0:
                    dve.wait_ge(s_kc, 32 * (l + 1))
                dve.wait_ge(s_S, 16 * l + h + 1)
                if h >= 2:
                    dve.wait_ge(s_p, 16 * l + h - 1)
                dve.scalar_tensor_tensor(out=neg_s[:, h % 2, :], in0=PS[:, score_bank(h), :], scalar=-1.0,
                                         in1=KC[:, K_BIAS:K_BIAS + 2 * S], op0=ALU.mult, op1=ALU.subtract).then_inc(s_sb, 1)
                dve.wait_ge(s_sb, 16 * l + h + 1)
                dve.tensor_reduce(neg_max[:, 2 * (h % 2):2 * (h % 2) + 2],
                                  neg_s[:, h % 2, :].rearrange("p (t k) -> p t k", t=NT), AX, ALU.min).then_inc(s_nm, 1)
            for h in heads_at(OUTPUT_AT, u):
                if h % 4 == 3:
                    g = h // 4
                    dve.wait_ge(s_o, 16 * l + h + 1)
                    dve.reciprocal(rden[:, 8 * g:8 * g + 8], den[:, 8 * g:8 * g + 8]).then_inc(s_rd, 1)
                    dve.wait_ge(s_rd, 4 * l + g + 1)
                    o = PS[:, 7, :].rearrange("p (h t e) -> p h t e", h=4, t=NT)
                    r = rden[:, 8 * g:8 * g + 8].rearrange("p (h t) -> p h t", t=NT)
                    dst = y_b[:, :, 256 * g:256 * g + 256].rearrange("p t (h e) -> p h t e", e=64)
                    dve.tensor_tensor(dst, o, r[:, :, :, None].to_broadcast((P, 4, NT, 64)), ALU.mult).then_inc(s_yb, 1)
            if u == POOL_RMS_AT:
                scale_by_root(0, ycT, s_ycn)
            if u == MEAN_AT:
                dve.wait_ge(s_cv, 4 * TAPS * (l + 1))
                dve.wait_ge(s_col, 4 * l + 2)
                for n in range(4):
                    ins = dve.scalar_tensor_tensor(out=acc[:, n, :], in0=PS[:, 3, 0:S], scalar=-1.0 / 512, in1=acc[:, n, :],
                                                   op0=ALU.mult, op1=ALU.add)
                ins.then_inc(s_lna, 1)
            if u == VAR_AT:
                dve.wait_ge(s_lna, 3 * l + 1)
                scale_by_root(1, acc, s_lna)
            if u == RMS_AT:
                scale_by_root(2, acc, s_ya)
            if u == SQUARES_AT[3]:
                dve.wait_ge(s_ssb, 8 * l + 8)
                dve.tensor_reduce(ssb, ssb4, AX, ALU.add).then_inc(s_sbs, 1)
                dve.wait_ge(s_rb, l + 1)
                dve.reciprocal(rinvb, rmsb).then_inc(s_rbi, 1)
                dve.wait_ge(s_rbi, l + 1)
                for t in range(NT):
                    dve.tensor_scalar(yb_n[:, t, :], y_b[:, t, :], rinvb[:, t:t + 1], None, ALU.mult).then_inc(s_ybn, 1)

        def ffn_dve(dve, splits, evac, q, l, ti):
            with dve.Fori(0, 11) as j:
                qj = q + 4 * j
                splits(qj, 4, 12)
                evac(ti + 2 * j, 0, f3(T1))
                splits(qj, 12, 20)
                evac(ti + 2 * j + 1, 4, f3(T2))
                dve.wait_ge(s_act, 11 * l + j + 1)
                dve.wait_ge(s_freeT, ti + 2 * j + 2)
                dve.tensor_tensor(f3(T3), f3(T1), f3(T2), ALU.mult).then_inc(s_h, 1)
                dve.wait_ge(s_hh, 11 * l + j + 1)
                dve.tensor_tensor(HT[:, bass.ds(4 * j, 4), 1, :], f3(T3), HT[:, bass.ds(4 * j, 4), 0, :].bitcast(F32),
                                  ALU.subtract).then_inc(s_ht, 1)

        def conv_ops(dve, dst, pad, tiles, taps, w0, b0, signal):
            ops = []
            count = [0]

            def op(tile, j, before):
                def run():
                    w = col(w0 + tiles * j + tile)
                    if j == 0:
                        if b0 is None:
                            ins = dve.tensor_scalar(dst[:, tile, :], pad[:, tile, 0:S], w, None, ALU.mult)
                        else:
                            ins = dve.tensor_scalar(dst[:, tile, :], pad[:, tile, 0:S], w, col(b0 + tile), ALU.mult, ALU.add)
                    else:
                        dve.wait_ge(signal, before)
                        ins = dve.scalar_tensor_tensor(out=dst[:, tile, :], in0=pad[:, tile, j:j + S], scalar=w,
                                                       in1=dst[:, tile, :], op0=ALU.mult, op1=ALU.add)
                    ins.then_inc(signal, 1)
                return run

            n = 0
            for g in range(tiles // 4):
                for j in range(taps):
                    for k in range(4):
                        ops.append(op(4 * g + k, j, n - 3))
                        n += 1
            return ops

        def mixers2_dve(dve, splits, q_out):
            chain = [0]

            def link(ins):
                chain[0] += 1
                ins.then_inc(s_dc, 1)
                dve.wait_ge(s_dc, chain[0])

            def over_root(k, y, signal, value):
                dve.wait_ge(s_crt, k)
                link(dve.reciprocal(XL[:, 1, :], XL[:, 0, :]))
                dve.tensor_tensor(y, y, XL[:, 1:2, :].to_broadcast((P, 4, S)), ALU.mult).then_inc(signal, 1)

            def low(i0, src, g):
                for i in range(4):
                    kt = OUT_ORDER2[i0 + i]
                    dve.wait_ge(s_y2h, i0 + i + 1 if i0 < 8 else i0 + 4)
                    dve.scalar_tensor_tensor(out=XT[:, kt, 1, :], in0=src(i), scalar=col(g + i) if i0 < 12 else col(g),
                                             in1=XT[:, kt, 0, :].bitcast(F32), op0=ALU.mult, op1=ALU.subtract).then_inc(s_y2t, 1)

            dve.wait_ge(s_ba, 1)
            ba = PS[:, 7, 0:16].rearrange("p (t n) -> p t n", t=NT)
            link(dve.tensor_tensor(gate_in[:, 0:8].rearrange("p (t h) -> p t h", t=NT), ba[:, :, 4:8],
                                   dt_bias[:, None, :].to_broadcast((P, NT, 4)), ALU.add))
            dve.tensor_scalar(gate_in[:, 8:12], PR[:, L_LAM:L_LAM + 4], -1.0, None, ALU.mult).then_inc(s_gin, 1)
            dve.wait_ge(s_freeT, TB + 8)
            link(dve.tensor_tensor(sc_pad[:, :, 2:2 + S], sc_pad[:, :, 2:2 + S], sc_c, ALU.mult))
            for f in conv_ops(dve, sc_c, sc_pad, 4, 3, S_CW, None, s_scv):
                f()
            dve.wait_ge(s_scv, 12)
            dve.tensor_tensor(sc_b, sc_b, sc_c, ALU.mult).then_inc(s_sy, 1)
            dve.wait_ge(s_gin, 1)
            dve.wait_ge(s_gln, 3)
            link(dve.tensor_scalar(gate_in, gate_in, 0.0, None, ALU.max))
            link(dve.tensor_tensor(gate_in, gate_in, gate_ln, ALU.add))
            link(dve.tensor_scalar(rate, gate_in[:, 8:12], -8.0, None, ALU.mult))
            dve.scalar_tensor_tensor(out=g_tok.rearrange("p (t h) -> p t h", t=NT),
                                     in0=gate_in[:, 0:8].rearrange("p (t h) -> p t h", t=NT), scalar=-1.0,
                                     in1=a_log[:, None, :].to_broadcast((P, NT, 4)), op0=ALU.mult, op1=ALU.mult).then_inc(s_g, 1)
            dve.tensor_scalar(nbeta, beta, -1.0, None, ALU.mult).then_inc(s_g, 1)
            over_root(1, sc_b, s_cn, 1)
            dve.wait_ge(s_lg, 2)
            for n in range(4):
                ins = dve.tensor_scalar(lru_r[:, n, :], lru_r[:, n, :], rate[:, n:n + 1], None, ALU.mult)
            ins.then_inc(s_la, 1)
            link(dve.tensor_tensor(lru_i, lru_i, lru_xc, ALU.mult))
            dve.wait_ge(s_lt, 2)
            link(dve.tensor_scalar(lru_r, f3(T1), -1.0, 1.0, ALU.mult, ALU.add))
            link(dve.reciprocal(lru_r, lru_r))
            dve.scalar_tensor_tensor(out=f3(T1), in0=f3(T1), scalar=-2.0, in1=lru_r, op0=ALU.mult, op1=ALU.mult).then_inc(s_lr, 1)
            dve.wait_ge(s_lsq, 1)
            link(dve.tensor_tensor(lru_i, lru_i, f3(T1), ALU.mult))
            for n in range(4):
                ins = dve.tensor_tensor_scan(lru_xc[:, n, :], f3(T2)[:, n, :], lru_i[:, n, :], 0.0, ALU.mult, ALU.add)
            link(ins)
            dve.wait_ge(s_lsq, 2)
            dve.tensor_tensor(lru_xc, lru_xc, lru_gate, ALU.mult).then_inc(s_ly, 1)
            low(0, lambda i: sc_b[:, i, :], G2_GRP + 8)
            over_root(2, lru_xc, s_cn, 2)
            dve.wait_ge(s_gelu, 1)
            link(dve.tensor_reduce(vm, sgu_v, AX, ALU.add))
            link(dve.tensor_scalar(vm, vm, -1.0 / 512, None, ALU.mult))
            for t in range(NT):
                ins = dve.tensor_scalar(sgu_v[:, t, :], sgu_v[:, t, :], vm[:, t:t + 1], None, ALU.add)
            ins.then_inc(s_gn, 1)
            link(dve.tensor_tensor(sgu_ws, sgu_ws, C[:, C_TRIL:C_TRIL + P][:, None, :].to_broadcast((P, 4, P)), ALU.mult))
            dve.sem_inc(s_wsm, 1)
            dve.wait_ge(s_groot, 1)
            link(dve.reciprocal(vr, vs))
            for t in range(NT):
                ins = dve.scalar_tensor_tensor(out=sgu_v[:, t, :], in0=sgu_v[:, t, :], scalar=vr[:, t:t + 1], in1=sgu_lnw,
                                               op0=ALU.mult, op1=ALU.mult)
            link(ins)
            dve.tensor_tensor(sgu_v, sgu_v, sgu_lnb[:, None, :].to_broadcast((P, NT, 512)), ALU.add).then_inc(s_gvn, 1)
            low(4, lambda i: lru_xc[:, i, :], G2_GRP)
            dve.wait_ge(s_gm, 1)
            dve.wait_ge(s_gelu, 2)
            for t in range(NT):
                for g in range(4):
                    ins = dve.scalar_tensor_tensor(out=sgu_v[:, t, g * P:(g + 1) * P], in0=PS[:, 4 + t, g * P:(g + 1) * P],
                                                   scalar=col(SGU_B + g), in1=sgu_u[:, t, g * P:(g + 1) * P],
                                                   op0=ALU.add, op1=ALU.mult)
            ins.then_inc(s_gy, 1)
            dve.wait_ge(s_groot, 2)
            link(dve.reciprocal(ci, cr))
            for t in range(NT):
                dve.tensor_scalar(sgu_v[:, t, :], sgu_v[:, t, :], ci[:, t:t + 1], None, ALU.mult).then_inc(s_gyn, 1)
            low(8, lambda i: quad(6)[:, i, :], G2_GRP + 4)
            for k, (y, r) in enumerate(((qh, T2), (kh, T3))):
                dve.wait_ge(s_l2r, k + 1)
                link(dve.reciprocal(f3(r), f3(r)))
                dve.tensor_tensor(y, y, f3(r), ALU.mult).then_inc(s_l2n, 1)
            dve.wait_ge(s_gcum, 1)
            dve.wait_ge(s_eg, 1)
            for k, (d, at) in enumerate(((dec, C_STRICT), (decT, C_CAUSAL_T))):
                for m in range(8):
                    if k == 0:
                        ins = dve.tensor_scalar(d[:, m, :], pair(2)[:, m, :], -1.0, gcum[:, m:m + 1], ALU.mult, ALU.add)
                    else:
                        ins = dve.tensor_scalar(d[:, m, :], pair(2)[:, m, :], gcum[:, m:m + 1], None, ALU.subtract)
                link(ins)
                dve.tensor_tensor(d, d, mask(at), ALU.mult).then_inc(s_dd, 1)
            for r in (0, 64):
                ins = dve.tensor_tensor(gtail[r:r + 64, :], pair(2)[r:r + 64, :, r + 63], gcum[r:r + 64, :], ALU.subtract)
            ins.then_inc(s_fac, 1)
            for k, (d, at) in enumerate(((dec, C_STRICT), (decT, C_CAUSAL_T))):
                dve.wait_ge(s_de, k + 1)
                dve.tensor_tensor(d, d, mask(at), ALU.mult).then_inc(s_dm, 1)
            dve.wait_ge(s_fac2, 1)
            dve.tensor_tensor(gbeta, gbeta, beta, ALU.mult).then_inc(s_fac, 1)
            dve.wait_ge(s_dm, 1)
            dve.wait_ge(s_kk, 1)
            for m in range(8):
                ins = dve.scalar_tensor_tensor(out=Pm[:, m, :], in0=pair(6)[:, m, :], scalar=nbeta[:, m:m + 1], in1=dec[:, m, :],
                                               op0=ALU.mult, op1=ALU.mult)
            ins.then_inc(s_P, 1)
            dve.wait_ge(s_kk, 2)
            dve.wait_ge(s_dm, 2)
            dve.tensor_tensor(decT, pair(2), decT, ALU.mult).then_inc(s_att, 1)
            dve.wait_ge(s_pte, 1)
            dve.tensor_tensor(Tt, PmT, mask(C_ID), ALU.add).then_inc(s_tt, 1)
            for r in range(5):
                dve.wait_ge(s_sq, min(2 * r + 2, 9))
                dve.tensor_copy(Pm, pair(2)).then_inc(s_P, 1)
                dve.wait_ge(s_te, r + 1)
                dve.tensor_tensor(Tt, Tt, pair(6), ALU.add).then_inc(s_tt, 1)
            dve.wait_ge(s_wu, 2)
            dve.tensor_copy(u_by, pair(4)).then_inc(s_wue2, 1)
            dve.tensor_tensor(qh.rearrange("p h (t c) -> p t h c", t=NT), qh.rearrange("p h (t c) -> p t h c", t=NT),
                              egrow.rearrange("p (t h) c -> p t h c", t=NT), ALU.mult).then_inc(s_qg, 1)
            for n in range(4):
                t, r = n // 2, 64 * (n % 2)
                u = u_by[r:r + 64, 4 * t:4 * t + 4, :].rearrange("p a b -> p (a b)")
                if n:
                    dve.wait_ge(s_vn, n)
                    dve.tensor_tensor(u, u, PS[r:r + 64, 2, :], ALU.subtract).then_inc(s_vne, 1)
                if n < 3:
                    dve.wait_ge(s_ks, n + 1)
                    if n:
                        dve.wait_ge(s_os, n + 1)
                        dve.wait_ge(s_st, n)
                    for h in range(4):
                        if n == 0:
                            ins = dve.tensor_copy(state[:, h, :], PS[:, 6, h * P:(h + 1) * P])
                        else:
                            m = 4 * t + h
                            ins = dve.scalar_tensor_tensor(out=state[:, h, :], in0=state[:, h, :],
                                                           scalar=egrow[:, m, r + 63:r + 64], in1=PS[:, 6, h * P:(h + 1) * P],
                                                           op0=ALU.mult, op1=ALU.add)
                    ins.then_inc(s_st, 1)
            dve.wait_ge(s_oe, 4)
            link(dve.tensor_tensor(k_sq, o_by, o_by, ALU.mult))
            dve.tensor_reduce(o_ss, k_sq, AX, ALU.add).then_inc(s_on, 1)
            dve.wait_ge(s_on2, 1)
            link(dve.reciprocal(o_rinv, o_rms))
            link(dve.tensor_tensor(o_by, o_by, eight(o_rinv), ALU.mult))
            dve.wait_ge(s_zs, 1)
            zz = z.rearrange("p t (h c) -> p (t h) c", c=P)
            dve.tensor_tensor(o_by, o_by, zz, ALU.mult).then_inc(s_oz, 1)
            low(12, lambda i: quad(6)[:, i, :], G2_GDN)

        def ffn2_dve(dve, splits, evac, q):
            ti = TB + T_IN2
            dve.memset(ffn_pad[:, :, 0:2], 0.0)
            splits(q, 4, 6)
            with dve.Fori(0, 11) as j:
                qj = q + 4 * j
                for k in range(4):
                    for g in range(2):
                        ins = dve.tensor_copy(conv_j[:, k, g, :], PR[:, bass.ds(4 * j + (F_CW + 88 * k + 44 * g), 4)])
                ins.then_inc(s_cj, 1)
                for g, dst in ((0, T2), (1, T3)):
                    splits(qj, 6 + 8 * g, 12 + 8 * g)
                    evac(ti + 2 * j + g, 4 * g, ffn_pad[:, :, 2:2 + S])
                    dve.wait_ge(s_tap, 2 * j + g + 1)
                    for k in range(2):
                        if k:
                            dve.wait_ge(s_scv, 12 + 2 * j + g + 1)
                        for n in range(4):
                            ins = dve.scalar_tensor_tensor(out=f3(dst)[:, n, :], in0=ffn_pad[:, n, k:k + S],
                                                           scalar=conv_j[:, k, g, n:n + 1], in1=f3(dst)[:, n, :],
                                                           op0=ALU.mult, op1=ALU.add)
                        ins.then_inc(s_fc if k else s_scv, 1)
                        splits(qj, 12 + 8 * g + k, 13 + 8 * g + k)
                dve.wait_ge(s_act, 11 * LB + j + 1)
                dve.wait_ge(s_fc, 2 * j + 2)
                dve.tensor_tensor(f3(T3), f3(T3), f3(T2), ALU.mult).then_inc(s_h, 1)
                dve.wait_ge(s_hh, 11 * LB + j + 1)
                dve.tensor_tensor(HT[:, bass.ds(4 * j, 4), 1, :], f3(T3), HT[:, bass.ds(4 * j, 4), 0, :].bitcast(F32),
                                  ALU.subtract).then_inc(s_ht, 1)

        @block.vector
        def _(dve):
            def split(q, i):
                dve.wait_ge(s_hi, 4 * q + i + 1)
                dve.tensor_tensor(WL[:, i % RING, :], WS[:, i % RING, :], WH[:, i % RING, :].bitcast(F32),
                                  ALU.subtract).then_inc(s_lo, 1)

            def splits(q, i0, i1):
                for i in range(i0, i1):
                    split(q, i)

            def evac(ti, base, dst):
                dve.wait_ge(s_xl, ti + 1)
                dve.tensor_tensor(dst, PS[:, base:base + 4, 0:S], XL[:, :, :], ALU.add).then_inc(s_freeT, 1)

            def norm_in(n, g):
                for t in range(NT):
                    dve.wait_ge(s_ss, 4 * n + 2 * t + 2)
                    dve.tensor_tensor(ss[:, t:t + 1], ssp[:, 2 * t:2 * t + 1], ssp[:, 2 * t + 1:2 * t + 2], ALU.add).then_inc(s_sst, 1)
                    dve.wait_ge(s_rms, 2 * n + t + 1)
                    dve.reciprocal(rinv[:, t:t + 1], rms[:, t:t + 1]).then_inc(s_rinv, 1)
                    dve.wait_ge(s_rinv, 2 * n + t + 1)
                    dve.tensor_scalar(xs[:, t, 0:1024], x[:, t, 0:1024], rinv[:, t:t + 1], None, ALU.mult).then_inc(s_xs, 1)
                for kt in range(KT):
                    dve.wait_ge(s_xh, 16 * n + 2 * (kt // 2) + 2)
                    dve.scalar_tensor_tensor(out=XT[:, kt, 1, :], in0=PS[:, kt // 2, (kt % 2) * S:(kt % 2 + 1) * S],
                                             scalar=col(g + kt), in1=XT[:, kt, 0, :].bitcast(F32), op0=ALU.mult,
                                             op1=ALU.subtract).then_inc(s_xt, 1)

            def post_weighted(down, m, c):
                tmp = post_tmp(down)
                dve.wait_ge(s_gb, 32 * (m + 1))
                for t in range(NT):
                    dve.wait_ge(s_sf, 4 * m + 2 * c + t + 1)
                    dve.tensor_tensor(tmp[:, c, t, :], flat(PS[:, 4 * c + 2 * t:4 * c + 2 * t + 2, :]), gbc[c][:, 0:1024],
                                      ALU.mult).then_inc(s_pn, 1)

            def post(down, m):
                tmp = post_tmp(down)
                dve.wait_ge(s_sf, 4 * m + 4)
                dve.tensor_tensor(ssf2, ssf[:, 0:2], ssf[:, 2:4], ALU.add).then_inc(s_sfs, 1)
                post_weighted(down, m, 1)
                dve.wait_ge(s_rf, m + 1)
                dve.reciprocal(rinvf, rmsf).then_inc(s_rfi, 1)
                dve.wait_ge(s_rfi, m + 1)
                dve.wait_ge(s_pn, 4 * m + 4)
                for t in range(NT):
                    for c in range(2):
                        v = x[:, t, c * 1024:(c + 1) * 1024]
                        dve.scalar_tensor_tensor(out=v, in0=tmp[:, c, t, :], scalar=rinvf[:, t:t + 1], in1=v,
                                                 op0=ALU.mult, op1=ALU.add).then_inc(s_x, 1)

            def conv(l, i0, i1):
                for i in range(i0, i1):
                    j, n = divmod(i, 4)
                    if i == 0:
                        dve.wait_ge(s_glu, l + 1)
                    if j:
                        dve.wait_ge(s_cv, 4 * TAPS * l + i - 3)
                    w = col(CONV_W + 4 * j + n)
                    if j == 0:
                        dve.tensor_scalar(acc[:, n, :], hpad[:, n, 0:S], w, col(CONV_B + n), ALU.mult, ALU.add).then_inc(s_cv, 1)
                    else:
                        dve.scalar_tensor_tensor(out=acc[:, n, :], in0=hpad[:, n, j:j + S], scalar=w, in1=acc[:, n, :],
                                                 op0=ALU.mult, op1=ALU.add).then_inc(s_cv, 1)

            dve.memset(ROWS[:, :, :], 0.0).then_inc(s_eps, 1)
            dve.memset(epsc, EPS).then_inc(s_eps, 1)
            dve.sem_inc(s_lo, 4)
            dve.wait_ge(s_xload, 32)
            dve.sem_inc(s_x, 4)
            splits(0, 0, 4)
            with dve.Fori(0, DEPTH) as l:
                q = l * (U_LAYER // 4)
                dve.wait_ge(s_par, 2 * l + 2)
                norm_in(2 * l, G_PRE)
                ti = l * T_LAYER
                for v in (hpad[:, :, 0:15], hpad[:, :, 15 + S:HP], upad[:, :, 0:8], upad[:, :, 8 + S:UP]):
                    ins = dve.memset(v, 0.0)
                ins.then_inc(s_pad, 1)
                for c in range(9):
                    for i in range(8):
                        u = 8 * c + i
                        split(q, u + RING)
                        if u >= CONV_FROM:
                            conv(l, 3 * (u - CONV_FROM), min(3 * (u + 1 - CONV_FROM), 4 * TAPS))
                        if i < 7:
                            mixers_dve(dve, l, u)
                    if c < 3:
                        evac(ti + c, 4 * (c % 2), (aT, gT, upad[:, :, 8:8 + S])[c])
                    if c == 1:
                        dve.wait_ge(s_sg, l + 1)
                        dve.wait_ge(s_freeT, ti + 1)
                        dve.tensor_tensor(hpad[:, :, 15:15 + S], aT, f3(T1), ALU.mult).then_inc(s_glu, 1)
                    if c == 8:
                        for i in range(8):
                            kt = OUT_ORDER[i]
                            dve.wait_ge(s_yh, 16 * l + i + 1)
                            dve.scalar_tensor_tensor(out=XT[:, kt, 1, :], in0=(acc if i < 4 else ycT)[:, i % 4, :],
                                                     scalar=col(G_MIX + kt), in1=XT[:, kt, 0, :].bitcast(F32), op0=ALU.mult,
                                                     op1=ALU.subtract).then_inc(s_yt, 1)
                    mixers_dve(dve, l, 8 * c + 7)
                for u in range(U_IN1, U_IN1 + 8):
                    split(q, u + RING)
                    mixers_dve(dve, l, u)
                for i in range(8):
                    kt = 4 + i
                    dve.wait_ge(s_yh, 16 * l + 8 + 2 * (i // 2) + 2)
                    dve.scalar_tensor_tensor(out=XT[:, kt, 1, :], in0=PS[:, 4 + i // 2, (i % 2) * S:(i % 2 + 1) * S],
                                             scalar=col(G_MIX + kt), in1=XT[:, kt, 0, :].bitcast(F32), op0=ALU.mult,
                                             op1=ALU.subtract).then_inc(s_yt, 1)
                splits(q + U_IN1 // 4, 12, KT + 4)
                post_weighted(False, 2 * l, 0)
                splits(q + U_IN1 // 4, KT + 4, U_OUT + 4)
                post(False, 2 * l)
                norm_in(2 * l + 1, G_FFN)
                ffn_dve(dve, splits, evac, q + (U_IN1 + U_OUT) // 4, l, ti + T_IN1)
                q3 = q + (U_IN1 + U_OUT + U_UP) // 4
                splits(q3, 4, FKT + 4)
                post_weighted(True, 2 * l + 1, 0)
                splits(q3, FKT + 4, U_DOWN + 4)
                post(True, 2 * l + 1)

            dve.wait_ge(s_x, 8 * LB + 4)
            dve.memset(wa_bd, 0.0).then_inc(s_bd, 1)
            dve.memset(wx_bd, 0.0).then_inc(s_bd, 1)
            dve.memset(epsc_q, 128 * EPS)
            dve.memset(onec, 1.0)
            dve.wait_ge(s_par2, 5)
            norm_in(2 * LB, G2_PRE)
            dve.wait_ge(s_wb, 1)
            dve.tensor_tensor(w_bal[:, :, :], w_ba, w_bah[:, :, :].bitcast(F32), ALU.subtract).then_inc(s_wbl, 1)
            for v in (qkv_pad[:, :, 0:3], sc_pad[:, :, 0:2], lru_pad[:, :, 0:3]):
                dve.memset(v, 0.0)
            q = DEPTH * (U_LAYER // 4)
            lists = {3: conv_ops(dve, qkvT, qkv_pad, 12, 4, GDN_CW, None, s_qc),
                     5: conv_ops(dve, lru_xc, lru_pad, 4, 4, L_CW, L_CB, s_lc)}
            pending = []
            for c in range(11):
                for i in range(8 * c + 4, 8 * c + 12):
                    split(q, i)
                    if c >= 3:
                        for _ in range(2):
                            if pending:
                                pending.pop(0)()
                if c < T_IN2:
                    dst = (qkv_pad[:, 0:4, 3:3 + S], qkv_pad[:, 4:8, 3:3 + S], qkv_pad[:, 8:12, 3:3 + S], lru_pad[:, :, 3:3 + S],
                           lru_gate, sc_b, sc_c, sc_pad[:, :, 2:2 + S])[c]
                    evac(TB + c, 4 * (c % 2), dst)
                if c == 2:
                    pending += lists[3]
                if c == 4:
                    pending += lists[5]
            for f in pending:
                f()
            mixers2_dve(dve, splits, q + U_IN2 // 4)
            q += U_IN2 // 4
            splits(q, 4, KT + 4)
            post_weighted(False, 2 * LB, 0)
            splits(q, KT + 4, U_OUT + 4)
            post(False, 2 * LB)
            norm_in(2 * LB + 1, G2_FFN)
            q += U_OUT // 4
            ffn2_dve(dve, splits, evac, q)
            q += U_UP // 4
            splits(q, 6, FKT + 4)
            post_weighted(True, 2 * LB + 1, 0)
            splits(q, FKT + 4, U_DOWN)
            post(True, 2 * LB + 1)

        @block.gpsimd
        def _(pool):
            def rope_half(l, w, half, i):
                n = 3 * half + w
                pool.wait_ge(s_freeN, N_IN1 * l + n + 1)
                v = (q_nat, k_nat)[w][:, :, half * 512:(half + 1) * 512].rearrange("p t (h e) -> p t h e", e=64)
                t1, t2 = v[:, :, :, 0:8], v[:, :, :, 8:16]
                cos = C[:, C_ROPE:C_ROPE + 16].rearrange("p (t e) -> p t e", t=NT)[:, :, None, :].to_broadcast((P, NT, 8, 8))
                sin = C[:, C_ROPE + 16:C_ROPE + 32].rearrange("p (t e) -> p t e", t=NT)[:, :, None, :].to_broadcast((P, NT, 8, 8))
                r = [rope[:, k, :].rearrange("p (t h e) -> p t h e", t=NT, h=8) for k in range(4)]
                pool.wait_ge(s_roped, 8 * l + 2 * i)
                for k, (u, f) in enumerate(((t1, cos), (t2, sin), (t2, cos), (t1, sin))):
                    ins = pool.tensor_tensor(r[k], u, f, ALU.mult)
                ins.then_inc(s_rope, 1)
                pool.wait_ge(s_rope, 4 * l + i + 1)
                pool.tensor_tensor(t1, r[0], r[1], ALU.subtract).then_inc(s_roped, 1)
                pool.tensor_tensor(t2, r[2], r[3], ALU.add).then_inc(s_roped, 1)

            pool.wait_ge(s_const, 16)
            with pool.Fori(0, DEPTH) as l:
                pool.wait_ge(s_pad, l + 1)
                pool.wait_ge(s_kc, 32 * (l + 1))
                pool.wait_ge(s_freeT, l * T_LAYER + 3)
                inv = KC[:, K_INV:K_END].rearrange("p (n s) -> p n s", n=4)
                src, width, did = upad, UP, 0
                for k in range(4):
                    d, win = 1 << k, 2 << k
                    width -= d
                    dst = (win_a, win_b)[k % 2]
                    if did:
                        pool.wait_ge(s_pool, 12 * l + did)
                    pool.tensor_tensor(dst[:, k:4, 0:width], src[:, k:4, 0:width], src[:, k:4, d:d + width],
                                       ALU.add).then_inc(s_pool, 1)
                    pool.wait_ge(s_pool, 12 * l + did + 1)
                    at = 8 - win // 2
                    pool.tensor_tensor(pooled[:, k, :], dst[:, k, at:at + S], inv[:, k, :], ALU.mult).then_inc(s_pool, 1)
                    pool.wait_ge(s_pool, 12 * l + did + 2)
                    ins = pool.tensor_tensor(pooled[:, k, :], pooled[:, k, :], upad[:, k, 8:8 + S], ALU.subtract)
                    ins.then_inc(s_pool, 1)
                    did += 3
                    src = dst
                i = 0
                for half in range(2):
                    for w in range(2):
                        rope_half(l, w, half, i)
                        i += 1

        def mixers_pe(pe, mm, l, u):
            def column_sums(src):
                for n in range(4):
                    last = mm(PS[:, 3, 0:S], ones, src[:, n, :], n == 0, n == 3)
                last.then_inc(s_col, 1)

            if u == POOL_AT:
                pe.wait_ge(s_pool, 12 * (l + 1))
                pe.wait_ge(s_kc, 32 * (l + 1))
                for n in range(4):
                    last = mm(PS[:, 6 + n // 2, (n % 2) * S:(n % 2 + 1) * S], pw[:, n, :], pooled[:, n, :], True, True)
                last.then_inc(s_mix, 1)
            if u == POOL_RMS_AT:
                pe.wait_ge(s_sqr, 3 * l + 1)
                column_sums(sq)
            if u == MEAN_AT:
                pe.wait_ge(s_cv, 4 * TAPS * (l + 1))
                column_sums(acc)
            if u == VAR_AT:
                pe.wait_ge(s_sqr, 3 * l + 2)
                column_sums(sq)
            if u == RMS_AT:
                pe.wait_ge(s_sqr, 3 * l + 3)
                pe.wait_ge(s_std, 3 * l + 2)
                column_sums(sq)
            if u in TURN_QK_AT:
                i = TURN_QK_AT.index(u)
                half, src = i // 2, (q_nat, k_nat)[i % 2]
                pe.wait_ge(s_roped, 8 * l + 2 * i + 2)
                if i in (0, 2):
                    pe.wait_ge(s_std, 3 * l + (1, 3)[i // 2])
                if i == 1:
                    pe.wait_ge(s_yc, l + 1)
                if i == 2:
                    pe.wait_ge(s_sb, 16 * l + 8)
                if i == 3:
                    pe.wait_ge(s_freeN, N_IN1 * l + 5)
                for j in range(4):
                    for t in range(NT):
                        b = TURN_QK_BANK[i] + j // 2
                        last = pe.transpose(PS[:, b, (j % 2) * S + t * P:(j % 2) * S + (t + 1) * P],
                                            src[:, t, (4 * half + j) * P:(4 * half + j + 1) * P], ident)
                last.then_inc(s_qkt, 1)
            for h in heads_at(OUTPUT_AT, u):
                pe.wait_ge(s_pt, 16 * l + h + 1)
                if h % 8 == 0:
                    pe.wait_ge(s_freeN, N_IN1 * l + 3 * (h // 8) + 3)
                if h % 4 == 0 and h:
                    pe.wait_ge(s_yb, 4 * l + h // 4)
                for t in range(NT):
                    o = PS[:, 7, (h % 4) * 128 + t * 64:(h % 4) * 128 + (t + 1) * 64]
                    for k in range(2):
                        last = mm(o, probT[:, h % 2, k * S + t * P:k * S + (t + 1) * P], v_nat[:, k, h * 64:(h + 1) * 64], k == 0, k == 1)
                last.then_inc(s_o, 1)
            for h in heads_at(SCORES_AT, u):
                if h % 8 == 0:
                    pe.wait_ge(s_qk, 4 * l + h // 4 + 2)
                if h % 8 and h < 8:
                    pe.wait_ge(s_sb, 16 * l + h)
                if h >= 10:
                    pe.wait_ge(s_sb, 16 * l + h - 1)
                p0 = 64 * (h % 2)
                for t in range(NT):
                    last = mm(PS[:, score_bank(h), t * S:(t + 1) * S], qT[p0:p0 + 64, h // 2, t * P:(t + 1) * P],
                              kT[p0:p0 + 64, h // 2, :], True, True)
                last.then_inc(s_S, 1)
            for h in heads_at(TURN_AT, u):
                pe.wait_ge(s_p, 16 * l + h + 1)
                if h:
                    pe.wait_ge(s_pt, 16 * l + h)
                for t in range(NT):
                    for k in range(2):
                        last = pe.transpose(PS[:, 6, k * S + t * P:k * S + (t + 1) * P],
                                            prob[:, h % 2, t * S + k * P:t * S + (k + 1) * P], ident)
                last.then_inc(s_ptr, 1)

        def ffn_pe(pe, chunk_T, q, ti, xt):
            with pe.Fori(0, 11) as j:
                pe.wait_ge(s_xt, xt)
                pe.wait_ge(s_freeT, ti + 2 * j - 1)
                chunk_T(q + 4 * j, 0, 0)
                pe.wait_ge(s_freeT, ti + 2 * j)
                chunk_T(q + 4 * j + 2, 0, 4)

        def down_pe(pe, wide_units, q, l):
            for c in range(2):
                wide_units(q, FKT * c, HT, list(range(FKT)), c, 0, FKT, lambda i, kt: None if c else pe.wait_ge(s_ht, 11 * l + i // 4 + 1))

        def mixers2_pe(pe, mm):
            def column_sums(src):
                for n in range(4):
                    last = mm(PS[:, 6, 0:S], ones, src[:, n, :], n == 0, n == 3)
                last.then_inc(s_csum, 1)

            def each(bank, lhs, rhs, signal):
                for m in range(8):
                    last = mm(pair(bank)[:, m, :], lhs(m), rhs(m), True, True)
                last.then_inc(signal, 1)

            head = lambda v, m: v[:, m % 4, (m // 4) * P:(m // 4 + 1) * P]
            pe.wait_ge(s_freeN, N_IN1 * LB + 3)
            pe.wait_ge(s_csq, 1)
            column_sums(f3(T1))
            pe.wait_ge(s_lc, 16)
            pe.wait_ge(s_w2, 160)
            for n in range(4):
                mm(quad(2)[:, n, :], wa_bd[:, n, :], lru_xc[:, n, :], True, True)
                last = mm(quad(4)[:, n, :], wx_bd[:, n, :], lru_xc[:, n, :], True, True)
            last.then_inc(s_lm, 1)
            pe.wait_ge(s_csq, 2)
            pe.wait_ge(s_crt, 1)
            column_sums(f3(T1))
            pe.wait_ge(s_wsm, 1)
            pe.wait_ge(s_lg, 2)
            for g in range(4):
                last = pe.transpose(PS[:, 2, g * P:(g + 1) * P], sgu_ws[:, g, :], ident)
            last.then_inc(s_wsm, 1)
            pe.wait_ge(s_gvn, 1)
            pe.wait_ge(s_wst, 1)
            for t in range(NT):
                for g in range(4):
                    last = mm(PS[:, 4 + t, g * P:(g + 1) * P], sgu_wsT[:, g, :], sgu_v[:, t, g * P:(g + 1) * P], True, True)
            last.then_inc(s_gm, 1)
            pe.wait_ge(s_crt, 2)
            for t in range(NT):
                pe.wait_ge(s_gyn, t + 1)
                for g in range(4):
                    last = pe.transpose(quad(6)[:, g, t * P:(t + 1) * P], sgu_v[:, t, g * P:(g + 1) * P], ident)
                last.then_inc(s_gyt, 1)
            for k, b in ((0, 2), (1, 4)):
                pe.wait_ge(s_l2s, k + 1)
                if k:
                    pe.wait_ge(s_gy, 1)
                for h in range(4):
                    last = mm(quad(b)[:, h, :], ones, f3(T1)[:, h, :], True, True)
                last.then_inc(s_l2m, 1)
            pe.wait_ge(s_l2n, 2)
            for k, (b, src) in enumerate(((2, kh), (4, vh))):
                for m in range(8):
                    last = pe.transpose(pair(b)[:, m, :], head(src, m), ident)
                last.then_inc(s_kv, 1)
            pe.wait_ge(s_g, 1)
            pe.wait_ge(s_y2t, 12)
            ct = C[:, C_CAUSAL_T:C_CAUSAL_T + P]
            mm(PS[:, 6, 0:8], ct, g_tok, True, True).then_inc(s_gcm, 1)
            pe.wait_ge(s_kvb, 2)
            each(2, lambda m: g_tok[:, m:m + 1].to_broadcast((P, P)), lambda m: ct, s_grow)
            pe.wait_ge(s_gcum, 1)
            each(6, lambda m: head(kh, m), lambda m: head(kh, m), s_kk)
            pe.wait_ge(s_dd, 2)
            pe.wait_ge(s_fac, 1)
            each(2, lambda m: head(kh, m), lambda m: head(qh, m), s_kk)
            pe.wait_ge(s_P, 1)
            for m in range(8):
                last = pe.transpose(pair(4)[:, m, :], Pm[:, m, :], ident)
            last.then_inc(s_Pt, 1)
            pe.wait_ge(s_att, 1)
            for r in range(5):
                pe.wait_ge(s_pte, r + 1)
                each(2, lambda m: PmT[:, m, :], lambda m: Pm[:, m, :], s_sq)
                if r < 4:
                    each(4, lambda m: Pm[:, m, :], lambda m: PmT[:, m, :], s_sq)
                pe.wait_ge(s_P, r + 2)
                pe.wait_ge(s_tt, r + 1)
                each(6, lambda m: Pm[:, m, :], lambda m: Tt[:, m, :], s_te)
            pe.wait_ge(s_tt, 6)
            pe.wait_ge(s_kbg, 3)
            each(2, lambda m: kbg[:, m, :], lambda m: Tt[:, m, :], s_wu)
            each(4, lambda m: Tt[:, m, :], lambda m: v_beta[:, m, :], s_wu)
            pe.wait_ge(s_wue, 1)
            pe.wait_ge(s_wue2, 1)
            pe.wait_ge(s_qg, 1)
            for n in range(4):
                t, r = n // 2, 64 * (n % 2)
                if n:
                    pe.wait_ge(s_st, n)
                    for h in range(4):
                        last = mm(PS[r:r + 64, 2, h * P:(h + 1) * P], wT[:, 4 * t + h, r:r + 64], state[:, h, :], True, True)
                    last.then_inc(s_vn, 1)
                    pe.wait_ge(s_vne, n)
                    pe.wait_ge(s_oe, n)
                if n < 3:
                    for h in range(4):
                        m = 4 * t + h
                        last = mm(PS[:, 6, h * P:(h + 1) * P], kg[r:r + 64, m, :], u_by[r:r + 64, m, :], True, True)
                    last.then_inc(s_ks, 1)
                for h in range(4):
                    m = 4 * t + h
                    o = PS[r:r + 64, 3, h * P:(h + 1) * P]
                    if n:
                        mm(o, head(qh, m)[:, r:r + 64], state[:, h, :], True, False)
                    last = mm(o, decT[r:r + 64, m, r:r + 64], u_by[r:r + 64, m, :], n == 0, True)
                last.then_inc(s_os, 1)
            pe.wait_ge(s_oz, 1)
            for m in range(8):
                last = pe.transpose(quad(6)[:, m % 4, (m // 4) * P:(m // 4 + 1) * P], o_by[:, m, :], ident)
            last.then_inc(s_ot, 1)

        @block.tensor
        def _(pe):
            def unit_ready(q, i):
                pe.wait_ge(s_lo, 4 * q + i + 5)

            def mm(o, w, r, start, stop):
                return pe.matmul(o, w, r, start=start, stop=stop, skip_group_check=True)

            def chunk_T(q, i0, base, xready=None, beside=None):
                for i in range(8):
                    unit_ready(q, i0 + i)
                    slot = (i0 + i) % RING
                    for k in range(2):
                        kt = 2 * i + k
                        if xready:
                            xready(kt)
                        for n in range(4):
                            c = k * CHUNK + n * P
                            mm(PS[:, base + n, :], WH[:, slot, c:c + P], XT[:, kt, :, :].rearrange("p a b -> p (a b)"), kt == 0, False)
                            last = mm(PS[:, base + n, 0:S], WL[:, slot, c:c + P], XT[:, kt, 0, :], False, kt == KT - 1)
                    last.then_inc(s_pe, 1)
                    if beside:
                        beside(i)

            def three(out_of, xt, tok, wh, wl, cols, first, final):
                hi, lo = xt[:, 0, tok], xt[:, 1, tok]
                for n in range(cols):
                    mm(out_of(n), hi, wh[:, n * CHUNK:(n + 1) * CHUNK], first, False)
                for n in range(cols):
                    mm(out_of(n), hi, wl[:, n * CHUNK:(n + 1) * CHUNK], False, False)
                for n in range(cols):
                    last = mm(out_of(n), lo, wh[:, n * CHUNK:(n + 1) * CHUNK], False, final)
                return last

            def chunk_N(q, i0, base, beside=None):
                for i in range(8):
                    unit_ready(q, i0 + i)
                    slot = (i0 + i) % RING
                    for k in range(2):
                        kt = 2 * i + k
                        for t in range(NT):
                            last = three(lambda n: PS[:, base + t, :], XT[:, kt], slice(t * P, (t + 1) * P),
                                         WH[:, slot, k * CHUNK:(k + 1) * CHUNK], WL[:, slot, k * CHUNK:(k + 1) * CHUNK],
                                         1, kt == 0, kt == KT - 1)
                    last.then_inc(s_pe, 1)
                    if beside:
                        beside(i)

            def wide_units(q, i0, src, order, c, lo_, hi_, ready):
                for i in range(lo_, hi_):
                    unit_ready(q, i0 + i)
                    ready(i, order[i])
                    slot = (i0 + i) % RING
                    for t in range(NT):
                        last = three(lambda n: PS[:, 4 * c + 2 * t + n, :], src[:, order[i]], slice(t * P, (t + 1) * P),
                                     WH[:, slot, :], WL[:, slot, :], 2, i == 0, i == len(order) - 1)
                    last.then_inc(s_pe, 1)
                return last

            def norm_in(n):
                for t in range(NT):
                    pe.wait_ge(s_xs, 2 * n + t + 1)
                    for j in range(8):
                        if j == 4:
                            pe.wait_ge(s_xs2, 2 * n + t + 1)
                        for k in range(2):
                            kt = 2 * j + k
                            last = pe.transpose(PS[:, j, k * S + t * P:k * S + (t + 1) * P], xs[:, t, kt * P:(kt + 1) * P], ident)
                        if t == 1:
                            last.then_inc(s_tr, 1)

            pe.sem_inc(s_pe, 4)
            pe.wait_ge(s_const, 16)
            with pe.Fori(0, DEPTH) as l:
                q = l * (U_LAYER // 4)
                pe.wait_ge(s_rows, 16 * 8 * (l + 1))
                pe.wait_ge(s_x, 8 * l + 4)
                for r in range(2):
                    pe.transpose(PS[:, 0, r * P:(r + 1) * P], ROWS[:, r, :], ident).then_inc(s_prt, 1)
                pe.wait_ge(s_par, 2 * l + 2)
                norm_in(2 * l)
                ti, ni = T_LAYER * l, N_IN1 * l
                for c in range(9):
                    base = 4 * (c % 2)
                    if c == 0:
                        pe.wait_ge(s_xt, 32 * l + 8)
                    elif c == 1:
                        pe.wait_ge(s_xt, 32 * l + 16)
                    elif c < 5:
                        pe.wait_ge(s_freeT, ti + c - 1)
                    else:
                        pe.wait_ge(s_freeN, ni + c - 4)
                    if c < 3:
                        chunk_T(q, 8 * c, base, (lambda kt: pe.wait_ge(s_xt, 32 * l + kt + 1)) if c == 0 else None)
                    else:
                        chunk_N(q, 8 * c, base, lambda i: mixers_pe(pe, mm, l, 8 * c + i))
                q1 = q + U_IN1 // 4
                for i in range(8):
                    if i == 0:
                        pe.wait_ge(s_freeN, ni + 6)
                    wide_units(q1, 0, XT, OUT_ORDER, 0, i, i + 1, lambda i, kt: pe.wait_ge(s_yt, 16 * l + i + 1))
                    mixers_pe(pe, mm, l, U_IN1 + i)
                for t in range(NT):
                    pe.wait_ge(s_ybn, 2 * l + t + 1)
                    for j in range(4):
                        for k in range(2):
                            kt = 2 * j + k
                            last = pe.transpose(PS[:, 4 + j, k * S + t * P:k * S + (t + 1) * P], yb_n[:, t, kt * P:(kt + 1) * P], ident)
                        if t == 1:
                            last.then_inc(s_ybt, 1)
                wide_units(q1, 0, XT, OUT_ORDER, 0, 8, 16, lambda i, kt: pe.wait_ge(s_yt, 16 * l + i + 1))
                wide_units(q1, 16, XT, OUT_ORDER, 1, 0, 16, lambda i, kt: None)
                pe.wait_ge(s_x, 8 * l + 8)
                norm_in(2 * l + 1)
                ffn_pe(pe, chunk_T, q1 + U_OUT // 4, ti + T_IN1, 32 * l + 32)
                q3 = q1 + (U_OUT + U_UP) // 4
                down_pe(pe, wide_units, q3, l)
            pe.wait_ge(s_rows2, 16 * 16)
            pe.wait_ge(s_x, 8 * LB + 4)
            for r in range(5):
                pe.transpose(PS[:, r // 4, (r % 4) * P:(r % 4 + 1) * P], rows2[:, r, :], ident).then_inc(s_prt2, 1)
            pe.wait_ge(s_par2, 5)
            norm_in(2 * LB)
            q = DEPTH * (U_LAYER // 4)
            for c in range(11):
                base = 4 * (c % 2)
                if c < 2:
                    pe.wait_ge(s_xt, 32 * LB + 8 * c + 8)
                elif c < 9:
                    pe.wait_ge(s_freeT, TB + c - 1)
                elif c == 9:
                    pe.wait_ge(s_freeT, TB + 8)
                    pe.wait_ge(s_wbl, 1)
                    for t in range(NT):
                        for kt in range(KT):
                            hi, lo = XT[:, kt, 0, t * P:(t + 1) * P], XT[:, kt, 1, t * P:(t + 1) * P]
                            o = PS[:, 7, 8 * t:8 * t + 8]
                            mm(o, hi, w_bah[:, kt, :], kt == 0, False)
                            mm(o, hi, w_bal[:, kt, :], False, False)
                            last = mm(o, lo, w_bah[:, kt, :], False, kt == KT - 1)
                    last.then_inc(s_ba, 1)
                else:
                    pe.wait_ge(s_freeN, N_IN1 * LB + 1)
                if c < T_IN2:
                    chunk_T(q, 8 * c, base, (lambda kt: pe.wait_ge(s_xt, 32 * LB + kt + 1)) if c == 0 else None)
                else:
                    chunk_N(q, 8 * c, base)
            mixers2_pe(pe, mm)
            q += U_IN2 // 4
            for c in range(2):
                wide_units(q, 16 * c, XT, OUT_ORDER2, c, 0, KT, (lambda i, kt: None) if c else (lambda i, kt: pe.wait_ge(s_y2t, i + 1)))
            pe.wait_ge(s_x, 8 * LB + 8)
            norm_in(2 * LB + 1)
            q += U_OUT // 4
            with pe.Fori(0, 11) as j:
                pe.wait_ge(s_xt, 32 * LB + 32)
                pe.wait_ge(s_freeT, TB + T_IN2 + 2 * j - 1)
                chunk_T(q + 4 * j, 0, 0)
                pe.wait_ge(s_freeT, TB + T_IN2 + 2 * j)
                chunk_T(q + 4 * j + 2, 0, 4)
            q += U_UP // 4
            down_pe(pe, wide_units, q, LB)


INPUTS = """x w_in conv_w conv_b conv_ln_g conv_ln_b pool_w pool_scale g_mix w_out g_pre_mix g_post_mix g_pre_ffn
g_post_ffn w_gate w_up w_down pre_mix_norm_2 w_in_2 gdn_conv_w_2 gdn_a_log_2 gdn_dt_bias_2 gdn_norm_w_2 lru_conv_w_2
lru_conv_b_2 lru_wa_2 lru_ba_2 lru_wx_2 lru_bx_2 lru_lambda_2 sgu_ln_w_2 sgu_ln_b_2 sgu_ws_2 sgu_b_2 sconv_w_2
grp_norm_w_2 w_out_2 post_mix_norm_2 pre_ffn_norm_2 ffn_up_2 ffn_conv_w_2 ffn_conv_b_2 ffn_down_2
post_ffn_norm_2""".split()


def kernel(**inputs):
    import concourse.bacc as bacc
    from concourse.bass_utils import run_bass_kernel_spmd

    nc = bacc.Bacc("TRN2", target_bir_lowering=False, num_devices=1)
    constants, key_constants = shape_constants()
    arrays = {f"in_{n}_dram": np.ascontiguousarray(inputs[n]) for n in INPUTS}
    arrays["in_constants_dram"] = constants
    arrays["in_key_constants_dram"] = key_constants
    a = {n[3:-5]: nc.dram_tensor(n, v.shape, F32, kind="ExternalInput").ap() for n, v in arrays.items()}
    out = nc.dram_tensor("out_dram", (1, S, D), F32, kind="ExternalOutput").ap()
    build(nc, a, out)
    return run_bass_kernel_spmd(nc, [arrays], core_ids=[0]).results[0]["out_dram"]
```

```python
from contextlib import ExitStack

import numpy as np

import concourse.bass as bass
from concourse import mybir

F32 = mybir.dt.float32
F32R = mybir.dt.float32r
ALU = mybir.AluOpType
ACT = mybir.ActivationFunctionType
AX = mybir.AxisListType.X

P = 128
S = 256
NT = S // P
D = 2048
KT = D // P
FF = 5632
FKT = FF // P
DEPTH = 2
EPS = 1e-6
NEG = -1e30
RING = 4
CHUNK = 512
UNIT = 1024

C_ID, C_ONE, C_CAUSAL, C_STRICT, C_CAUSAL_T, C_TRIL = (P * i for i in range(6))
C_ROPE = 6 * P
C_END = C_ROPE + 2 * NT * 8
K_BIAS = 0
K_INV = 2 * S
K_END = K_INV + 4 * S


def shape_constants():
    c = np.zeros((P, C_END), np.float32)
    i = np.arange(P)
    same = (i[:, None] // 64) == (i[None, :] // 64)
    c[:, C_ID:C_ID + P] = np.eye(P)
    c[:, C_ONE:C_ONE + P] = 1.0
    c[:, C_CAUSAL:C_CAUSAL + P] = same & (i[:, None] >= i[None, :])
    c[:, C_STRICT:C_STRICT + P] = same & (i[:, None] > i[None, :])
    c[:, C_CAUSAL_T:C_CAUSAL_T + P] = same & (i[:, None] <= i[None, :])
    c[:, C_TRIL:C_TRIL + P] = i[:, None] >= i[None, :]
    pos = np.arange(S, dtype=np.float32)
    inv = np.float32(500000.0) ** (-np.arange(0, 16, 2, dtype=np.float32) / np.float32(16))
    ang = (pos[:, None] * inv[None, :]).astype(np.float32).reshape(NT, P, 8).transpose(1, 0, 2)
    c[:, C_ROPE:C_ROPE + 16] = np.cos(ang).reshape(P, 16)
    c[:, C_ROPE + 16:C_ROPE + 32] = np.sin(ang).reshape(P, 16)
    k = np.zeros((P, K_END), np.float32)
    q, key = np.arange(S)[:, None], np.arange(S)[None, :]
    count = (abs(q - key) <= 64).astype(int) + ((q - key) % 4 == 0) + ((q - key) % 16 == 0)
    bias = np.where(count > 0, np.log(np.maximum(count, 1)), NEG).astype(np.float32)
    k[:, 0:2 * S] = bias.reshape(NT, P, S).transpose(1, 0, 2).reshape(P, NT * S)
    t = np.arange(S)
    for n, win in enumerate((2, 4, 8, 16)):
        size = np.clip(t + win - win // 2, 0, S) - np.clip(t - win // 2, 0, S)
        k[:, K_INV + n * S:K_INV + (n + 1) * S] = (1.0 / size.astype(np.float32))[None, :]
    return c, k


U_IN1, U_OUT, U_UP, U_DOWN = 9 * 8, 2 * KT, 22 * 8, 2 * FKT
U_LAYER = U_IN1 + U_OUT + U_UP + U_DOWN
U_IN2 = 11 * 8
T_IN1, N_IN1, T_LAYER = 3, 6, 3 + 22
OUT_ORDER = [0, 1, 2, 3, 12, 13, 14, 15, 4, 5, 6, 7, 8, 9, 10, 11]
TAPS = 31
HEADS = 16
TURN_QK_BANK = [2, 6, 2, 4]
score_bank = lambda h: 2 if h < 8 else 4 + h % 2
SCORES_AT = [47 + 2 * h for h in range(8)] + [69 + h for h in range(8)]
TURN_AT = [s + 1 for s in SCORES_AT]
OUTPUT_AT = [s + 2 for s in SCORES_AT[:8]] + [72, 73, 73] + [74 + h for h in range(5)]
POOL_AT, POOL_RMS_AT = 40, 42
TURN_QK_AT = [44, 46, 64, 67]
CONV_FROM, MEAN_AT, VAR_AT, RMS_AT = 16, 58, 60, 62
SQUARES_AT = [65, 65, 75, 78]
heads_at = lambda table, u: [h for h in range(HEADS) if table[h] == u]
IN2 = dict(lru_x=2056, lru_gate=2568, q=0, k=512, v=1024, z=1536, sgu_v=3592, sgu_u=3080, sc_c=4616, sc_h=5128, sc_b=4104)
BY_TOKEN2 = ("z", "sgu_v", "sgu_u")
BA = 2048
OUT_ORDER2 = [4, 5, 6, 7, 8, 9, 10, 11, 0, 1, 2, 3, 12, 13, 14, 15]
GATES_SPLIT_AT, GATES_MM_AT, GATES_AT = 7, 9, 10
LRU_CONV_AT, LRU_MIX_AT, LRU_A_AT, LRU_SCAN_AT, LRU_SQ_AT, LRU_RMS_AT = 8, 13, 15, 17, 19, 21
GCUM_AT, DECAY_AT, DECAY_T_AT, DECAY_EXP_AT, DECAY_MASK_AT = 22, 23, 24, 25, 26
CONV_AT, SILU_AT, L2_AT = (27, 32, 44), (31, 36, 48), (32, 37)
KK_AT, K_TURN_AT, KQ_AT, P_TURN_AT = 38, 39, 40, 41
POWER_AT, PRODUCT_AT = [42 + 2 * r for r in range(5)], [43 + 2 * r for r in range(5)]
V_TURN_AT, GATED_AT, WU_AT = 49, (49, 51, 50), 53
STATE_AT, CHUNK_AT = (0, 57, 60, 63), (55, 58, 61, 64)
GDN_SQ_AT, GDN_RMS_AT, GDN_TURN_AT, Z_AT = 65, 66, 67, 50
SGU_GELU_AT, SGU_MEAN_AT, SGU_NORM_AT, SGU_U_AT, SGU_W_AT, SGU_MIX_AT, SGU_RMS_AT, SGU_TURN_AT = 56, 57, 59, 68, 66, 69, 70, 72
SC_MUL_AT, SC_CONV_AT, SC_OUT_AT, SC_SQ_AT, SC_RMS_AT, SC_SPLIT_AT = 80, 81, 87, 88, 89, 90


def build(nc, a, out, stop=None):
    with ExitStack() as ctx:
        def sb(name, shape, dt=F32):
            return ctx.enter_context(nc.sbuf_tensor(name, shape, dt))

        def sem(name):
            return ctx.enter_context(nc.semaphore(name))

        x = sb("x", [P, NT, D])
        with nc.sbuf_tensor("XT", [P, KT, 2, S], F32R) as XT:
            pass
        XS = sb("XS", [P, KT * 2 * S])
        WS = sb("WS", [P, RING, UNIT])
        WH = sb("WH", [P, RING, UNIT], F32R)
        WL = sb("WL", [P, RING, UNIT], F32R)
        XL = sb("XL", [P, 4, S])
        T1 = sb("T1", [P, 1032])
        T2 = sb("T2", [P, 1024])
        T3 = sb("T3", [P, 1024])
        C = sb("C", [P, C_END])
        PR = sb("PR", [P, 512])
        ROWS = sb("ROWS", [P, 2, P])
        SM = sb("SM", [P, 164])
        w_ba2 = sb("w_ba2", [P, KT, 16], F32R)
        with nc.sbuf_tensor("HT", [P, FKT, 2, S], F32R) as HT:
            pass
        SCR = sb("SCR", [P, FKT * 2 * S])
        PS = ctx.enter_context(nc.psum_tensor("PS", [P, 8, CHUNK], F32))

        def scr(at, *dims):
            n = int(np.prod(dims))
            v = SCR[:, at:at + n]
            if len(dims) == 2:
                v = v.rearrange("p (a b) -> p a b", a=dims[0])
            if len(dims) == 3:
                v = v.rearrange("p (a b c) -> p a b c", a=dims[0], b=dims[1])
            return v

        ident = C[:, C_ID:C_ID + P]
        ones = C[:, C_ONE:C_ONE + P]

        xs = scr(9528, NT, D)
        junk = scr(4216, NT, D)
        aT, gT = scr(0, 4, S), scr(1024, 4, S)
        HP = S + TAPS - 1
        hpad = scr(2048, 4, HP)
        acc = scr(3192, 4, S)
        UP = S + 16
        upad = scr(4216, 4, UP)
        win_a, win_b = scr(5304, 4, UP), scr(6392, 4, UP)
        pooled = scr(7480, 4, S)
        ycT = scr(8504, 4, S)
        q_nat, k_nat, v_nat = scr(9528, NT, 1024), scr(11576, NT, 1024), scr(13624, NT, 1024)
        qT, kT = scr(15672, 8, S), scr(17720, 8, S)
        KC = scr(19768, K_END)
        rope = scr(21304, 4, 128)
        pw = scr(21816, 4, P)
        neg_s = scr(0, 2, NT * S)
        prob = scr(1024, 2, NT * S)
        probT = scr(5304, 2, NT * S)
        y_b = q_nat
        yb_n = k_nat
        gbc = (T1, T2)
        post_tmp = lambda down: scr(0, 2, NT, 1024) if not down else (
            XS[:, 0:4096].rearrange("p (c t n) -> p c t n", c=2, t=NT))
        sq = T3[:, :].rearrange("p (a b) -> p a b", a=4)
        f3 = lambda t: t[:, 0:1024].rearrange("p (a b) -> p a b", a=4)
        flat = lambda v: v.rearrange("p a b -> p (a b)")

        LB = DEPTH
        TB, NB = LB * T_LAYER, LB * N_IN1
        qkv_pad = scr(0, 12, S + 3)
        k_by, v_by, kbg = (scr(1024 * i, 8, P) for i in range(3))
        qkvT = scr(3108, 12, S)
        qh, kh, vh = (qkvT[:, 4 * i:4 * i + 4, :] for i in range(3))
        sc_b, sc_c, sc_pad = scr(6180, 4, S), scr(7204, 4, S), scr(8228, 4, S + 2)
        lru_pad, lru_gate, lru_xc = scr(9260, 4, S + 3), scr(10296, 4, S), scr(11320, 4, S)
        lru_r, lru_i = scr(12344, 4, S), scr(13368, 4, S)
        z, sgu_u, sgu_v = (scr(14392 + 1024 * i, NT, 512) for i in range(3))
        dec, decT, Pm, PmT = (scr(17464 + 1024 * i, 8, P) for i in range(4))
        wa_bd, wx_bd = scr(17464, 4, P), scr(17976, 4, P)
        sgu_lnw, sgu_lnb = scr(12344, 512), scr(12856, 512)
        sgu_ws, sgu_wsT = scr(13368, 4, P), scr(13880, 4, P)
        sqs = scr(9260, 4, S)
        sgu_yT, gdn_yT = lru_gate, qh
        w_ba = scr(20536, KT, 8)
        state = scr(21560, 4, P)
        wT, u_by, kg = Pm, PmT, dec
        o_by, k_sq = scr(0, 8, P), scr(1024, 8, P)
        egrow = T1[:, 0:1024].rearrange("p (a b) -> p a b", a=8)
        v_beta = T2[:, :].rearrange("p (a b) -> p a b", a=8)
        Tt = T3[:, :].rearrange("p (a b) -> p a b", a=8)
        rows2 = XS[:, 4096:4096 + 5 * P].rearrange("p (a b) -> p a b", a=5)
        baT, ba = T2[0:16, 0:2 * S], T3[:, 0:16].rearrange("p (t n) -> p t n", t=NT)
        ffn_pad = T1[:, :].rearrange("p (a b) -> p a b", a=4)
        conv_j = C[:, C_ROPE:C_ROPE + 32].rearrange("p (k g n) -> p k g n", k=4, g=2)
        mask = lambda at: C[:, at:at + P][:, None, :].to_broadcast((P, 8, P))
        eight = lambda v: v[:, :, None].to_broadcast((P, 8, P))
        pair = lambda b: PS[:, b:b + 2, :].rearrange("p a (m c) -> p (a m) c", c=P)
        quad = lambda b: PS[:, b:b + 2, :].rearrange("p a (m c) -> p (a m) c", c=S)

        ssp = SM[:, 160:164]
        ss, rms, rinv = SM[:, 0:2], SM[:, 2:4], SM[:, 4:6]
        ssf, ssf2, rmsf, rinvf = SM[:, 6:10], SM[:, 10:12], SM[:, 12:14], SM[:, 14:16]
        neg_max = SM[:, 16:20]
        den = SM[:, 20:52]
        rden = SM[:, 52:84]
        ssb, rmsb, rinvb = SM[:, 84:86], SM[:, 86:88], SM[:, 88:90]
        ssb4 = SM[:, 140:148].rearrange("p (t g) -> p t g", t=NT)
        epsc, epsc_q, onec = SM[:, 90:91], SM[:, 91:92], SM[:, 92:93]
        gate_in = SM[:, 96:108]
        gate_abs, gate_ln = SM[:, 108:120], SM[:, 120:132]
        a_log, dt_bias = SM[:, 132:136], SM[:, 136:140]
        g_tok, beta, nbeta = SM[:, 16:24], SM[:, 24:32], SM[:, 32:40]
        gcum, gbeta, gtail = SM[:, 40:48], SM[:, 48:56], SM[:, 56:64]
        o_ss, o_rms, o_rinv = SM[:, 64:72], SM[:, 72:80], SM[:, 80:88]
        vm, vv, vs, vr = (SM[:, 140 + 2 * i:142 + 2 * i] for i in range(4))
        cs, cr, ci = (SM[:, 148 + 2 * i:150 + 2 * i] for i in range(3))
        rate = SM[:, 154:158]
        (G2_PRE, G2_FFN, G2_GRP, G2_GDN, L_CB, L_LAM, L_BA, L_BX, L_CW, S_CW, SGU_B) = (
            0, 16, 32, 44, 45, 49, 53, 57, 61, 77, 89)
        GDN_CW, F_CW = 93, 141
        G_PRE, G_FFN, G_MIX, CONV_B, LN_G, LN_B, POOL_SC, CONV_W = 0, 16, 32, 48, 52, 56, 60, 64
        col = lambda i: PR[:, i:i + 1]

        s_stage = [sem(f"s_stage{i}") for i in range(RING)]
        s_hi, s_lo, s_pe = sem("s_hi"), sem("s_lo"), sem("s_pe")
        s_const, s_xload, s_eps = sem("s_const"), sem("s_xload"), sem("s_eps")
        s_rows, s_prt, s_par = sem("s_rows"), sem("s_prt"), sem("s_par")
        s_x = sem("s_x")
        s_ss, s_sst, s_rms, s_rinv, s_xs, s_xs2, s_tr, s_xh, s_xt = (
            sem("s_" + n) for n in "ss ss_total rms rinv xs xs2 tr xh xt".split())
        s_xl, s_freeT, s_freeN = (sem("s_" + n) for n in "xl freeT freeN".split())
        s_sg, s_pad, s_glu, s_cv = (sem("s_" + n) for n in "sg pad glu cv".split())
        s_act, s_h, s_hh, s_ht = (sem("s_" + n) for n in "act h hh ht".split())
        s_gb, s_sf, s_sfs, s_rf, s_rfi, s_pn = (sem("s_" + n) for n in "gb sf sfs rf rfi pn".split())
        s_pool, s_mix, s_yc = (sem("s_" + n) for n in "pool mix yc".split())
        s_rope, s_roped, s_qkt, s_qk = (sem("s_" + n) for n in "rope roped qkt qk".split())
        s_S, s_sb, s_nm, s_p, s_ptr, s_pt, s_o, s_rd, s_yb = (sem("s_" + n) for n in "S sb nm p ptr pt o rd yb".split())
        s_sqr, s_col, s_std, s_rstd, s_ya, s_ycn, s_lna = (sem("s_" + n) for n in "sqr col std rstd ya ycn lna".split())
        s_ssb, s_sbs, s_rb, s_rbi, s_ybn, s_ybt, s_yh, s_yt = (sem("s_" + n) for n in "ssb sbs rb rbi ybn ybt yh yt".split())
        s_out, s_kc = sem("s_out"), sem("s_kc")
        s_rows2, s_prt2, s_par2, s_w2, s_bd = (sem("s2_" + n) for n in "rows prt par small bd".split())
        s_wb, s_wbl, s_ba = (sem("s2_" + n) for n in "wb wbl ba".split())
        s_qc, s_qs, s_l2s, s_l2m, s_l2r, s_l2n = (sem("s2_" + n) for n in "qconv qsilu l2sq l2sum l2root l2n".split())
        s_kv, s_kvb = sem("s2_kvT"), sem("s2_kv_by")
        s_dc, s_ac = sem("s2_dve_chain"), sem("s2_act_chain")
        s_gin, s_gln, s_g, s_gcm, s_gcum, s_grow = (sem("s2_" + n) for n in "gin gln g gcm gcum grow".split())
        s_dd, s_de, s_dm, s_kk, s_P, s_Pt, s_att = (sem("s2_" + n) for n in "dd de dm kk P Pt att".split())
        s_sq, s_te, s_tt = (sem("s2_" + n) for n in "sq te tt".split())
        s_fac, s_kbg, s_wu, s_wue = (sem("s2_" + n) for n in "fac kbg wu wue".split())
        s_vn, s_vne, s_os, s_oe, s_st, s_qg = (sem("s2_" + n) for n in "vn vne os oe st qg".split())
        s_on, s_ot = sem("s2_on"), sem("s2_ot")
        s_lm, s_lg, s_la, s_lt, s_lr, s_lsq, s_ly = (sem("s2_" + n) for n in "lm lg la lt lrec lsqrt ly".split())
        s_sy, s_csq, s_csum, s_crt, s_cn = (sem("s2_" + n) for n in "sy csq csum croot cn".split())
        s_gelu, s_gn, s_wsm, s_gm, s_gy, s_gyn, s_gyt = (sem("s2_" + n) for n in "gelu gn wsm gm gy gyn gyt".split())
        s_groot, s_wst, s_eg, s_fac2, s_pte, s_on2, s_tap, s_fc = (sem("s2_" + n) for n in "groot wst eg fac2 pte on2 tap fc".split())
        s_lc, s_scv, s_gvn, s_wue2, s_ks, s_oz = (sem("s2_" + n) for n in "lc scv gvn wue2 ks oz".split())
        s_zs, s_y2h, s_y2t, s_cj = (sem("s2_" + n) for n in "zs y2h y2t cj".split())

        block = ctx.enter_context(nc.Block())

        @block.sync
        def _(sp):
            def load(q, i, src, width):
                sp.wait_ge(s_lo, 4 * q + i + 1)
                dst = WS[:, i % RING, :]
                if width:
                    dst = dst.rearrange("p (k n) -> p k n", n=width)
                sp.dma_start(dst, src).then_inc(s_stage[i % RING], 16)

            def chunk512(q, w, c):
                for i in range(8):
                    load(q, i, w[2 * i * P:(2 * i + 2) * P, c].rearrange("(k p) n -> p k n", p=P), CHUNK)

            def out_proj(q, w):
                for c in range(2):
                    for i, kt in enumerate(OUT_ORDER):
                        load(q, 16 * c + i, w[kt * P:(kt + 1) * P, c * 1024:(c + 1) * 1024], 0)

            def down_proj(q, w):
                for c in range(2):
                    with sp.Fori(0, FKT // 4) as r:
                        rows = w.rearrange("(r k p) n -> r k p n", k=4, p=P)
                        for i in range(4):
                            load(q + r + 11 * c, i, rows[r, i, :, c * 1024:(c + 1) * 1024], 0)

            sp.dma_start(C[:, :], a["constants"]).then_inc(s_const, 16)
            for t in range(NT):
                sp.dma_start(x[:, t, :], a["x"][0, t * P:(t + 1) * P, :]).then_inc(s_xload, 16)
            with sp.Fori(0, DEPTH) as l:
                q = l * (U_LAYER // 4)
                sp.wait_ge(s_eps, 1)
                sp.wait_ge(s_prt, 2 * l)
                small = [("g_pre_mix", 16), ("g_pre_ffn", 16), ("g_mix", 16), ("conv_b", 4), ("conv_ln_g", 4),
                         ("conv_ln_b", 4), ("pool_scale", 4)]
                at = 0
                for name, n in small:
                    sp.dma_start(ROWS[at:at + n, 0, :], a[name][l].rearrange("(n p) -> n p", p=P)).then_inc(s_rows, 16)
                    at += n
                sp.dma_start(ROWS[0:4 * TAPS, 1, :], a["conv_w"][l].rearrange("j (n p) -> (j n) p", p=P)).then_inc(s_rows, 16)
                w = a["w_in"][l]
                order = [0, 1, 8, 2, 4, 6, 3, 5, 7]
                for n, c in enumerate(order):
                    chunk512(q + 2 * n, w, slice(c * CHUNK, (c + 1) * CHUNK))
                q1 = q + U_IN1 // 4
                out_proj(q1, a["w_out"][l])
                q2 = q1 + U_OUT // 4
                with sp.Fori(0, 11) as j:
                    chunk512(q2 + 4 * j, a["w_gate"][l], bass.ds(j * CHUNK, CHUNK))
                    chunk512(q2 + 4 * j + 2, a["w_up"][l], bass.ds(j * CHUNK, CHUNK))
                q3 = q2 + U_UP // 4
                down_proj(q3, a["w_down"][l])
            a2 = lambda n: a[n + "_2"][0]
            at = 0
            for name, n in (("pre_mix_norm", 16), ("pre_ffn_norm", 16), ("grp_norm_w", 12), ("gdn_norm_w", 1), ("lru_conv_b", 4),
                            ("lru_lambda", 4), ("lru_ba", 4), ("lru_bx", 4), ("lru_conv_w", 16), ("sconv_w", 12), ("sgu_b", 4)):
                v = a2(name)
                if name in ("lru_ba", "lru_bx"):
                    v = v.rearrange("(n h) p -> n (h p)", h=2)
                elif name == "gdn_norm_w":
                    v = v.rearrange("(n p) -> n p", p=P)
                elif len(v.shape) == 1:
                    v = v.rearrange("(n p) -> n p", p=P)
                elif name != "sgu_b":
                    v = v.rearrange("j (n p) -> (j n) p", p=P)
                sp.dma_start(rows2[at:at + n, 0, :], v).then_inc(s_rows2, 16)
                at += n
            sp.dma_start(rows2[0:48, 1, :], a2("gdn_conv_w").rearrange("j (n p) -> (j n) p", p=P)).then_inc(s_rows2, 16)
            taps = a2("ffn_conv_w").rearrange("j (n p) -> (j n) p", p=P)
            sp.dma_start(rows2[:, 2, :], taps[0:128]).then_inc(s_rows2, 16)
            sp.dma_start(rows2[:, 3, :], taps[128:256]).then_inc(s_rows2, 16)
            sp.dma_start(rows2[0:8, 4, :], taps[256:264]).then_inc(s_rows2, 16)
            sp.dma_start(rows2[8:96, 4, :], a2("ffn_conv_b").rearrange("(n p) -> n p", p=P)).then_inc(s_rows2, 16)
            q = DEPTH * (U_LAYER // 4)
            for n, c in enumerate(IN2.values()):
                chunk512(q + 2 * n, a["w_in_2"][0], slice(c, c + CHUNK))
            q += U_IN2 // 4
            for c in range(2):
                for i, kt in enumerate(OUT_ORDER2):
                    load(q, 16 * c + i, a["w_out_2"][0, kt * P:(kt + 1) * P, c * 1024:(c + 1) * 1024], 0)
            q += U_OUT // 4
            with sp.Fori(0, 11) as j:
                chunk512(q + 4 * j, a["ffn_up_2"][0], bass.ds(j * CHUNK, CHUNK))
                chunk512(q + 4 * j + 2, a["ffn_up_2"][0], bass.ds(j * CHUNK + FF, CHUNK))
            q += U_UP // 4
            down_proj(q, a["ffn_down_2"][0])
            sp.wait_ge(s_x, 4 + 8 * (DEPTH + 1))
            for t in range(NT):
                sp.dma_start(out[0, t * P:(t + 1) * P, :], x[:, t, :]).then_inc(s_out, 16)
            sp.wait_ge(s_out, 32)

        def mixers_act(act, l, u):
            def root_of_sums(k):
                act.wait_ge(s_col, 4 * l + k + 1)
                act.activation(XL[:, 0, :], PS[:, 3, 0:S], ACT.Sqrt, scale=1.0 / 512, bias=epsc).then_inc(s_std, 1)

            if u == POOL_AT:
                act.wait_ge(s_mix, l + 1)
                for n in range(4):
                    ins = act.activation(ycT[:, n, :], PS[:, 6 + n // 2, (n % 2) * S:(n % 2 + 1) * S], ACT.Copy,
                                         scale=col(POOL_SC + n))
                ins.then_inc(s_yc, 1)
                act.wait_ge(s_yc, l + 1)
                act.activation(sq, ycT, ACT.Square).then_inc(s_sqr, 1)
            if u == POOL_RMS_AT:
                root_of_sums(0)
            if u == MEAN_AT:
                act.wait_ge(s_lna, 3 * l + 1)
                act.activation(sq, acc, ACT.Square).then_inc(s_sqr, 1)
            if u == VAR_AT:
                act.wait_ge(s_rstd, 3 * l + 1)
                root_of_sums(2)
                act.wait_ge(s_lna, 3 * l + 2)
                for n in range(4):
                    ins = act.activation(acc[:, n, :], acc[:, n, :], ACT.Silu, scale=col(LN_G + n), bias=col(LN_B + n))
                ins.then_inc(s_lna, 1)
                act.wait_ge(s_lna, 3 * l + 3)
                act.activation(sq, acc, ACT.Square).then_inc(s_sqr, 1)
            if u == RMS_AT:
                act.wait_ge(s_rstd, 3 * l + 2)
                root_of_sums(3)
            if u in TURN_QK_AT:
                i = TURN_QK_AT.index(u)
                half, dst = i // 2, (qT, kT)[i % 2]
                act.wait_ge(s_qkt, 4 * l + i + 1)
                act.activation(flat(dst[:, 4 * half:4 * half + 4, :]), flat(PS[:, TURN_QK_BANK[i]:TURN_QK_BANK[i] + 2, :]),
                               ACT.Copy).then_inc(s_qk, 1)
            for h in heads_at(SCORES_AT, u):
                act.wait_ge(s_nm, 16 * l + h + 1)
                if h >= 2:
                    act.wait_ge(s_ptr, 16 * l + h - 1)
                for t in range(NT):
                    ins = act.activation(prob[:, h % 2, t * S:(t + 1) * S], neg_s[:, h % 2, t * S:(t + 1) * S], ACT.Exp,
                                         bias=neg_max[:, 2 * (h % 2) + t:2 * (h % 2) + t + 1], scale=-1.0,
                                         accum_out=den[:, 2 * h + t:2 * h + t + 1])
                ins.then_inc(s_p, 1)
            for h in heads_at(TURN_AT, u):
                act.wait_ge(s_ptr, 16 * l + h + 1)
                if h >= 2:
                    act.wait_ge(s_o, 16 * l + h - 1)
                act.activation(probT[:, h % 2, :], PS[:, 6, :], ACT.Copy).then_inc(s_pt, 1)
            for g in [g for g in range(4) if SQUARES_AT[g] == u]:
                act.wait_ge(s_yb, 4 * l + g + 1)
                if g >= 2:
                    act.wait_ge(s_ssb, 8 * l + 2 * g - 2)
                for t in range(NT):
                    at = (2 * (g % 2) + t) * 256
                    act.activation(T3[:, at:at + 256], y_b[:, t, 256 * g:256 * g + 256], ACT.Square,
                                   accum_out=ssb4[:, t, g:g + 1]).then_inc(s_ssb, 1)
                if g == 3:
                    act.wait_ge(s_sbs, l + 1)
                    act.activation(rmsb, ssb, ACT.Sqrt, scale=1.0 / 1024, bias=epsc).then_inc(s_rb, 1)

        def ffn_act(act, splits, evac_low, q, l, ti):
            with act.Fori(0, 11) as j:
                qj = q + 4 * j
                splits(qj, 4, 12)
                evac_low(qj, 7, ti + 2 * j, 0)
                act.wait_ge(s_freeT, ti + 2 * j + 1)
                act.activation(f3(T1), f3(T1), ACT.Silu).then_inc(s_act, 1)
                splits(qj, 12, 20)
                evac_low(qj, 15, ti + 2 * j + 1, 4)
                act.wait_ge(s_h, 11 * l + j + 1)
                act.activation(HT[:, bass.ds(4 * j, 4), 0, :], f3(T3), ACT.Copy).then_inc(s_hh, 1)

        act_chain, dve_chain = [0], [0]

        def mixers2_act(act, u):
            def link(ins):
                act_chain[0] += 1
                ins.then_inc(s_ac, 1)
                act.wait_ge(s_ac, act_chain[0])

            def root_of_sums(k):
                act.wait_ge(s_csum, k)
                act.activation(XL[:, 0, :], PS[:, 6, 0:S], ACT.Sqrt, scale=1.0 / 512, bias=epsc).then_inc(s_crt, 1)

            def high(i0, src, g):
                for i in range(4):
                    act.activation(XT[:, OUT_ORDER2[i0 + i], 0, :], src[:, i, :], ACT.Copy, scale=g(i)).then_inc(s_y2h, 1)

            if u == GATES_SPLIT_AT:
                act.wait_ge(s_w2, 112)
                act.activation(w_ba2[:, :, 0:8], w_ba, ACT.Copy).then_inc(s_wb, 1)
            if u == GATES_MM_AT:
                act.wait_ge(s_ba, 1)
                act.activation(baT, PS[0:16, 7, :], ACT.Copy).then_inc(s_ba, 1)
            if u == GATES_AT:
                act.wait_ge(s_gin, 1)
                link(act.activation(gate_abs, gate_in, ACT.Abs))
                link(act.activation(gate_abs, gate_abs, ACT.Exp, scale=-1.0))
                act.activation(gate_ln, gate_abs, ACT.Ln, bias=onec).then_inc(s_gln, 1)
                act.activation(a_log, a_log, ACT.Exp).then_inc(s_gln, 1)
                act.activation(beta.rearrange("p (t h) -> p t h", t=NT), ba[:, :, 0:4], ACT.Sigmoid).then_inc(s_gln, 1)
            if u == LRU_MIX_AT:
                act.wait_ge(s_lm, 1)
                for k, (dst, b) in enumerate(((lru_r, L_BA), (lru_i, L_BX))):
                    for n in range(4):
                        ins = act.activation(dst[:, n, :], quad(2 + 4 * k)[:, n, :], ACT.Sigmoid, bias=col(b + n))
                    ins.then_inc(s_lg, 1)
            if u == LRU_A_AT:
                act.wait_ge(s_la, 1)
                act.activation(f3(T1), lru_r, ACT.Tanh).then_inc(s_lt, 1)
                act.activation(f3(T2), lru_r, ACT.Exp).then_inc(s_lt, 1)
            if u == LRU_SCAN_AT:
                act.wait_ge(s_lr, 1)
                act.activation(f3(T1), f3(T1), ACT.Sqrt).then_inc(s_lsq, 1)
                act.wait_ge(s_freeN, NB + 2)
                act.activation(lru_gate, lru_gate, ACT.Gelu_apprx_tanh).then_inc(s_lsq, 1)
            if u == LRU_SQ_AT:
                act.wait_ge(s_ly, 1)
                act.activation(f3(T1), lru_xc, ACT.Square).then_inc(s_csq, 1)
                act.dma_start(sgu_lnw, a["sgu_ln_w_2"].to_broadcast((P, 512))).then_inc(s_w2, 16)
                act.dma_start(sgu_lnb, a["sgu_ln_b_2"].to_broadcast((P, 512))).then_inc(s_w2, 16)
                act.dma_start(sgu_ws, a["sgu_ws_2"][0].rearrange("g t s -> t g s")).then_inc(s_w2, 16)
            if u == LRU_RMS_AT:
                root_of_sums(1)
            if u == GCUM_AT:
                act.wait_ge(s_gcm, 1)
                act.activation(gcum, PS[:, 6, 0:8], ACT.Copy).then_inc(s_gcum, 1)
            if u == DECAY_AT:
                act.wait_ge(s_grow, 1)
                act.activation(egrow, pair(2), ACT.Exp).then_inc(s_eg, 1)
            if u == DECAY_T_AT:
                act.wait_ge(s_dd, 1)
                act.activation(dec, dec, ACT.Exp).then_inc(s_de, 1)
            if u == DECAY_EXP_AT:
                act.wait_ge(s_dd, 2)
                act.activation(decT, decT, ACT.Exp).then_inc(s_de, 1)
                act.wait_ge(s_gcum, 1)
                link(act.activation(gbeta, gcum, ACT.Exp))
                act.wait_ge(s_fac, 1)
                act.activation(gtail, gtail, ACT.Exp).then_inc(s_fac2, 1)
            if u in SILU_AT:
                k = SILU_AT.index(u)
                act.wait_ge(s_qc, 16 * (k + 1))
                y = (qh, kh, vh)[k]
                act.activation(y, y, ACT.Silu).then_inc(s_qs, 1)
                if k < 2:
                    act.wait_ge(s_qs, k + 1)
                    act.wait_ge(s_l2m if k else s_cn, 1)
                    act.activation(XL[:, :, :], y, ACT.Square).then_inc(s_l2s, 1)
            if u in L2_AT:
                k = L2_AT.index(u)
                act.wait_ge(s_l2m, k + 1)
                if k:
                    act.wait_ge(s_l2n, 1)
                act.activation(f3(T2), quad(2), ACT.Sqrt, scale=1.0 if k else 128.0, bias=epsc if k else epsc_q).then_inc(s_l2r, 1)
            if u in (K_TURN_AT, V_TURN_AT):
                k = int(u == V_TURN_AT)
                act.wait_ge(s_kv, k + 1)
                act.activation((k_by, v_by)[k], pair(2 + 4 * k), ACT.Copy).then_inc(s_kvb, 1)
            if u == P_TURN_AT:
                act.wait_ge(s_Pt, 1)
                act.activation(PmT, pair(6), ACT.Copy).then_inc(s_pte, 1)
            if u in POWER_AT[:4]:
                r = POWER_AT.index(u)
                if r == 0:
                    act.wait_ge(s_tt, 1)
                act.wait_ge(s_sq, 2 * r + 2)
                act.activation(PmT, pair(6), ACT.Copy).then_inc(s_pte, 1)
            if u in GATED_AT:
                k = GATED_AT.index(u)
                if k == 0:
                    act.wait_ge(s_fac, 2)
                    act.wait_ge(s_qc, 48)
                    act.wait_ge(s_kvb, 2)
                    act.wait_ge(s_l2n, 2)
                    act.wait_ge(s_P, 1)
                dst, src, gate = ((kbg, k_by, gbeta), (v_beta, v_by, beta), (kg, k_by, gtail))[k]
                for m in range(8):
                    ins = act.activation(dst[:, m, :], src[:, m, :], ACT.Copy, scale=gate[:, m:m + 1])
                ins.then_inc(s_kbg, 1)
            if u == Z_AT:
                act.wait_ge(s_freeN, NB + 6)
                act.activation(z, z, ACT.Silu).then_inc(s_zs, 1)
            if u == WU_AT:
                act.wait_ge(s_wu, 1)
                act.activation(wT, pair(2), ACT.Copy).then_inc(s_wue, 1)
            if u in CHUNK_AT:
                n = CHUNK_AT.index(u)
                t, r = n // 2, 64 * (n % 2)
                act.wait_ge(s_os, n + 1)
                act.activation(flat(o_by[r:r + 64, 4 * t:4 * t + 4, :]), PS[r:r + 64, 3, :], ACT.Copy).then_inc(s_oe, 1)
            if u == GDN_SQ_AT:
                act.wait_ge(s_on, 1)
                act.activation(o_rms, o_ss, ACT.Sqrt, scale=1.0 / P, bias=epsc).then_inc(s_on2, 1)
            if u == GDN_TURN_AT:
                act.wait_ge(s_ot, 1)
                link(act.activation(gdn_yT, quad(2), ACT.Copy))
            if u == SGU_GELU_AT:
                act.wait_ge(s_freeN, NB + 7)
                act.activation(sgu_v, sgu_v, ACT.Gelu_apprx_tanh).then_inc(s_gelu, 1)
            if u == SGU_MEAN_AT:
                act.wait_ge(s_gn, 1)
                for t in range(NT):
                    link(act.activation(sqs[:, 2 * t:2 * t + 2, :].rearrange("p a b -> p (a b)"), sgu_v[:, t, :], ACT.Square,
                                        accum_out=vv[:, t:t + 1]))
                act.activation(vs, vv, ACT.Sqrt, scale=1.0 / 512, bias=epsc).then_inc(s_groot, 1)
            if u == SGU_W_AT:
                act.wait_ge(s_wsm, 2)
                act.activation(flat(sgu_wsT), PS[:, 6, :], ACT.Copy).then_inc(s_wst, 1)
            if u == SGU_U_AT:
                act.wait_ge(s_freeN, NB + 8)
                act.activation(sgu_u, sgu_u, ACT.Gelu_apprx_tanh).then_inc(s_gelu, 1)
            if u == SGU_MIX_AT:
                act.wait_ge(s_gy, 1)
                for t in range(NT):
                    link(act.activation(sqs[:, 2 * t:2 * t + 2, :].rearrange("p a b -> p (a b)"), sgu_v[:, t, :], ACT.Square,
                                        accum_out=cs[:, t:t + 1]))
                act.activation(cr, cs, ACT.Sqrt, scale=1.0 / 512, bias=epsc).then_inc(s_groot, 1)
            if u == SGU_TURN_AT:
                act.wait_ge(s_gyt, 2)
                link(act.activation(sgu_yT, quad(6), ACT.Copy))
            if u == SC_OUT_AT:
                act.wait_ge(s_cn, 1)
                high(0, lru_xc, lambda i: col(G2_GRP + i))
                high(4, sgu_yT, lambda i: col(G2_GRP + 4 + i))
                high(8, gdn_yT, lambda i: col(G2_GDN))
            if u == SC_SQ_AT:
                act.wait_ge(s_sy, 1)
                act.activation(sqs, sc_b, ACT.Square).then_inc(s_csq, 1)
            if u == SC_RMS_AT:
                act.wait_ge(s_l2m, 2)
                root_of_sums(2)
            if u == SC_SPLIT_AT:
                act.wait_ge(s_cn, 2)
                high(12, sc_b, lambda i: col(G2_GRP + 8 + i))

        def ffn2_act(act, splits, evac_low, q):
            ti = TB
            splits(q, 4, 7)
            with act.Fori(0, 11) as j:
                qj = q + 4 * j
                for g, dst in ((0, T2), (1, T3)):
                    splits(qj, 7 if g == 0 else 14, 12 + 8 * g)
                    evac_low(qj, 7 + 8 * g, ti + 2 * j + g, 4 * g)
                    act.wait_ge(s_freeT, ti + 2 * j + g + 1)
                    act.wait_ge(s_cj, j + 1)
                    for n in range(4):
                        ins = act.activation(f3(dst)[:, n, :], ffn_pad[:, n, 2:2 + S], ACT.Identity, scale=conv_j[:, 2, g, n:n + 1],
                                             bias=conv_j[:, 3, g, n:n + 1])
                    ins.then_inc(s_tap, 1)
                    splits(qj, 12 + 8 * g, 14 + 9 * g)
                    if g == 0:
                        act.wait_ge(s_fc, 2 * j + 1)
                        act.activation(f3(T2), f3(T2), ACT.Gelu_apprx_tanh).then_inc(s_act, 1)
                act.wait_ge(s_h, 11 * LB + j + 1)
                act.activation(HT[:, bass.ds(4 * j, 4), 0, :], f3(T3), ACT.Copy).then_inc(s_hh, 1)

        @block.scalar
        def _(act):
            def split(q, i):
                act.wait_ge(s_stage[i % RING], 16 * (q + i // RING + 1))
                act.wait_ge(s_pe, 4 * q + i + 1)
                act.activation(WH[:, i % RING, :], WS[:, i % RING, :], ACT.Copy).then_inc(s_hi, 1)

            def splits(q, i0, i1):
                for i in range(i0, i1):
                    split(q, i)

            def product_done(q, i):
                act.wait_ge(s_pe, 4 * q + i + 5)

            def evac_low(q, i, ti, base):
                product_done(q, i)
                act.wait_ge(s_freeT, ti)
                act.activation(XL[:, :, :], PS[:, base:base + 4, S:2 * S], ACT.Copy).then_inc(s_xl, 1)

            def norm_in(n, g, q):
                def root(t):
                    act.wait_ge(s_sst, 2 * n + t + 1)
                    act.activation(rms[:, t:t + 1], ss[:, t:t + 1], ACT.Sqrt, scale=1.0 / D, bias=epsc).then_inc(s_rms, 1)

                def scale_half(t):
                    act.wait_ge(s_rinv, 2 * n + t + 1)
                    act.activation(xs[:, t, 1024:2048], x[:, t, 1024:2048], ACT.Copy, scale=rinv[:, t:t + 1]).then_inc(s_xs2, 1)

                for t in range(NT):
                    for c in range(2):
                        if (t, c) == (1, 1):
                            root(0)
                        act.wait_ge(s_x, 4 * n + 2 * t + c + 1)
                        act.activation(junk[:, t, c * 1024:(c + 1) * 1024], x[:, t, c * 1024:(c + 1) * 1024], ACT.Square,
                                       accum_out=ssp[:, 2 * t + c:2 * t + c + 1]).then_inc(s_ss, 1)
                scale_half(0)
                root(1)
                scale_half(1)
                split(q, 3)
                for kt in range(KT):
                    if kt % 2 == 0:
                        act.wait_ge(s_tr, 8 * n + kt // 2 + 1)
                    act.activation(XT[:, kt, 0, :], PS[:, kt // 2, (kt % 2) * S:(kt % 2 + 1) * S], ACT.Copy,
                                   scale=col(g + kt)).then_inc(s_xh, 1)

            def load_post_weight(gname_row):
                for h in range(2):
                    act.dma_start(gbc[h][:, 0:1024], gname_row[:, h * 1024:(h + 1) * 1024].to_broadcast((P, 1024))).then_inc(s_gb, 16)

            def post_squares(m, c):
                for t in range(NT):
                    if t + c:
                        act.wait_ge(s_sf, 4 * m + 2 * c + t)
                    act.activation(XL[:, :, :].rearrange("p a b -> p (a b)"),
                                   PS[:, 4 * c + 2 * t:4 * c + 2 * t + 2, :].rearrange("p a b -> p (a b)"), ACT.Square,
                                   accum_out=ssf[:, 2 * c + t:2 * c + t + 1]).then_inc(s_sf, 1)

            def post_root(m):
                act.wait_ge(s_sfs, m + 1)
                act.activation(rmsf, ssf2, ACT.Sqrt, scale=1.0 / D, bias=epsc).then_inc(s_rf, 1)

            def y_high(kt, src, g):
                act.activation(XT[:, kt, 0, :], src, ACT.Copy, scale=g).then_inc(s_yh, 1)

            def wide_phase(q, m, n_units, first=4, last=False):
                for c in range(2):
                    splits(q, n_units * c + (4 if c else first), n_units * (c + 1) + (4, 0 if last else 3)[c])
                    product_done(q, n_units * c + n_units - 1)
                    post_squares(m, c)
                post_root(m)

            act.wait_ge(s_eps, 2)
            act.wait_ge(s_const, 16)
            splits(0, 0, 3)
            with act.Fori(0, DEPTH) as l:
                q = l * (U_LAYER // 4)
                act.wait_ge(s_prt, 2 * l + 2)
                act.activation(PR[:, 0:64], PS[:, 0, 0:64], ACT.Copy).then_inc(s_par, 1)
                act.activation(PR[:, 64:64 + P], PS[:, 0, P:2 * P], ACT.Copy).then_inc(s_par, 1)
                act.wait_ge(s_par, 2 * l + 2)
                norm_in(2 * l, G_PRE, q)
                act.dma_start(KC, a["key_constants"]).then_inc(s_kc, 16)
                act.dma_start(pw, a["pool_w"][l].rearrange("g c d -> c g d")).then_inc(s_kc, 16)
                ti, ni = l * T_LAYER, l * N_IN1
                for c in range(9):
                    for i in range(8):
                        split(q, 8 * c + 4 + i)
                        if i < 7:
                            mixers_act(act, l, 8 * c + i)
                    if c < 3:
                        evac_low(q, 8 * c + 7, ti + c, 4 * (c % 2))
                        if c == 1:
                            act.wait_ge(s_freeT, ti + 2)
                            act.activation(f3(T1), gT, ACT.Sigmoid).then_inc(s_sg, 1)
                    else:
                        n = c - 3
                        base = 4 * (c % 2)
                        dst = (q_nat, k_nat, v_nat)[n % 3]
                        half = n // 3
                        product_done(q, 8 * c + 7)
                        for t in range(NT):
                            ins = act.activation(dst[:, t, half * 512:(half + 1) * 512], PS[:, base + t, :], ACT.Copy,
                                                 scale=0.125 if n % 3 == 0 else 1.0)
                        ins.then_inc(s_freeN, 1)
                    if c == 3:
                        act.wait_ge(s_glu, l + 1)
                        load_post_weight(a["g_post_mix"][bass.ds(l, 1)])
                    if c == 8:
                        for i in range(8):
                            kt = OUT_ORDER[i]
                            act.wait_ge(s_ya if i < 4 else s_ycn, l + 1)
                            y_high(kt, (acc if i < 4 else ycT)[:, i % 4, :], col(G_MIX + kt))
                    mixers_act(act, l, 8 * c + 7)
                for u in range(U_IN1, U_IN1 + 8):
                    if u == SQUARES_AT[3]:
                        mixers_act(act, l, u)
                    split(q, u + RING)
                    if u != SQUARES_AT[3]:
                        mixers_act(act, l, u)
                for i in range(8):
                    if i % 2 == 0:
                        act.wait_ge(s_ybt, 4 * l + i // 2 + 1)
                    y_high(4 + i, PS[:, 4 + i // 2, (i % 2) * S:(i % 2 + 1) * S], col(G_MIX + 4 + i))
                wide_phase(q + U_IN1 // 4, 2 * l, KT, 12)
                norm_in(2 * l + 1, G_FFN, q + (U_IN1 + U_OUT) // 4)
                ffn_act(act, splits, evac_low, q + (U_IN1 + U_OUT) // 4, l, ti + T_IN1)
                act.wait_ge(s_h, 11 * l + 11)
                load_post_weight(a["g_post_ffn"][bass.ds(l, 1)])
                wide_phase(q + (U_IN1 + U_OUT + U_UP) // 4, 2 * l + 1, FKT)

            a2 = lambda n: a[n + "_2"][0]
            act.wait_ge(s_prt2, 5)
            for r, (at, n) in enumerate(((0, 93), (GDN_CW, 48), (F_CW, 128), (F_CW + 128, 128), (F_CW + 256, 96))):
                act.activation(PR[:, at:at + n], PS[:, r // 4, (r % 4) * P:(r % 4) * P + n], ACT.Copy).then_inc(s_par2, 1)
            act.wait_ge(s_par2, 5)
            norm_in(2 * LB, G2_PRE, DEPTH * (U_LAYER // 4))
            act.dma_start(w_ba, a2("w_in")[:, BA:BA + 8].rearrange("(k p) n -> p k n", p=P)).then_inc(s_w2, 16)
            act.dma_start(a_log, a["gdn_a_log_2"].to_broadcast((P, 4))).then_inc(s_w2, 16)
            act.dma_start(dt_bias, a["gdn_dt_bias_2"].to_broadcast((P, 4))).then_inc(s_w2, 16)
            act.wait_ge(s_bd, 2)
            for w, bd in (("lru_wa", wa_bd), ("lru_wx", wx_bd)):
                m = a2(w).rearrange("(n b) i j -> b i n j", b=2)
                for b in range(2):
                    act.dma_start(bd[64 * b:64 * b + 64, :, 64 * b:64 * b + 64], m[b]).then_inc(s_w2, 16)
            q = DEPTH * (U_LAYER // 4)
            dst2 = dict(lru_x=lru_pad[:, :, 3:3 + S], lru_gate=lru_gate, q=qkv_pad[:, 0:4, 3:3 + S], k=qkv_pad[:, 4:8, 3:3 + S],
                        v=qkv_pad[:, 8:12, 3:3 + S], z=z, sgu_v=sgu_v, sgu_u=sgu_u, sc_c=sc_c, sc_h=sc_pad[:, :, 2:2 + S], sc_b=sc_b)
            for c, name in enumerate(IN2):
                for i in range(8):
                    split(q, 8 * c + i + RING)
                    if i < 7:
                        mixers2_act(act, 8 * c + i)
                product_done(q, 8 * c + 7)
                base = 4 * (c % 2)
                act.activation(dst2[name], PS[:, base:base + 2, :] if name in BY_TOKEN2 else quad(base), ACT.Copy).then_inc(s_freeN, 1)
                mixers2_act(act, 8 * c + 7)
            for u in range(U_IN2, U_IN2 + 8):
                split(q, u + RING)
                mixers2_act(act, u)
            q += U_IN2 // 4
            load_post_weight(a["post_mix_norm_2"])
            wide_phase(q, 2 * LB, KT, 12)
            norm_in(2 * LB + 1, G2_FFN, q + U_OUT // 4)
            q += U_OUT // 4
            ffn2_act(act, splits, evac_low, q)
            act.wait_ge(s_h, 11 * LB + 11)
            load_post_weight(a["post_ffn_norm_2"])
            q += U_UP // 4
            wide_phase(q, 2 * LB + 1, FKT, 7, last=True)

        def mixers_dve(dve, l, u):
            def scale_by_root(k, y, signal):
                dve.wait_ge(s_std, 3 * l + k + 1)
                dve.reciprocal(XL[:, 1, :], XL[:, 0, :]).then_inc(s_rstd, 1)
                dve.wait_ge(s_rstd, 3 * l + k + 1)
                dve.tensor_tensor(y, y, XL[:, 1:2, :].to_broadcast((P, 4, S)), ALU.mult).then_inc(signal, 1)

            for h in heads_at(SCORES_AT, u):
                if h == 0:
                    dve.wait_ge(s_kc, 32 * (l + 1))
                dve.wait_ge(s_S, 16 * l + h + 1)
                if h >= 2:
                    dve.wait_ge(s_p, 16 * l + h - 1)
                dve.scalar_tensor_tensor(out=neg_s[:, h % 2, :], in0=PS[:, score_bank(h), :], scalar=-1.0,
                                         in1=KC[:, K_BIAS:K_BIAS + 2 * S], op0=ALU.mult, op1=ALU.subtract).then_inc(s_sb, 1)
                dve.wait_ge(s_sb, 16 * l + h + 1)
                dve.tensor_reduce(neg_max[:, 2 * (h % 2):2 * (h % 2) + 2],
                                  neg_s[:, h % 2, :].rearrange("p (t k) -> p t k", t=NT), AX, ALU.min).then_inc(s_nm, 1)
            for h in heads_at(OUTPUT_AT, u):
                if h % 4 == 3:
                    g = h // 4
                    dve.wait_ge(s_o, 16 * l + h + 1)
                    dve.reciprocal(rden[:, 8 * g:8 * g + 8], den[:, 8 * g:8 * g + 8]).then_inc(s_rd, 1)
                    dve.wait_ge(s_rd, 4 * l + g + 1)
                    o = PS[:, 7, :].rearrange("p (h t e) -> p h t e", h=4, t=NT)
                    r = rden[:, 8 * g:8 * g + 8].rearrange("p (h t) -> p h t", t=NT)
                    dst = y_b[:, :, 256 * g:256 * g + 256].rearrange("p t (h e) -> p h t e", e=64)
                    dve.tensor_tensor(dst, o, r[:, :, :, None].to_broadcast((P, 4, NT, 64)), ALU.mult).then_inc(s_yb, 1)
            if u == POOL_RMS_AT:
                scale_by_root(0, ycT, s_ycn)
            if u == MEAN_AT:
                dve.wait_ge(s_cv, 4 * TAPS * (l + 1))
                dve.wait_ge(s_col, 4 * l + 2)
                for n in range(4):
                    ins = dve.scalar_tensor_tensor(out=acc[:, n, :], in0=PS[:, 3, 0:S], scalar=-1.0 / 512, in1=acc[:, n, :],
                                                   op0=ALU.mult, op1=ALU.add)
                ins.then_inc(s_lna, 1)
            if u == VAR_AT:
                dve.wait_ge(s_lna, 3 * l + 1)
                scale_by_root(1, acc, s_lna)
            if u == RMS_AT:
                scale_by_root(2, acc, s_ya)
            if u == SQUARES_AT[3]:
                dve.wait_ge(s_ssb, 8 * l + 8)
                dve.tensor_reduce(ssb, ssb4, AX, ALU.add).then_inc(s_sbs, 1)
                dve.wait_ge(s_rb, l + 1)
                dve.reciprocal(rinvb, rmsb).then_inc(s_rbi, 1)
                dve.wait_ge(s_rbi, l + 1)
                for t in range(NT):
                    dve.tensor_scalar(yb_n[:, t, :], y_b[:, t, :], rinvb[:, t:t + 1], None, ALU.mult).then_inc(s_ybn, 1)

        def ffn_dve(dve, splits, evac, q, l, ti):
            with dve.Fori(0, 11) as j:
                qj = q + 4 * j
                splits(qj, 4, 12)
                evac(ti + 2 * j, 0, f3(T1))
                splits(qj, 12, 20)
                evac(ti + 2 * j + 1, 4, f3(T2))
                dve.wait_ge(s_act, 11 * l + j + 1)
                dve.wait_ge(s_freeT, ti + 2 * j + 2)
                dve.tensor_tensor(f3(T3), f3(T1), f3(T2), ALU.mult).then_inc(s_h, 1)
                dve.wait_ge(s_hh, 11 * l + j + 1)
                dve.tensor_tensor(HT[:, bass.ds(4 * j, 4), 1, :], f3(T3), HT[:, bass.ds(4 * j, 4), 0, :].bitcast(F32),
                                  ALU.subtract).then_inc(s_ht, 1)

        def causal_taps(dve, dst, pad, tile0, tiles, w0, b0, signal, done, i0, i1):
            for i in range(i0, i1):
                j, tile = i // 4, tile0 + i % 4
                w = col(w0 + tiles * j + tile)
                if j == 0:
                    if b0 is None:
                        ins = dve.tensor_scalar(dst[:, tile, :], pad[:, tile, 0:S], w, None, ALU.mult)
                    else:
                        ins = dve.tensor_scalar(dst[:, tile, :], pad[:, tile, 0:S], w, col(b0 + tile), ALU.mult, ALU.add)
                else:
                    dve.wait_ge(signal, done + i - 3)
                    ins = dve.scalar_tensor_tensor(out=dst[:, tile, :], in0=pad[:, tile, j:j + S], scalar=w,
                                                   in1=dst[:, tile, :], op0=ALU.mult, op1=ALU.add)
                ins.then_inc(signal, 1)

        def mixers2_dve(dve, u):
            def link(ins):
                dve_chain[0] += 1
                ins.then_inc(s_dc, 1)
                dve.wait_ge(s_dc, dve_chain[0])

            def over_root(k, y, signal):
                dve.wait_ge(s_crt, k)
                link(dve.reciprocal(XL[:, 1, :], XL[:, 0, :]))
                dve.tensor_tensor(y, y, XL[:, 1:2, :].to_broadcast((P, 4, S)), ALU.mult).then_inc(signal, 1)

            def low(i0, src, g):
                for i in range(4):
                    kt = OUT_ORDER2[i0 + i]
                    dve.wait_ge(s_y2h, i0 + i + 1)
                    dve.scalar_tensor_tensor(out=XT[:, kt, 1, :], in0=src[:, i, :], scalar=g(i),
                                             in1=XT[:, kt, 0, :].bitcast(F32), op0=ALU.mult, op1=ALU.subtract).then_inc(s_y2t, 1)

            if u == GATES_SPLIT_AT:
                dve.wait_ge(s_wb, 1)
                dve.tensor_tensor(w_ba2[:, :, 8:16], w_ba, w_ba2[:, :, 0:8].bitcast(F32), ALU.subtract).then_inc(s_wbl, 1)
            if u == GATES_AT:
                dve.wait_ge(s_ba, 3)
                link(dve.tensor_reduce(ba, PS[:, 6, 0:64].rearrange("p (t k n) -> p t n k", t=NT, k=4), AX, ALU.add))
                link(dve.tensor_tensor(gate_in[:, 0:8].rearrange("p (t h) -> p t h", t=NT), ba[:, :, 4:8],
                                       dt_bias[:, None, :].to_broadcast((P, NT, 4)), ALU.add))
                dve.tensor_scalar(gate_in[:, 8:12], PR[:, L_LAM:L_LAM + 4], -1.0, None, ALU.mult).then_inc(s_gin, 1)
                dve.wait_ge(s_gin, 1)
                dve.wait_ge(s_gln, 3)
                link(dve.tensor_scalar(gate_in, gate_in, 0.0, None, ALU.max))
                link(dve.tensor_tensor(gate_in, gate_in, gate_ln, ALU.add))
                link(dve.tensor_scalar(rate, gate_in[:, 8:12], -8.0, None, ALU.mult))
                dve.scalar_tensor_tensor(out=g_tok.rearrange("p (t h) -> p t h", t=NT),
                                         in0=gate_in[:, 0:8].rearrange("p (t h) -> p t h", t=NT), scalar=-1.0,
                                         in1=a_log[:, None, :].to_broadcast((P, NT, 4)), op0=ALU.mult, op1=ALU.mult).then_inc(s_g, 1)
                dve.tensor_scalar(nbeta, beta, -1.0, None, ALU.mult).then_inc(s_g, 1)
            if LRU_CONV_AT <= u < LRU_CONV_AT + 4:
                k = u - LRU_CONV_AT
                dve.wait_ge(s_freeN, NB + 1)
                causal_taps(dve, lru_xc, lru_pad, 0, 4, L_CW, L_CB, s_lc, 0, 4 * k, 4 * k + 4)
            if u == LRU_MIX_AT:
                dve.wait_ge(s_lg, 2)
                for n in range(4):
                    ins = dve.tensor_scalar(lru_r[:, n, :], lru_r[:, n, :], rate[:, n:n + 1], None, ALU.mult)
                ins.then_inc(s_la, 1)
                link(dve.tensor_tensor(lru_i, lru_i, lru_xc, ALU.mult))
            if u == LRU_A_AT:
                dve.wait_ge(s_lt, 2)
                link(dve.tensor_scalar(lru_r, f3(T1), -1.0, 1.0, ALU.mult, ALU.add))
                link(dve.reciprocal(lru_r, lru_r))
                dve.scalar_tensor_tensor(out=f3(T1), in0=f3(T1), scalar=-2.0, in1=lru_r, op0=ALU.mult, op1=ALU.mult).then_inc(s_lr, 1)
            if u == LRU_SCAN_AT:
                dve.wait_ge(s_lsq, 1)
                link(dve.tensor_tensor(lru_i, lru_i, f3(T1), ALU.mult))
                for n in range(4):
                    ins = dve.tensor_tensor_scan(lru_xc[:, n, :], f3(T2)[:, n, :], lru_i[:, n, :], 0.0, ALU.mult, ALU.add)
                link(ins)
                dve.wait_ge(s_lsq, 2)
                dve.tensor_tensor(lru_xc, lru_xc, lru_gate, ALU.mult).then_inc(s_ly, 1)
            if u == LRU_RMS_AT:
                over_root(1, lru_xc, s_cn)
            if u in (DECAY_AT, DECAY_T_AT):
                k = int(u == DECAY_T_AT)
                d, at = ((dec, C_STRICT), (decT, C_CAUSAL_T))[k]
                dve.wait_ge(s_gcum, 1)
                dve.wait_ge(s_eg, 1)
                for m in range(8):
                    if k == 0:
                        ins = dve.tensor_scalar(d[:, m, :], pair(2)[:, m, :], -1.0, gcum[:, m:m + 1], ALU.mult, ALU.add)
                    else:
                        ins = dve.tensor_scalar(d[:, m, :], pair(2)[:, m, :], gcum[:, m:m + 1], None, ALU.subtract)
                link(ins)
                dve.tensor_tensor(d, d, mask(at), ALU.mult).then_inc(s_dd, 1)
                if k:
                    for r in (0, 64):
                        ins = dve.tensor_tensor(gtail[r:r + 64, :], pair(2)[r:r + 64, :, r + 63], gcum[r:r + 64, :], ALU.subtract)
                    ins.then_inc(s_fac, 1)
            if u == DECAY_MASK_AT:
                for k, (d, at) in enumerate(((dec, C_STRICT), (decT, C_CAUSAL_T))):
                    dve.wait_ge(s_de, k + 1)
                    dve.tensor_tensor(d, d, mask(at), ALU.mult).then_inc(s_dm, 1)
                dve.wait_ge(s_fac2, 1)
                dve.tensor_tensor(gbeta, gbeta, beta, ALU.mult).then_inc(s_fac, 1)
            for g in range(3):
                k = u - CONV_AT[g]
                if 0 <= k < 4:
                    dve.wait_ge(s_freeN, NB + 3 + g)
                    causal_taps(dve, qkvT, qkv_pad, 4 * g, 12, GDN_CW, None, s_qc, 16 * g, 4 * k, 4 * k + 4)
            if u in L2_AT:
                k = L2_AT.index(u)
                y = (qh, kh)[k]
                dve.wait_ge(s_l2r, k + 1)
                link(dve.reciprocal(f3(T2), f3(T2)))
                dve.tensor_tensor(y, y, f3(T2), ALU.mult).then_inc(s_l2n, 1)
            if u == KK_AT:
                dve.wait_ge(s_dm, 1)
                dve.wait_ge(s_g, 2)
                dve.wait_ge(s_kk, 1)
                for m in range(8):
                    ins = dve.scalar_tensor_tensor(out=Pm[:, m, :], in0=pair(6)[:, m, :], scalar=nbeta[:, m:m + 1],
                                                   in1=dec[:, m, :], op0=ALU.mult, op1=ALU.mult)
                ins.then_inc(s_P, 1)
            if u == KQ_AT:
                dve.wait_ge(s_kk, 2)
                dve.wait_ge(s_dm, 2)
                dve.tensor_tensor(decT, pair(2), decT, ALU.mult).then_inc(s_att, 1)
            if u == P_TURN_AT:
                dve.wait_ge(s_pte, 1)
                dve.tensor_tensor(Tt, PmT, mask(C_ID), ALU.add).then_inc(s_tt, 1)
            if u in POWER_AT:
                r = POWER_AT.index(u)
                dve.wait_ge(s_sq, min(2 * r + 2, 9))
                dve.tensor_copy(Pm, pair(2)).then_inc(s_P, 1)
            if u in PRODUCT_AT:
                r = PRODUCT_AT.index(u)
                dve.wait_ge(s_te, r + 1)
                dve.wait_ge(s_tt, r + 1)
                dve.tensor_tensor(Tt, Tt, pair(2), ALU.add).then_inc(s_tt, 1)
            if u == WU_AT:
                dve.wait_ge(s_wu, 2)
                dve.tensor_copy(u_by, pair(6)).then_inc(s_wue2, 1)
                dve.tensor_tensor(qh.rearrange("p h (t c) -> p t h c", t=NT), qh.rearrange("p h (t c) -> p t h c", t=NT),
                                  egrow.rearrange("p (t h) c -> p t h c", t=NT), ALU.mult).then_inc(s_qg, 1)
            for n in range(4):
                t, r = n // 2, 64 * (n % 2)
                if n and u == STATE_AT[n]:
                    v = flat(u_by[r:r + 64, 4 * t:4 * t + 4, :])
                    dve.wait_ge(s_vn, n)
                    dve.tensor_tensor(v, v, PS[r:r + 64, 2, :], ALU.subtract).then_inc(s_vne, 1)
                if n < 3 and u == CHUNK_AT[n]:
                    dve.wait_ge(s_ks, n + 1)
                    if n:
                        dve.wait_ge(s_os, n + 1)
                        dve.wait_ge(s_st, n)
                    for h in range(4):
                        if n == 0:
                            ins = dve.tensor_copy(state[:, h, :], PS[:, 6, h * P:(h + 1) * P])
                        else:
                            m = 4 * t + h
                            ins = dve.scalar_tensor_tensor(out=state[:, h, :], in0=state[:, h, :],
                                                           scalar=egrow[:, m, r + 63:r + 64], in1=PS[:, 6, h * P:(h + 1) * P],
                                                           op0=ALU.mult, op1=ALU.add)
                    ins.then_inc(s_st, 1)
            if u == GDN_SQ_AT:
                dve.wait_ge(s_oe, 4)
                link(dve.tensor_tensor(k_sq, o_by, o_by, ALU.mult))
                dve.tensor_reduce(o_ss, k_sq, AX, ALU.add).then_inc(s_on, 1)
            if u == GDN_RMS_AT:
                dve.wait_ge(s_on2, 1)
                link(dve.reciprocal(o_rinv, o_rms))
                link(dve.tensor_tensor(o_by, o_by, eight(o_rinv), ALU.mult))
                dve.wait_ge(s_zs, 1)
                dve.tensor_tensor(o_by, o_by, z.rearrange("p t (h c) -> p (t h) c", c=P), ALU.mult).then_inc(s_oz, 1)
            if u == SGU_MEAN_AT:
                dve.wait_ge(s_gelu, 1)
                link(dve.tensor_reduce(vm, sgu_v, AX, ALU.add))
                link(dve.tensor_scalar(vm, vm, -1.0 / 512, None, ALU.mult))
                for t in range(NT):
                    ins = dve.tensor_scalar(sgu_v[:, t, :], sgu_v[:, t, :], vm[:, t:t + 1], None, ALU.add)
                ins.then_inc(s_gn, 1)
            if u == SGU_NORM_AT:
                dve.wait_ge(s_w2, 160)
                dve.tensor_tensor(sgu_ws, sgu_ws, C[:, C_TRIL:C_TRIL + P][:, None, :].to_broadcast((P, 4, P)),
                                  ALU.mult).then_inc(s_wsm, 1)
                dve.wait_ge(s_groot, 1)
                link(dve.reciprocal(vr, vs))
                for t in range(NT):
                    ins = dve.scalar_tensor_tensor(out=sgu_v[:, t, :], in0=sgu_v[:, t, :], scalar=vr[:, t:t + 1], in1=sgu_lnw,
                                                   op0=ALU.mult, op1=ALU.mult)
                link(ins)
                dve.tensor_tensor(sgu_v, sgu_v, sgu_lnb[:, None, :].to_broadcast((P, NT, 512)), ALU.add).then_inc(s_gvn, 1)
            if u == SGU_MIX_AT:
                dve.wait_ge(s_gm, 1)
                dve.wait_ge(s_gelu, 2)
                for t in range(NT):
                    for g in range(4):
                        ins = dve.scalar_tensor_tensor(out=sgu_v[:, t, g * P:(g + 1) * P], in0=PS[:, 6 + t, g * P:(g + 1) * P],
                                                       scalar=col(SGU_B + g), in1=sgu_u[:, t, g * P:(g + 1) * P],
                                                       op0=ALU.add, op1=ALU.mult)
                ins.then_inc(s_gy, 1)
            if u == SGU_RMS_AT:
                dve.wait_ge(s_groot, 2)
                link(dve.reciprocal(ci, cr))
                for t in range(NT):
                    dve.tensor_scalar(sgu_v[:, t, :], sgu_v[:, t, :], ci[:, t:t + 1], None, ALU.mult).then_inc(s_gyn, 1)
            if u == SC_MUL_AT:
                dve.wait_ge(s_freeN, NB + 10)
                link(dve.tensor_tensor(sc_pad[:, :, 2:2 + S], sc_pad[:, :, 2:2 + S], sc_c, ALU.mult))
            if SC_CONV_AT <= u < SC_CONV_AT + 3:
                k = u - SC_CONV_AT
                causal_taps(dve, sc_c, sc_pad, 0, 4, S_CW, None, s_scv, 0, 4 * k, 4 * k + 4)
            if u == SC_OUT_AT:
                low(0, lru_xc, lambda i: col(G2_GRP + i))
                dve.wait_ge(s_freeN, NB + 11)
                dve.wait_ge(s_scv, 12)
                dve.tensor_tensor(sc_b, sc_b, sc_c, ALU.mult).then_inc(s_sy, 1)
                low(4, sgu_yT, lambda i: col(G2_GRP + 4 + i))
                low(8, gdn_yT, lambda i: col(G2_GDN))
            if u == SC_RMS_AT:
                over_root(2, sc_b, s_cn)
            if u == SC_SPLIT_AT:
                low(12, sc_b, lambda i: col(G2_GRP + 8 + i))

        def ffn2_dve(dve, split, splits, evac, q):
            ti = TB
            dve.memset(ffn_pad[:, :, 0:2], 0.0)
            splits(q, 4, 7)
            with dve.Fori(0, 11) as j:
                qj = q + 4 * j
                for g, dst in ((0, T2), (1, T3)):
                    splits(qj, 7 if g == 0 else 14, 12 + 8 * g)
                    if g == 0:
                        for k in range(4):
                            for half in range(2):
                                ins = dve.tensor_copy(conv_j[:, k, half, :], PR[:, bass.ds(4 * j + (F_CW + 88 * k + 44 * half), 4)])
                        ins.then_inc(s_cj, 1)
                    evac(ti + 2 * j + g, 4 * g, ffn_pad[:, :, 2:2 + S])
                    dve.wait_ge(s_tap, 2 * j + g + 1)
                    for k in range(2):
                        if k:
                            dve.wait_ge(s_scv, 12 + 2 * j + g + 1)
                        for n in range(4):
                            ins = dve.scalar_tensor_tensor(out=f3(dst)[:, n, :], in0=ffn_pad[:, n, k:k + S],
                                                           scalar=conv_j[:, k, g, n:n + 1], in1=f3(dst)[:, n, :],
                                                           op0=ALU.mult, op1=ALU.add)
                        ins.then_inc(s_fc if k else s_scv, 1)
                        splits(qj, 12 + 8 * g + k, 13 + 8 * g + k)
                dve.wait_ge(s_act, 11 * LB + j + 1)
                dve.wait_ge(s_fc, 2 * j + 2)
                dve.tensor_tensor(f3(T3), f3(T3), f3(T2), ALU.mult).then_inc(s_h, 1)
                split(qj, 22)
                dve.wait_ge(s_hh, 11 * LB + j + 1)
                dve.tensor_tensor(HT[:, bass.ds(4 * j, 4), 1, :], f3(T3), HT[:, bass.ds(4 * j, 4), 0, :].bitcast(F32),
                                  ALU.subtract).then_inc(s_ht, 1)

        @block.vector
        def _(dve):
            def split(q, i):
                dve.wait_ge(s_hi, 4 * q + i + 1)
                dve.tensor_tensor(WL[:, i % RING, :], WS[:, i % RING, :], WH[:, i % RING, :].bitcast(F32),
                                  ALU.subtract).then_inc(s_lo, 1)

            def splits(q, i0, i1):
                for i in range(i0, i1):
                    split(q, i)

            def evac(ti, base, dst):
                dve.wait_ge(s_xl, ti + 1)
                dve.tensor_tensor(dst, PS[:, base:base + 4, 0:S], XL[:, :, :], ALU.add).then_inc(s_freeT, 1)

            def norm_in(n, g, q):
                for t in range(NT):
                    dve.wait_ge(s_ss, 4 * n + 2 * t + 2)
                    dve.tensor_tensor(ss[:, t:t + 1], ssp[:, 2 * t:2 * t + 1], ssp[:, 2 * t + 1:2 * t + 2], ALU.add).then_inc(s_sst, 1)
                    dve.wait_ge(s_rms, 2 * n + t + 1)
                    dve.reciprocal(rinv[:, t:t + 1], rms[:, t:t + 1]).then_inc(s_rinv, 1)
                    dve.wait_ge(s_rinv, 2 * n + t + 1)
                    dve.tensor_scalar(xs[:, t, 0:1024], x[:, t, 0:1024], rinv[:, t:t + 1], None, ALU.mult).then_inc(s_xs, 1)
                split(q, 3)
                for kt in range(KT):
                    dve.wait_ge(s_xh, 16 * n + 2 * (kt // 2) + 2)
                    dve.scalar_tensor_tensor(out=XT[:, kt, 1, :], in0=PS[:, kt // 2, (kt % 2) * S:(kt % 2 + 1) * S],
                                             scalar=col(g + kt), in1=XT[:, kt, 0, :].bitcast(F32), op0=ALU.mult,
                                             op1=ALU.subtract).then_inc(s_xt, 1)

            def post_weighted(down, m, c):
                tmp = post_tmp(down)
                dve.wait_ge(s_gb, 32 * (m + 1))
                for t in range(NT):
                    dve.wait_ge(s_sf, 4 * m + 2 * c + t + 1)
                    dve.tensor_tensor(tmp[:, c, t, :], flat(PS[:, 4 * c + 2 * t:4 * c + 2 * t + 2, :]), gbc[c][:, 0:1024],
                                      ALU.mult).then_inc(s_pn, 1)

            def post(down, m):
                tmp = post_tmp(down)
                dve.wait_ge(s_sf, 4 * m + 4)
                dve.tensor_tensor(ssf2, ssf[:, 0:2], ssf[:, 2:4], ALU.add).then_inc(s_sfs, 1)
                post_weighted(down, m, 1)
                dve.wait_ge(s_rf, m + 1)
                dve.reciprocal(rinvf, rmsf).then_inc(s_rfi, 1)
                dve.wait_ge(s_rfi, m + 1)
                dve.wait_ge(s_pn, 4 * m + 4)
                for t in range(NT):
                    for c in range(2):
                        v = x[:, t, c * 1024:(c + 1) * 1024]
                        dve.scalar_tensor_tensor(out=v, in0=tmp[:, c, t, :], scalar=rinvf[:, t:t + 1], in1=v,
                                                 op0=ALU.mult, op1=ALU.add).then_inc(s_x, 1)

            def conv(l, i0, i1):
                for i in range(i0, i1):
                    j, n = divmod(i, 4)
                    if i == 0:
                        dve.wait_ge(s_glu, l + 1)
                    if j:
                        dve.wait_ge(s_cv, 4 * TAPS * l + i - 3)
                    w = col(CONV_W + 4 * j + n)
                    if j == 0:
                        dve.tensor_scalar(acc[:, n, :], hpad[:, n, 0:S], w, col(CONV_B + n), ALU.mult, ALU.add).then_inc(s_cv, 1)
                    else:
                        dve.scalar_tensor_tensor(out=acc[:, n, :], in0=hpad[:, n, j:j + S], scalar=w, in1=acc[:, n, :],
                                                 op0=ALU.mult, op1=ALU.add).then_inc(s_cv, 1)

            dve.memset(ROWS[:, :, :], 0.0).then_inc(s_eps, 1)
            dve.memset(epsc, EPS).then_inc(s_eps, 1)
            dve.sem_inc(s_lo, 4)
            dve.wait_ge(s_xload, 32)
            dve.sem_inc(s_x, 4)
            splits(0, 0, 3)
            with dve.Fori(0, DEPTH) as l:
                q = l * (U_LAYER // 4)
                dve.wait_ge(s_par, 2 * l + 2)
                norm_in(2 * l, G_PRE, q)
                ti = l * T_LAYER
                for v in (hpad[:, :, 0:15], hpad[:, :, 15 + S:HP], upad[:, :, 0:8], upad[:, :, 8 + S:UP]):
                    ins = dve.memset(v, 0.0)
                ins.then_inc(s_pad, 1)
                for c in range(9):
                    for i in range(8):
                        u = 8 * c + i
                        if i < 7:
                            mixers_dve(dve, l, u)
                        split(q, u + RING)
                        if u >= CONV_FROM:
                            conv(l, 3 * (u - CONV_FROM), min(3 * (u + 1 - CONV_FROM), 4 * TAPS))
                    if c < 3:
                        evac(ti + c, 4 * (c % 2), (aT, gT, upad[:, :, 8:8 + S])[c])
                    if c == 1:
                        dve.wait_ge(s_sg, l + 1)
                        dve.wait_ge(s_freeT, ti + 1)
                        dve.tensor_tensor(hpad[:, :, 15:15 + S], aT, f3(T1), ALU.mult).then_inc(s_glu, 1)
                    if c == 8:
                        for i in range(8):
                            kt = OUT_ORDER[i]
                            dve.wait_ge(s_yh, 16 * l + i + 1)
                            dve.scalar_tensor_tensor(out=XT[:, kt, 1, :], in0=(acc if i < 4 else ycT)[:, i % 4, :],
                                                     scalar=col(G_MIX + kt), in1=XT[:, kt, 0, :].bitcast(F32), op0=ALU.mult,
                                                     op1=ALU.subtract).then_inc(s_yt, 1)
                    mixers_dve(dve, l, 8 * c + 7)
                for u in range(U_IN1, U_IN1 + 8):
                    mixers_dve(dve, l, u)
                    split(q, u + RING)
                for i in range(8):
                    kt = 4 + i
                    dve.wait_ge(s_yh, 16 * l + 8 + 2 * (i // 2) + 2)
                    dve.scalar_tensor_tensor(out=XT[:, kt, 1, :], in0=PS[:, 4 + i // 2, (i % 2) * S:(i % 2 + 1) * S],
                                             scalar=col(G_MIX + kt), in1=XT[:, kt, 0, :].bitcast(F32), op0=ALU.mult,
                                             op1=ALU.subtract).then_inc(s_yt, 1)
                splits(q + U_IN1 // 4, 12, KT + 4)
                post_weighted(False, 2 * l, 0)
                splits(q + U_IN1 // 4, KT + 4, U_OUT + 3)
                post(False, 2 * l)
                norm_in(2 * l + 1, G_FFN, q + (U_IN1 + U_OUT) // 4)
                ffn_dve(dve, splits, evac, q + (U_IN1 + U_OUT) // 4, l, ti + T_IN1)
                q3 = q + (U_IN1 + U_OUT + U_UP) // 4
                splits(q3, 4, FKT + 4)
                post_weighted(True, 2 * l + 1, 0)
                splits(q3, FKT + 4, U_DOWN + 3)
                post(True, 2 * l + 1)

            dve.wait_ge(s_par2, 5)
            norm_in(2 * LB, G2_PRE, DEPTH * (U_LAYER // 4))
            dve.memset(wa_bd, 0.0).then_inc(s_bd, 1)
            dve.memset(wx_bd, 0.0).then_inc(s_bd, 1)
            dve.memset(epsc_q, 128 * EPS)
            dve.memset(onec, 1.0)
            for v in (qkv_pad[:, :, 0:3], sc_pad[:, :, 0:2], lru_pad[:, :, 0:3]):
                dve.memset(v, 0.0)
            q = DEPTH * (U_LAYER // 4)
            for u in range(U_IN2 + 8):
                long = u in (GATES_AT, LRU_A_AT, LRU_SCAN_AT) + L2_AT
                if long:
                    split(q, u + RING)
                mixers2_dve(dve, u)
                if not long:
                    split(q, u + RING)
            q += U_IN2 // 4
            splits(q, 12, KT + 4)
            post_weighted(False, 2 * LB, 0)
            splits(q, KT + 4, U_OUT + 3)
            post(False, 2 * LB)
            norm_in(2 * LB + 1, G2_FFN, q + U_OUT // 4)
            q += U_OUT // 4
            ffn2_dve(dve, split, splits, evac, q)
            q += U_UP // 4
            splits(q, 7, FKT + 4)
            post_weighted(True, 2 * LB + 1, 0)
            splits(q, FKT + 4, U_DOWN)
            post(True, 2 * LB + 1)

        @block.gpsimd
        def _(pool):
            def rope_half(l, w, half, i):
                n = 3 * half + w
                pool.wait_ge(s_freeN, N_IN1 * l + n + 1)
                v = (q_nat, k_nat)[w][:, :, half * 512:(half + 1) * 512].rearrange("p t (h e) -> p t h e", e=64)
                t1, t2 = v[:, :, :, 0:8], v[:, :, :, 8:16]
                cos = C[:, C_ROPE:C_ROPE + 16].rearrange("p (t e) -> p t e", t=NT)[:, :, None, :].to_broadcast((P, NT, 8, 8))
                sin = C[:, C_ROPE + 16:C_ROPE + 32].rearrange("p (t e) -> p t e", t=NT)[:, :, None, :].to_broadcast((P, NT, 8, 8))
                r = [rope[:, k, :].rearrange("p (t h e) -> p t h e", t=NT, h=8) for k in range(4)]
                pool.wait_ge(s_roped, 8 * l + 2 * i)
                for k, (u, f) in enumerate(((t1, cos), (t2, sin), (t2, cos), (t1, sin))):
                    ins = pool.tensor_tensor(r[k], u, f, ALU.mult)
                ins.then_inc(s_rope, 1)
                pool.wait_ge(s_rope, 4 * l + i + 1)
                pool.tensor_tensor(t1, r[0], r[1], ALU.subtract).then_inc(s_roped, 1)
                pool.tensor_tensor(t2, r[2], r[3], ALU.add).then_inc(s_roped, 1)

            pool.wait_ge(s_const, 16)
            with pool.Fori(0, DEPTH) as l:
                pool.wait_ge(s_pad, l + 1)
                pool.wait_ge(s_kc, 32 * (l + 1))
                pool.wait_ge(s_freeT, l * T_LAYER + 3)
                inv = KC[:, K_INV:K_END].rearrange("p (n s) -> p n s", n=4)
                src, width, did = upad, UP, 0
                for k in range(4):
                    d, win = 1 << k, 2 << k
                    width -= d
                    dst = (win_a, win_b)[k % 2]
                    if did:
                        pool.wait_ge(s_pool, 12 * l + did)
                    pool.tensor_tensor(dst[:, k:4, 0:width], src[:, k:4, 0:width], src[:, k:4, d:d + width],
                                       ALU.add).then_inc(s_pool, 1)
                    pool.wait_ge(s_pool, 12 * l + did + 1)
                    at = 8 - win // 2
                    pool.tensor_tensor(pooled[:, k, :], dst[:, k, at:at + S], inv[:, k, :], ALU.mult).then_inc(s_pool, 1)
                    pool.wait_ge(s_pool, 12 * l + did + 2)
                    ins = pool.tensor_tensor(pooled[:, k, :], pooled[:, k, :], upad[:, k, 8:8 + S], ALU.subtract)
                    ins.then_inc(s_pool, 1)
                    did += 3
                    src = dst
                i = 0
                for half in range(2):
                    for w in range(2):
                        rope_half(l, w, half, i)
                        i += 1

        def mixers_pe(pe, mm, l, u):
            def column_sums(src):
                for n in range(4):
                    last = mm(PS[:, 3, 0:S], ones, src[:, n, :], n == 0, n == 3)
                last.then_inc(s_col, 1)

            if u == POOL_AT:
                pe.wait_ge(s_pool, 12 * (l + 1))
                pe.wait_ge(s_kc, 32 * (l + 1))
                for n in range(4):
                    last = mm(PS[:, 6 + n // 2, (n % 2) * S:(n % 2 + 1) * S], pw[:, n, :], pooled[:, n, :], True, True)
                last.then_inc(s_mix, 1)
            if u == POOL_RMS_AT:
                pe.wait_ge(s_sqr, 3 * l + 1)
                column_sums(sq)
            if u == MEAN_AT:
                pe.wait_ge(s_cv, 4 * TAPS * (l + 1))
                column_sums(acc)
            if u == VAR_AT:
                pe.wait_ge(s_sqr, 3 * l + 2)
                column_sums(sq)
            if u == RMS_AT:
                pe.wait_ge(s_sqr, 3 * l + 3)
                pe.wait_ge(s_std, 3 * l + 2)
                column_sums(sq)
            if u in TURN_QK_AT:
                i = TURN_QK_AT.index(u)
                half, src = i // 2, (q_nat, k_nat)[i % 2]
                pe.wait_ge(s_roped, 8 * l + 2 * i + 2)
                if i in (0, 2):
                    pe.wait_ge(s_std, 3 * l + (1, 3)[i // 2])
                if i == 1:
                    pe.wait_ge(s_yc, l + 1)
                if i == 2:
                    pe.wait_ge(s_sb, 16 * l + 8)
                if i == 3:
                    pe.wait_ge(s_freeN, N_IN1 * l + 5)
                for j in range(4):
                    for t in range(NT):
                        b = TURN_QK_BANK[i] + j // 2
                        last = pe.transpose(PS[:, b, (j % 2) * S + t * P:(j % 2) * S + (t + 1) * P],
                                            src[:, t, (4 * half + j) * P:(4 * half + j + 1) * P], ident)
                last.then_inc(s_qkt, 1)
            for h in heads_at(OUTPUT_AT, u):
                pe.wait_ge(s_pt, 16 * l + h + 1)
                if h % 8 == 0:
                    pe.wait_ge(s_freeN, N_IN1 * l + 3 * (h // 8) + 3)
                if h % 4 == 0 and h:
                    pe.wait_ge(s_yb, 4 * l + h // 4)
                for t in range(NT):
                    o = PS[:, 7, (h % 4) * 128 + t * 64:(h % 4) * 128 + (t + 1) * 64]
                    for k in range(2):
                        last = mm(o, probT[:, h % 2, k * S + t * P:k * S + (t + 1) * P], v_nat[:, k, h * 64:(h + 1) * 64], k == 0, k == 1)
                last.then_inc(s_o, 1)
            for h in heads_at(SCORES_AT, u):
                if h % 8 == 0:
                    pe.wait_ge(s_qk, 4 * l + h // 4 + 2)
                if h % 8 and h < 8:
                    pe.wait_ge(s_sb, 16 * l + h)
                if h >= 10:
                    pe.wait_ge(s_sb, 16 * l + h - 1)
                p0 = 64 * (h % 2)
                for t in range(NT):
                    last = mm(PS[:, score_bank(h), t * S:(t + 1) * S], qT[p0:p0 + 64, h // 2, t * P:(t + 1) * P],
                              kT[p0:p0 + 64, h // 2, :], True, True)
                last.then_inc(s_S, 1)
            for h in heads_at(TURN_AT, u):
                pe.wait_ge(s_p, 16 * l + h + 1)
                if h:
                    pe.wait_ge(s_pt, 16 * l + h)
                for t in range(NT):
                    for k in range(2):
                        last = pe.transpose(PS[:, 6, k * S + t * P:k * S + (t + 1) * P],
                                            prob[:, h % 2, t * S + k * P:t * S + (k + 1) * P], ident)
                last.then_inc(s_ptr, 1)

        def ffn_pe(pe, chunk_T, q, ti, xt):
            with pe.Fori(0, 11) as j:
                pe.wait_ge(s_freeT, ti + 2 * j - 1)
                chunk_T(q + 4 * j, 0, 0, xt)
                pe.wait_ge(s_freeT, ti + 2 * j)
                chunk_T(q + 4 * j + 2, 0, 4)

        def down_pe(pe, wide_units, q, l):
            for c in range(2):
                wide_units(q, FKT * c, HT, list(range(FKT)), c, 0, FKT, lambda i, kt: None if c else pe.wait_ge(s_ht, 11 * l + i // 4 + 1))

        def mixers2_pe(pe, mm, u):
            def column_sums(src):
                for n in range(4):
                    last = mm(PS[:, 6, 0:S], ones, src[:, n, :], n == 0, n == 3)
                last.then_inc(s_csum, 1)

            def each(bank, lhs, rhs, signal):
                for m in range(8):
                    last = mm(pair(bank)[:, m, :], lhs(m), rhs(m), True, True)
                last.then_inc(signal, 1)

            head = lambda v, m: v[:, m % 4, (m // 4) * P:(m // 4 + 1) * P]
            ct = C[:, C_CAUSAL_T:C_CAUSAL_T + P]
            if u == GATES_MM_AT:
                pe.wait_ge(s_wbl, 1)
                for kt in range(KT):
                    last = mm(PS[0:16, 7, :], w_ba2[:, kt, :], XT[:, kt, :, :].rearrange("p a b -> p (a b)"), kt == 0, kt == KT - 1)
                last.then_inc(s_ba, 1)
            if u == GATES_AT:
                pe.wait_ge(s_ba, 2)
                for part in range(2):
                    for t in range(NT):
                        at = 32 * t + 16 * part
                        last = pe.transpose(PS[:, 6, at:at + 16], baT[:, part * S + t * P:part * S + (t + 1) * P], ident[0:16, 0:16])
                last.then_inc(s_ba, 1)
            if u == LRU_MIX_AT:
                pe.wait_ge(s_gln, 3)
                pe.wait_ge(s_lc, 16)
                pe.wait_ge(s_w2, 112)
                for n in range(4):
                    mm(quad(2)[:, n, :], wa_bd[:, n, :], lru_xc[:, n, :], True, True)
                    last = mm(quad(6)[:, n, :], wx_bd[:, n, :], lru_xc[:, n, :], True, True)
                last.then_inc(s_lm, 1)
            if u == LRU_RMS_AT:
                pe.wait_ge(s_lg, 2)
                pe.wait_ge(s_csq, 1)
                column_sums(f3(T1))
            if u == GCUM_AT:
                pe.wait_ge(s_g, 1)
                pe.wait_ge(s_crt, 1)
                mm(PS[:, 6, 0:8], ct, g_tok, True, True).then_inc(s_gcm, 1)
            if u == DECAY_AT:
                each(2, lambda m: g_tok[:, m:m + 1].to_broadcast((P, P)), lambda m: ct, s_grow)
            if u in L2_AT:
                k = L2_AT.index(u)
                if k == 0:
                    pe.wait_ge(s_fac, 1)
                    pe.wait_ge(s_dd, 2)
                else:
                    pe.wait_ge(s_l2r, 1)
                pe.wait_ge(s_l2s, k + 1)
                for h in range(4):
                    last = mm(quad(2)[:, h, :], ones, XL[:, h, :], True, True)
                last.then_inc(s_l2m, 1)
            if u == KK_AT:
                pe.wait_ge(s_gcum, 1)
                pe.wait_ge(s_l2n, 2)
                each(6, lambda m: head(kh, m), lambda m: head(kh, m), s_kk)
            if u in (K_TURN_AT, V_TURN_AT):
                k = int(u == V_TURN_AT)
                pe.wait_ge(s_pte if k else s_l2r, 5 if k else 2)
                if k:
                    pe.wait_ge(s_qs, 3)
                for m in range(8):
                    last = pe.transpose(pair(2 + 4 * k)[:, m, :], head((kh, vh)[k], m), ident)
                last.then_inc(s_kv, 1)
            if u == KQ_AT:
                pe.wait_ge(s_kvb, 1)
                each(2, lambda m: head(kh, m), lambda m: head(qh, m), s_kk)
            if u == P_TURN_AT:
                pe.wait_ge(s_P, 1)
                for m in range(8):
                    last = pe.transpose(pair(6)[:, m, :], Pm[:, m, :], ident)
                last.then_inc(s_Pt, 1)
            if u in POWER_AT:
                r = POWER_AT.index(u)
                pe.wait_ge(s_pte, r + 1)
                pe.wait_ge(s_tt if r else s_att, r + 1)
                each(2, lambda m: PmT[:, m, :], lambda m: Pm[:, m, :], s_sq)
                if r < 4:
                    each(6, lambda m: Pm[:, m, :], lambda m: PmT[:, m, :], s_sq)
            if u in PRODUCT_AT:
                r = PRODUCT_AT.index(u)
                pe.wait_ge(s_P, r + 2)
                pe.wait_ge(s_tt, r + 1)
                each(2, lambda m: Pm[:, m, :], lambda m: Tt[:, m, :], s_te)
            if u == WU_AT:
                pe.wait_ge(s_tt, 6)
                pe.wait_ge(s_kbg, 3)
                each(2, lambda m: kbg[:, m, :], lambda m: Tt[:, m, :], s_wu)
                each(6, lambda m: Tt[:, m, :], lambda m: v_beta[:, m, :], s_wu)
            for n in range(4):
                t, r = n // 2, 64 * (n % 2)
                if n and u == STATE_AT[n]:
                    pe.wait_ge(s_st, n)
                    for h in range(4):
                        last = mm(PS[r:r + 64, 2, h * P:(h + 1) * P], wT[:, 4 * t + h, r:r + 64], state[:, h, :], True, True)
                    last.then_inc(s_vn, 1)
                if u == CHUNK_AT[n]:
                    if n == 0:
                        pe.wait_ge(s_wue, 1)
                        pe.wait_ge(s_wue2, 1)
                        pe.wait_ge(s_qg, 1)
                    else:
                        pe.wait_ge(s_vne, n)
                        pe.wait_ge(s_oe, n)
                    if n < 3:
                        for h in range(4):
                            m = 4 * t + h
                            last = mm(PS[:, 6, h * P:(h + 1) * P], kg[r:r + 64, m, :], u_by[r:r + 64, m, :], True, True)
                        last.then_inc(s_ks, 1)
                    for h in range(4):
                        m = 4 * t + h
                        o = PS[r:r + 64, 3, h * P:(h + 1) * P]
                        if n:
                            mm(o, head(qh, m)[:, r:r + 64], state[:, h, :], True, False)
                        last = mm(o, decT[r:r + 64, m, r:r + 64], u_by[r:r + 64, m, :], n == 0, True)
                    last.then_inc(s_os, 1)
            if u == GDN_TURN_AT:
                pe.wait_ge(s_oz, 1)
                for m in range(8):
                    last = pe.transpose(quad(2)[:, m % 4, (m // 4) * P:(m // 4 + 1) * P], o_by[:, m, :], ident)
                last.then_inc(s_ot, 1)
            if u == SGU_W_AT:
                pe.wait_ge(s_wsm, 1)
                pe.wait_ge(s_st, 3)
                for g in range(4):
                    last = pe.transpose(PS[:, 6, g * P:(g + 1) * P], sgu_ws[:, g, :], ident)
                last.then_inc(s_wsm, 1)
            if u == SGU_MIX_AT:
                pe.wait_ge(s_gvn, 1)
                pe.wait_ge(s_wst, 1)
                for t in range(NT):
                    for g in range(4):
                        last = mm(PS[:, 6 + t, g * P:(g + 1) * P], sgu_wsT[:, g, :], sgu_v[:, t, g * P:(g + 1) * P], True, True)
                last.then_inc(s_gm, 1)
            if u == SGU_TURN_AT:
                for t in range(NT):
                    pe.wait_ge(s_gyn, t + 1)
                    for g in range(4):
                        last = pe.transpose(quad(6)[:, g, t * P:(t + 1) * P], sgu_v[:, t, g * P:(g + 1) * P], ident)
                    last.then_inc(s_gyt, 1)
            if u == SC_RMS_AT:
                pe.wait_ge(s_csq, 2)
                column_sums(sqs)

        @block.tensor
        def _(pe):
            def unit_ready(q, i):
                pe.wait_ge(s_lo, 4 * q + i + 5)

            def mm(o, w, r, start, stop):
                return pe.matmul(o, w, r, start=start, stop=stop, skip_group_check=True)

            def chunk_T(q, i0, base, xt=None):
                for i in range(8):
                    unit_ready(q, i0 + i)
                    slot = (i0 + i) % RING
                    for k in range(2):
                        kt = 2 * i + k
                        if xt is not None and kt:
                            pe.wait_ge(s_xt, xt + kt + 1)
                        for n in range(4):
                            if xt is not None and kt == 0:
                                pe.wait_ge(s_xt, xt + 2 * n + 2)
                            c = k * CHUNK + n * P
                            mm(PS[:, base + n, :], WH[:, slot, c:c + P], XT[:, kt, :, :].rearrange("p a b -> p (a b)"), kt == 0, False)
                            last = mm(PS[:, base + n, 0:S], WL[:, slot, c:c + P], XT[:, kt, 0, :], False, kt == KT - 1)
                    last.then_inc(s_pe, 1)

            def three(out_of, xt, tok, wh, wl, cols, first, final):
                hi, lo = xt[:, 0, tok], xt[:, 1, tok]
                for n in range(cols):
                    mm(out_of(n), hi, wh[:, n * CHUNK:(n + 1) * CHUNK], first, False)
                for n in range(cols):
                    mm(out_of(n), hi, wl[:, n * CHUNK:(n + 1) * CHUNK], False, False)
                for n in range(cols):
                    last = mm(out_of(n), lo, wh[:, n * CHUNK:(n + 1) * CHUNK], False, final)
                return last

            def chunk_T2(q, i0, base, xready=None, beside=None):
                o = quad(base)
                for i in range(8):
                    unit_ready(q, i0 + i)
                    slot = (i0 + i) % RING
                    for k in range(2):
                        kt = 2 * i + k
                        if xready:
                            xready(kt)
                        for n in range(4):
                            c = k * CHUNK + n * P
                            mm(o[:, n, :], WH[:, slot, c:c + P], XT[:, kt, 0, :], kt == 0 and n % 2 == 0, False)
                            mm(o[:, n, :], WH[:, slot, c:c + P], XT[:, kt, 1, :], False, False)
                            last = mm(o[:, n, :], WL[:, slot, c:c + P], XT[:, kt, 0, :], False, kt == KT - 1)
                    last.then_inc(s_pe, 1)
                    if beside:
                        beside(i)

            def chunk_N(q, i0, base, beside=None):
                for i in range(8):
                    unit_ready(q, i0 + i)
                    slot = (i0 + i) % RING
                    for k in range(2):
                        kt = 2 * i + k
                        for t in range(NT):
                            last = three(lambda n: PS[:, base + t, :], XT[:, kt], slice(t * P, (t + 1) * P),
                                         WH[:, slot, k * CHUNK:(k + 1) * CHUNK], WL[:, slot, k * CHUNK:(k + 1) * CHUNK],
                                         1, kt == 0, kt == KT - 1)
                    last.then_inc(s_pe, 1)
                    if beside:
                        beside(i)

            def wide_units(q, i0, src, order, c, lo_, hi_, ready):
                for i in range(lo_, hi_):
                    unit_ready(q, i0 + i)
                    ready(i, order[i])
                    slot = (i0 + i) % RING
                    for t in range(NT):
                        last = three(lambda n: PS[:, 4 * c + 2 * t + n, :], src[:, order[i]], slice(t * P, (t + 1) * P),
                                     WH[:, slot, :], WL[:, slot, :], 2, i == 0, i == len(order) - 1)
                    last.then_inc(s_pe, 1)
                return last

            def norm_in(n):
                for t in range(NT):
                    pe.wait_ge(s_xs, 2 * n + t + 1)
                    for j in range(8):
                        if j == 4:
                            pe.wait_ge(s_xs2, 2 * n + t + 1)
                        for k in range(2):
                            kt = 2 * j + k
                            last = pe.transpose(PS[:, j, k * S + t * P:k * S + (t + 1) * P], xs[:, t, kt * P:(kt + 1) * P], ident)
                        if t == 1:
                            last.then_inc(s_tr, 1)

            pe.sem_inc(s_pe, 4)
            pe.wait_ge(s_const, 16)
            with pe.Fori(0, DEPTH) as l:
                q = l * (U_LAYER // 4)
                pe.wait_ge(s_rows, 16 * 8 * (l + 1))
                pe.wait_ge(s_x, 8 * l + 1)
                for r in range(2):
                    pe.transpose(PS[:, 0, r * P:(r + 1) * P], ROWS[:, r, :], ident).then_inc(s_prt, 1)
                pe.wait_ge(s_par, 2 * l + 2)
                norm_in(2 * l)
                ti, ni = T_LAYER * l, N_IN1 * l
                for c in range(9):
                    base = 4 * (c % 2)
                    if c == 1:
                        pe.wait_ge(s_xt, 32 * l + 16)
                    elif 2 <= c < 5:
                        pe.wait_ge(s_freeT, ti + c - 1)
                    elif c:
                        pe.wait_ge(s_freeN, ni + c - 4)
                    if c < 3:
                        chunk_T(q, 8 * c, base, 32 * l if c == 0 else None)
                    else:
                        chunk_N(q, 8 * c, base, lambda i: mixers_pe(pe, mm, l, 8 * c + i))
                q1 = q + U_IN1 // 4
                for i in range(8):
                    if i == 0:
                        pe.wait_ge(s_freeN, ni + 6)
                    if U_IN1 + i == SQUARES_AT[3]:
                        mixers_pe(pe, mm, l, U_IN1 + i)
                    wide_units(q1, 0, XT, OUT_ORDER, 0, i, i + 1, lambda i, kt: pe.wait_ge(s_yt, 16 * l + i + 1))
                    if U_IN1 + i != SQUARES_AT[3]:
                        mixers_pe(pe, mm, l, U_IN1 + i)
                for t in range(NT):
                    pe.wait_ge(s_ybn, 2 * l + t + 1)
                    for j in range(4):
                        for k in range(2):
                            kt = 2 * j + k
                            last = pe.transpose(PS[:, 4 + j, k * S + t * P:k * S + (t + 1) * P], yb_n[:, t, kt * P:(kt + 1) * P], ident)
                        if t == 1:
                            last.then_inc(s_ybt, 1)
                wide_units(q1, 0, XT, OUT_ORDER, 0, 8, 16, lambda i, kt: pe.wait_ge(s_yt, 16 * l + i + 1))
                wide_units(q1, 16, XT, OUT_ORDER, 1, 0, 16, lambda i, kt: None)
                pe.wait_ge(s_x, 8 * l + 8)
                norm_in(2 * l + 1)
                ffn_pe(pe, chunk_T, q1 + U_OUT // 4, ti + T_IN1, 32 * l + 16)
                q3 = q1 + (U_OUT + U_UP) // 4
                down_pe(pe, wide_units, q3, l)
            pe.wait_ge(s_rows2, 16 * 16)
            pe.wait_ge(s_pn, 8 * LB - 2)
            for r in range(5):
                pe.transpose(PS[:, r // 4, (r % 4) * P:(r % 4 + 1) * P], rows2[:, r, :], ident).then_inc(s_prt2, 1)
            pe.wait_ge(s_par2, 5)
            norm_in(2 * LB)
            q = DEPTH * (U_LAYER // 4)
            for c, name in enumerate(IN2):
                base = 4 * (c % 2)
                if c < 2:
                    pe.wait_ge(s_xt, 32 * LB + (4, 16)[c])
                else:
                    pe.wait_ge(s_freeN, NB + c - 1)
                beside = lambda i: mixers2_pe(pe, mm, 8 * c + i)
                if name in BY_TOKEN2:
                    chunk_N(q, 8 * c, base, beside)
                else:
                    chunk_T2(q, 8 * c, base, (lambda kt: pe.wait_ge(s_xt, 32 * LB + kt + 1)) if c == 0 else None, beside)
            q += U_IN2 // 4
            for i in range(KT):
                if i == 0:
                    pe.wait_ge(s_freeN, NB + 11)
                wide_units(q, 0, XT, OUT_ORDER2, 0, i, i + 1, lambda i, kt: pe.wait_ge(s_y2t, i + 1))
                if i < 8:
                    mixers2_pe(pe, mm, U_IN2 + i)
            wide_units(q, 16, XT, OUT_ORDER2, 1, 0, KT, lambda i, kt: None)
            pe.wait_ge(s_x, 8 * LB + 8)
            norm_in(2 * LB + 1)
            q += U_OUT // 4
            with pe.Fori(0, 11) as j:
                pe.wait_ge(s_freeT, TB + 2 * j - 1)
                chunk_T(q + 4 * j, 0, 0, 32 * LB + 16)
                pe.wait_ge(s_freeT, TB + 2 * j)
                chunk_T(q + 4 * j + 2, 0, 4)
            q += U_UP // 4
            down_pe(pe, wide_units, q, LB)


INPUTS = """x w_in conv_w conv_b conv_ln_g conv_ln_b pool_w pool_scale g_mix w_out g_pre_mix g_post_mix g_pre_ffn
g_post_ffn w_gate w_up w_down pre_mix_norm_2 w_in_2 gdn_conv_w_2 gdn_a_log_2 gdn_dt_bias_2 gdn_norm_w_2 lru_conv_w_2
lru_conv_b_2 lru_wa_2 lru_ba_2 lru_wx_2 lru_bx_2 lru_lambda_2 sgu_ln_w_2 sgu_ln_b_2 sgu_ws_2 sgu_b_2 sconv_w_2
grp_norm_w_2 w_out_2 post_mix_norm_2 pre_ffn_norm_2 ffn_up_2 ffn_conv_w_2 ffn_conv_b_2 ffn_down_2
post_ffn_norm_2""".split()


def kernel(**inputs):
    import concourse.bacc as bacc
    from concourse.bass_utils import run_bass_kernel_spmd

    nc = bacc.Bacc("TRN2", target_bir_lowering=False, num_devices=1)
    constants, key_constants = shape_constants()
    arrays = {f"in_{n}_dram": np.ascontiguousarray(inputs[n]) for n in INPUTS}
    arrays["in_constants_dram"] = constants
    arrays["in_key_constants_dram"] = key_constants
    a = {n[3:-5]: nc.dram_tensor(n, v.shape, F32, kind="ExternalInput").ap() for n, v in arrays.items()}
    out = nc.dram_tensor("out_dram", (1, S, D), F32, kind="ExternalOutput").ap()
    build(nc, a, out)
    return run_bass_kernel_spmd(nc, [arrays], core_ids=[0]).results[0]["out_dram"]
```
